# Optimizing a Trainium2 kernel written in Bass

```python
import jax, jax.numpy as jnp
from jax import lax
import numpy as np
import math
import jax
import jax.numpy as jnp

D_MODEL = 1024
BATCH = 1
SEQ = 256
DEPTH = 2

CHUNK = 64
N_META = 16
D_MIX = D_MODEL
D_POOL = D_MIX // 4
D_CONV = D_MIX // 4
D_RET = D_MIX - D_POOL - D_CONV
POOL_WINDOWS = (2, 4, 8, 16)
N_POOL_GROUPS = len(POOL_WINDOWS)
POOL_GROUP = D_POOL // N_POOL_GROUPS
CONV_WIDTH = 31
RET_HEADS = 4
RET_HEAD_DIM = D_RET // RET_HEADS
ROPE_BASE = 10000.0
D_FF = ((8 * D_MODEL // 3 + 63) // 64) * 64
D_IN = D_POOL + 2 * D_CONV + 4 * D_RET
DEEPNORM_ALPHA = (2.0 * DEPTH) ** 0.25
DEEPNORM_BETA = (8.0 * DEPTH) ** -0.25
LN_EPS = 1e-5


def layer_norm(x, g, b):
    xf = x.astype(jnp.float32)
    mu = jnp.mean(xf, axis=-1, keepdims=True)
    var = jnp.mean(jnp.square(xf - mu), axis=-1, keepdims=True)
    return ((xf - mu) * lax.rsqrt(var + LN_EPS) * g + b).astype(x.dtype)

def swiglu_ffn(x, w13, w2):
    a, u = jnp.split(x @ w13, 2, axis=-1)
    return (jax.nn.silu(a) * u) @ w2

def pool_mixer(xp, w_pool, scale):
    B, L, _ = xp.shape
    xf = xp.astype(jnp.float32)
    cs = jnp.concatenate([jnp.zeros((B, 1, D_POOL), jnp.float32), jnp.cumsum(xf, axis=1)], axis=1)
    t = jnp.arange(L)
    outs = []
    for gi, w in enumerate(POOL_WINDOWS):
        lo, hi = gi * POOL_GROUP, (gi + 1) * POOL_GROUP
        csg = cs[..., lo:hi]
        start = jnp.maximum(t + 1 - w, 0)
        win_sum = csg[:, 1:] - csg[:, start]
        count = (t + 1 - start).astype(jnp.float32)
        outs.append(win_sum / count[None, :, None] - xf[..., lo:hi])
    y = jnp.stack(outs, axis=2)
    y = jnp.einsum('blgc,gcd->blgd', y, w_pool.astype(jnp.float32)).reshape(B, L, D_POOL)
    return (y * scale).astype(xp.dtype)

def conv_module(a, gate, w_dw, b_dw, ln_g, ln_b, w_pw):
    u = a * jax.nn.sigmoid(gate)
    y = lax.conv_general_dilated(u, w_dw[:, None, :], window_strides=(1,),
                                 padding=[(CONV_WIDTH - 1, 0)],
                                 dimension_numbers=('NWC', 'WIO', 'NWC'),
                                 feature_group_count=D_CONV) + b_dw
    y = jax.nn.silu(layer_norm(y, ln_g, ln_b))
    return y @ w_pw

def rope(x, cos, sin):
    x1, x2 = jnp.split(x, 2, axis=-1)
    return jnp.concatenate([x1 * cos - x2 * sin, x2 * cos + x1 * sin], axis=-1)

def retention(q, k, v, g, gn_g):
    B, L, _ = q.shape
    f32 = jnp.float32
    pos = jnp.arange(L, dtype=f32)
    inv_freq = ROPE_BASE ** (-jnp.arange(0, RET_HEAD_DIM, 2, dtype=f32) / RET_HEAD_DIM)
    ang = pos[:, None] * inv_freq[None, :]
    cos, sin = jnp.cos(ang), jnp.sin(ang)
    heads = lambda t: t.astype(f32).reshape(B, L, RET_HEADS, RET_HEAD_DIM).transpose(0, 2, 1, 3)
    qh = rope(heads(q), cos, sin)
    kh = rope(heads(k), cos, sin) * (RET_HEAD_DIM ** -0.5)
    vh = heads(v)
    P = (-N_META) % CHUNK
    NC = (L + P) // CHUNK
    chunk = lambda t: jnp.pad(t, ((0, 0), (0, 0), (P, 0), (0, 0))).reshape(B, RET_HEADS, NC, CHUNK, RET_HEAD_DIM)
    qc, kc, vc = chunk(qh), chunk(kh), chunk(vh)
    log_gamma = jnp.log(1.0 - 2.0 ** (-5.0 - jnp.arange(RET_HEADS, dtype=f32)))
    i = jnp.arange(CHUNK, dtype=f32)
    intra_decay = jnp.exp(log_gamma[:, None, None] * jnp.abs(i[:, None] - i[None, :]))
    s = jnp.einsum('bhnid,bhnjd->bhnij', qc, kc) * intra_decay[None, :, None]
    o_intra = jnp.einsum('bhnij,bhnjd->bhnid', s, vc)
    q_decay = jnp.exp(log_gamma[:, None] * (i + 1.0))[None, :, :, None]
    k_decay = jnp.exp(log_gamma[:, None] * (CHUNK - 1.0 - i))[None, :, :, None]
    chunk_decay = jnp.exp(log_gamma * CHUNK)[None, :, None, None]

    def step(state, inp):
        q_n, k_n, v_n = inp
        o = jnp.einsum('bhid,bhde->bhie', q_n * q_decay, state)
        state = state * chunk_decay + jnp.einsum('bhjd,bhje->bhde', k_n * k_decay, v_n)
        return state, o

    to_scan = lambda t: t.transpose(2, 0, 1, 3, 4)
    state0 = jnp.zeros((B, RET_HEADS, RET_HEAD_DIM, RET_HEAD_DIM), f32)
    _, o_cross = lax.scan(step, state0, (to_scan(qc), to_scan(kc), to_scan(vc)))
    o = o_intra + o_cross.transpose(1, 2, 0, 3, 4)
    o = o.reshape(B, RET_HEADS, NC * CHUNK, RET_HEAD_DIM)[:, :, P:]
    mu = jnp.mean(o, axis=-1, keepdims=True)
    var = jnp.mean(jnp.square(o - mu), axis=-1, keepdims=True)
    o = ((o - mu) * lax.rsqrt(var + LN_EPS)).transpose(0, 2, 1, 3).reshape(B, L, D_RET) * gn_g
    return (jax.nn.silu(g.astype(f32)) * o).astype(g.dtype)

def token_mix(h, w_in, pool_w, pool_scale, conv_dw, conv_db, conv_ln_g, conv_ln_b, conv_pw, ret_gn_g, w_out):
    z = h @ w_in
    splits = [D_POOL, D_POOL + D_CONV, D_POOL + 2 * D_CONV,
              D_POOL + 2 * D_CONV + D_RET, D_POOL + 2 * D_CONV + 2 * D_RET,
              D_POOL + 2 * D_CONV + 3 * D_RET]
    xp, ca, cg, q, k, v, g = jnp.split(z, splits, axis=-1)
    y_pool = pool_mixer(xp, pool_w, pool_scale)
    y_conv = conv_module(ca, cg, conv_dw, conv_db, conv_ln_g, conv_ln_b, conv_pw)
    y_ret = retention(q, k, v, g, ret_gn_g)
    return jnp.concatenate([y_pool, y_conv, y_ret], axis=-1) @ w_out

def first_inputs(seed: int = 0) -> dict:
    key = jax.random.key(seed)
    ks = jax.random.split(key, 24)
    nrm = lambda k, shape, s: jax.random.normal(k, shape, jnp.float32) * s
    ones_n = lambda k, shape: 1.0 + 0.05 * jax.random.normal(k, shape, jnp.float32)
    return {
        "x": nrm(ks[0], (BATCH, SEQ, D_MODEL), 1.0),
        "meta": nrm(ks[1], (N_META, D_MODEL), 1.0),
        "ln_in_g": ones_n(ks[2], (D_MODEL,)),
        "ln_in_b": nrm(ks[3], (D_MODEL,), 0.02),
        "ffn1_w13": nrm(ks[4], (DEPTH, D_MODEL, 2 * D_FF), D_MODEL ** -0.5),
        "ffn1_w2": nrm(ks[5], (DEPTH, D_FF, D_MODEL), DEEPNORM_BETA * D_FF ** -0.5),
        "w_in": nrm(ks[6], (DEPTH, D_MODEL, D_IN), D_MODEL ** -0.5),
        "pool_w": nrm(ks[7], (DEPTH, N_POOL_GROUPS, POOL_GROUP, POOL_GROUP), POOL_GROUP ** -0.5),
        "pool_scale": ones_n(ks[8], (DEPTH, D_POOL)),
        "conv_dw": nrm(ks[9], (DEPTH, CONV_WIDTH, D_CONV), CONV_WIDTH ** -0.5),
        "conv_db": nrm(ks[10], (DEPTH, D_CONV), 0.02),
        "conv_ln_g": ones_n(ks[11], (DEPTH, D_CONV)),
        "conv_ln_b": nrm(ks[12], (DEPTH, D_CONV), 0.02),
        "conv_pw": nrm(ks[13], (DEPTH, D_CONV, D_CONV), D_CONV ** -0.5),
        "ret_gn_g": ones_n(ks[14], (DEPTH, D_RET)),
        "w_out": nrm(ks[15], (DEPTH, D_MIX, D_MODEL), DEEPNORM_BETA * D_MIX ** -0.5),
        "ffn2_w13": nrm(ks[16], (DEPTH, D_MODEL, 2 * D_FF), D_MODEL ** -0.5),
        "ffn2_w2": nrm(ks[17], (DEPTH, D_FF, D_MODEL), DEEPNORM_BETA * D_FF ** -0.5),
        "ln_g": ones_n(ks[18], (DEPTH, 3, D_MODEL)),
        "ln_b": nrm(ks[19], (DEPTH, 3, D_MODEL), 0.02),
    }

def first_block(x, meta, ln_in_g, ln_in_b, ffn1_w13, ffn1_w2, w_in, pool_w, pool_scale,
              conv_dw, conv_db, conv_ln_g, conv_ln_b, conv_pw, ret_gn_g, w_out,
              ffn2_w13, ffn2_w2, ln_g, ln_b):
    B = x.shape[0]
    h = jnp.concatenate([jnp.broadcast_to(meta[None].astype(x.dtype), (B, N_META, D_MODEL)), x], axis=1)
    h = layer_norm(h, ln_in_g, ln_in_b)
    for l in range(DEPTH):
        h = layer_norm(DEEPNORM_ALPHA * h + 0.5 * swiglu_ffn(h, ffn1_w13[l], ffn1_w2[l]), ln_g[l, 0], ln_b[l, 0])
        mix = token_mix(h, w_in[l], pool_w[l], pool_scale[l], conv_dw[l], conv_db[l],
                        conv_ln_g[l], conv_ln_b[l], conv_pw[l], ret_gn_g[l], w_out[l])
        h = layer_norm(DEEPNORM_ALPHA * h + mix, ln_g[l, 1], ln_b[l, 1])
        h = layer_norm(DEEPNORM_ALPHA * h + 0.5 * swiglu_ffn(h, ffn2_w13[l], ffn2_w2[l]), ln_g[l, 2], ln_b[l, 2])
    return h[:, N_META:]


GRID_W = 64
CTX_LEN = 256
EPS = 1e-6
NEG_INF = -1e30

NA_HEADS = 8
NA_HEAD_DIM = 64
NA_WIN_ROWS = 8
NA_WIN_COLS = 16
NA_WIDTH = NA_HEADS * NA_HEAD_DIM

ML_HEADS = 4
ML_HEAD_DIM = 128
ML_WIDTH = ML_HEADS * ML_HEAD_DIM
ML_CHUNK = 128
ML_CONV = 3
ML_GATES = 4 * ML_HEADS

EVEN_IN = 3 * NA_WIDTH + 4 * ML_WIDTH + ML_GATES
EVEN_SPLITS = (NA_WIDTH, 2 * NA_WIDTH, 3 * NA_WIDTH,
               3 * NA_WIDTH + 2 * ML_WIDTH, 3 * NA_WIDTH + 3 * ML_WIDTH,
               3 * NA_WIDTH + 4 * ML_WIDTH)
EVEN_OUT = NA_WIDTH + ML_WIDTH

MLA_HEADS = 16
MLA_NOPE = 64
MLA_ROPE = 32
MLA_V = 64
MLA_QK_DIM = MLA_NOPE + MLA_ROPE
MLA_Q_RANK = 256
MLA_KV_RANK = 128
ATTN_BLOCK = 128

FFN_HIDDEN = 2816
FFN_CONV = 3


def rms_norm(x, g):
    xf = x.astype(jnp.float32)
    y = xf * lax.rsqrt(jnp.mean(xf * xf, axis=-1, keepdims=True) + EPS)
    return (y * g.astype(jnp.float32)).astype(x.dtype)

def modulate(h, shift, scale):
    return h * (1 + scale) + shift

def dwconv_centred(x, w, b):
    k = w.shape[0]
    p = k // 2
    t = x.shape[1]
    xp = jnp.pad(x, ((0, 0), (p, p), (0, 0)))
    y = b + xp[:, 0:t] * w[0]
    for j in range(1, k):
        y = y + xp[:, j:j + t] * w[j]
    return y

def _rotate(x, pos):
    d = x.shape[-1]
    half = d // 2
    inv = ROPE_BASE ** (-jnp.arange(half, dtype=jnp.float32) / half)
    ang = pos.astype(jnp.float32)[:, None] * inv
    ang = ang.reshape((ang.shape[0],) + (1,) * (x.ndim - 3) + (half,))
    cos = jnp.cos(ang).astype(x.dtype)
    sin = jnp.sin(ang).astype(x.dtype)
    x1, x2 = x[..., :half], x[..., half:]
    return jnp.concatenate([x1 * cos - x2 * sin, x1 * sin + x2 * cos], axis=-1)

def rope_2d(x, row, col):
    a = x.shape[-1] // 2
    return jnp.concatenate([_rotate(x[..., :a], row), _rotate(x[..., a:], col)], axis=-1)

def dense_attention(q, k, v):
    s = jnp.einsum('bqhd,bkhd->bhqk', q, k).astype(jnp.float32) * (q.shape[-1] ** -0.5)
    p = jax.nn.softmax(s, axis=-1).astype(v.dtype)
    o = jnp.einsum('bhqk,bkhd->bqhd', p, v)
    return o.reshape(o.shape[0], o.shape[1], -1)

def blocked_attention(q, k, v):
    b, t, h, d = q.shape
    nb = t // ATTN_BLOCK
    qb = jnp.moveaxis(q.reshape(b, nb, ATTN_BLOCK, h, d), 1, 0)
    scale = d ** -0.5

    def one_block(qi):
        s = jnp.einsum('bqhd,bkhd->bhqk', qi, k).astype(jnp.float32) * scale
        p = jax.nn.softmax(s, axis=-1).astype(v.dtype)
        return jnp.einsum('bhqk,bkhd->bqhd', p, v)

    o = lax.map(one_block, qb)
    return jnp.moveaxis(o, 0, 1).reshape(b, t, -1)

def neighbourhood_attention(q, k, v, k_c, v_c, rpb):
    b, t, h, d = q.shape
    rows = t // GRID_W
    kh = min(NA_WIN_ROWS, rows)
    kw = NA_WIN_COLS
    scale = d ** -0.5
    qg = q.reshape(b, rows, GRID_W, h, d)
    kg = k.reshape(b, rows, GRID_W, h, d)
    vg = v.reshape(b, rows, GRID_W, h, d)
    col = jnp.arange(GRID_W)
    cs = jnp.clip(col - kw // 2, 0, GRID_W - kw)
    in_win = (col[None, :] >= cs[:, None]) & (col[None, :] < cs[:, None] + kw)
    dc_idx = jnp.clip(col[None, :] - col[:, None], -(kw - 1), kw - 1) + (NA_WIN_COLS - 1)
    rpb_cols = rpb.astype(jnp.float32)[:, :, dc_idx]

    def row_block(args):
        r, q_row = args
        rs = jnp.clip(r - kh // 2, 0, rows - kh)
        k_band = lax.dynamic_slice_in_dim(kg, rs, kh, axis=1).reshape(b, kh * GRID_W, h, d)
        v_band = lax.dynamic_slice_in_dim(vg, rs, kh, axis=1).reshape(b, kh * GRID_W, h, d)
        dr_idx = rs + jnp.arange(kh) - r + (NA_WIN_ROWS - 1)
        bias = jnp.take(rpb_cols, dr_idx, axis=1)
        bias = jnp.where(in_win[None, None], bias, NEG_INF)
        bias = bias.transpose(0, 2, 1, 3).reshape(h, GRID_W, kh * GRID_W)
        s_lat = jnp.einsum('bqhd,bkhd->bhqk', q_row, k_band).astype(jnp.float32) * scale + bias
        s_ctx = jnp.einsum('bqhd,bkhd->bhqk', q_row, k_c).astype(jnp.float32) * scale
        p = jax.nn.softmax(jnp.concatenate([s_lat, s_ctx], axis=-1), axis=-1).astype(v.dtype)
        nl = kh * GRID_W
        return (jnp.einsum('bhqk,bkhd->bqhd', p[..., :nl], v_band)
                + jnp.einsum('bhqk,bkhd->bqhd', p[..., nl:], v_c))

    o = lax.map(row_block, (jnp.arange(rows), jnp.moveaxis(qg, 1, 0)))
    return jnp.moveaxis(o, 0, 1).reshape(b, t, h * d)

def mlstm_chunked(q, k, v, i_pre, logf, state):
    b, h, t, d = q.shape
    nc = t // ML_CHUNK

    def to_chunks(a):
        return jnp.moveaxis(a.reshape(a.shape[:2] + (nc, ML_CHUNK) + a.shape[3:]), 2, 0)

    xs = tuple(to_chunks(a) for a in (q, k, v, i_pre, logf))
    lower = jnp.tril(jnp.ones((ML_CHUNK, ML_CHUNK), dtype=bool))

    def step(carry, chunk):
        c_st, n_st, m_st = carry
        qc, kc, vc, ic, fc = chunk
        bcum = jnp.cumsum(fc, axis=-1)
        d_in = jnp.where(lower, bcum[..., :, None] - bcum[..., None, :] + ic[..., None, :], -jnp.inf)
        m_inter = bcum + m_st[..., None]
        m_t = jnp.maximum(m_inter, jnp.max(d_in, axis=-1))
        w = jnp.exp(d_in - m_t[..., None])
        a = jnp.exp(m_inter - m_t)
        qk = jnp.einsum('bhtd,bhsd->bhts', qc, kc) * w
        num = (a[..., None] * jnp.einsum('bhvd,bhtd->bhtv', c_st, qc)
               + jnp.einsum('bhts,bhsv->bhtv', qk, vc))
        den = a * jnp.einsum('bhd,bhtd->bht', n_st, qc) + jnp.sum(qk, axis=-1)
        h_out = num / jnp.maximum(jnp.abs(den), jnp.exp(-m_t))[..., None]
        b_last = bcum[..., -1]
        g = b_last[..., None] - bcum + ic
        m_new = jnp.maximum(b_last + m_st, jnp.max(g, axis=-1))
        decay = jnp.exp(b_last + m_st - m_new)
        wk = jnp.exp(g - m_new[..., None])
        c_new = decay[..., None, None] * c_st + jnp.einsum('bhs,bhsv,bhsd->bhvd', wk, vc, kc)
        n_new = decay[..., None] * n_st + jnp.einsum('bhs,bhsd->bhd', wk, kc)
        return (c_new, n_new, m_new), h_out

    state, hs = lax.scan(step, state, xs)
    return jnp.moveaxis(hs, 0, 2).reshape(b, h, t, d), state

def _ml_heads(a):
    b, t, _ = a.shape
    return a.reshape(b, t, ML_HEADS, ML_HEAD_DIM).transpose(0, 2, 1, 3).astype(jnp.float32)

def _rev(a):
    return jnp.flip(a, axis=2)

def _mlstm_inputs(qk, v, g, conv_w, conv_b):
    qk = jax.nn.silu(dwconv_centred(qk, conv_w, conv_b))
    q, k = jnp.split(qk, 2, axis=-1)
    q = _ml_heads(q) * (ML_HEAD_DIM ** -0.5)
    g = g.astype(jnp.float32).transpose(0, 2, 1)
    i_f, f_f, i_b, f_b = jnp.split(g, 4, axis=1)
    return (_ml_heads(q.transpose(0, 2, 1, 3).reshape(q.shape[0], q.shape[2], ML_WIDTH)),
            _ml_heads(k), _ml_heads(v),
            i_f, jax.nn.log_sigmoid(f_f), i_b, jax.nn.log_sigmoid(f_b))

def _mlstm_output(h, o_pre, g):
    b, nh, t, d = h.shape
    o = jax.nn.sigmoid(o_pre.astype(jnp.float32)).reshape(b, t, nh, d).transpose(0, 2, 1, 3)
    h = o * h
    mu = jnp.mean(h, axis=-1, keepdims=True)
    var = jnp.mean(jnp.square(h - mu), axis=-1, keepdims=True)
    h = (h - mu) * lax.rsqrt(var + EPS)
    h = h.transpose(0, 2, 1, 3).reshape(b, t, nh * d) * g.astype(jnp.float32)
    return h.astype(o_pre.dtype)

def _zero_state(b):
    return (jnp.zeros((b, ML_HEADS, ML_HEAD_DIM, ML_HEAD_DIM), jnp.float32),
            jnp.zeros((b, ML_HEADS, ML_HEAD_DIM), jnp.float32),
            jnp.zeros((b, ML_HEADS), jnp.float32))

def even_mixer(hx, hc, w_in, gate_b, conv_w, conv_b, rpb, ml_norm_g, w_out, ctx_out):
    naq_x, nak_x, nav_x, mlqk_x, mlv_x, mlo_x, mlg_x = jnp.split(hx @ w_in, list(EVEN_SPLITS), axis=-1)
    naq_c, nak_c, nav_c, mlqk_c, mlv_c, mlo_c, mlg_c = jnp.split(hc @ w_in, list(EVEN_SPLITS), axis=-1)

    def heads(a):
        return a.reshape(a.shape[0], a.shape[1], NA_HEADS, NA_HEAD_DIM)

    na_x = neighbourhood_attention(heads(naq_x), heads(nak_x), heads(nav_x),
                                   heads(nak_c), heads(nav_c), rpb)

    q_x, k_x, v_x, if_x, lf_x, ib_x, lb_x = _mlstm_inputs(mlqk_x, mlv_x, mlg_x + gate_b, conv_w, conv_b)
    q_c, k_c, v_c, if_c, lf_c, ib_c, lb_c = _mlstm_inputs(mlqk_c, mlv_c, mlg_c + gate_b, conv_w, conv_b)
    zero = _zero_state(hx.shape[0])
    h_cf, st_f = mlstm_chunked(q_c, k_c, v_c, if_c, lf_c, zero)
    h_xf, _ = mlstm_chunked(q_x, k_x, v_x, if_x, lf_x, st_f)
    h_cb, st_b = mlstm_chunked(_rev(q_c), _rev(k_c), _rev(v_c), _rev(ib_c), _rev(lb_c), zero)
    h_xb, _ = mlstm_chunked(_rev(q_x), _rev(k_x), _rev(v_x), _rev(ib_x), _rev(lb_x), st_b)
    ml_x = _mlstm_output(h_xf + _rev(h_xb), mlo_x, ml_norm_g)
    y_x = jnp.concatenate([na_x, ml_x], axis=-1) @ w_out
    if not ctx_out:
        return y_x, None
    na_c = dense_attention(heads(naq_c), heads(nak_c), heads(nav_c))
    ml_c = _mlstm_output(h_cf + _rev(h_cb), mlo_c, ml_norm_g)
    y_c = jnp.concatenate([na_c, ml_c], axis=-1) @ w_out
    return y_x, y_c

def _mla_q(h, w_dq, q_norm_g, w_uq, row, col):
    b, t, _ = h.shape
    q = (rms_norm(h @ w_dq, q_norm_g) @ w_uq).reshape(b, t, MLA_HEADS, MLA_QK_DIM)
    if row is None:
        return q
    return jnp.concatenate([q[..., :MLA_NOPE], rope_2d(q[..., MLA_NOPE:], row, col)], axis=-1)

def _mla_kv(h, w_dkv, kv_norm_g, w_ukv, row, col):
    b, t, _ = h.shape
    ckv = h @ w_dkv
    c_kv, k_pe = ckv[..., :MLA_KV_RANK], ckv[..., MLA_KV_RANK:]
    if row is not None:
        k_pe = rope_2d(k_pe, row, col)
    kv = (rms_norm(c_kv, kv_norm_g) @ w_ukv).reshape(b, t, MLA_HEADS, MLA_NOPE + MLA_V)
    k = jnp.concatenate([kv[..., :MLA_NOPE],
                         jnp.broadcast_to(k_pe[:, :, None, :], (b, t, MLA_HEADS, MLA_ROPE))], axis=-1)
    return k, kv[..., MLA_NOPE:]

def odd_mixer(hx, hc, w_dq, q_norm_g, w_uq, w_dkv, kv_norm_g, w_ukv, w_o, row, col, ctx_out):
    q_x = _mla_q(hx, w_dq, q_norm_g, w_uq, row, col)
    k_x, v_x = _mla_kv(hx, w_dkv, kv_norm_g, w_ukv, row, col)
    k_c, v_c = _mla_kv(hc, w_dkv, kv_norm_g, w_ukv, None, None)
    y_x = blocked_attention(q_x, jnp.concatenate([k_x, k_c], axis=1),
                            jnp.concatenate([v_x, v_c], axis=1)) @ w_o
    if not ctx_out:
        return y_x, None
    q_c = _mla_q(hc, w_dq, q_norm_g, w_uq, None, None)
    return y_x, dense_attention(q_c, k_c, v_c) @ w_o

def conv_ffn(h, w_up, conv_w, conv_b, w_down):
    u = dwconv_centred(h @ w_up, conv_w, conv_b)
    a, g = jnp.split(u, 2, axis=-1)
    return (a * jax.nn.silu(g)) @ w_down

def second_inputs(seed: int = 0) -> dict:
    key = jax.random.key(seed)
    ks = jax.random.split(key, 32)
    n_even = (DEPTH + 1) // 2
    n_odd = DEPTH // 2
    f32 = jnp.float32

    def nrm(k, shape, scale):
        return jax.random.normal(k, shape, f32) * scale

    gk = jax.random.split(ks[15], 4)
    forget_b = jnp.linspace(3.0, 6.0, ML_HEADS, dtype=f32)
    gate_b = jnp.concatenate([
        nrm(gk[0], (n_even, ML_HEADS), 0.1),
        forget_b + nrm(gk[1], (n_even, ML_HEADS), 0.1),
        nrm(gk[2], (n_even, ML_HEADS), 0.1),
        forget_b + nrm(gk[3], (n_even, ML_HEADS), 0.1)], axis=-1)
    return {
        "x": nrm(ks[0], (BATCH, SEQ, D_MODEL), 1.0),
        "c": nrm(ks[1], (BATCH, D_MODEL), 1.0),
        "ctx": nrm(ks[2], (BATCH, CTX_LEN, D_MODEL), 1.0),
        "c_ctx": nrm(ks[3], (D_MODEL,), 1.0),
        "ada_w": nrm(ks[4], (DEPTH, D_MODEL, 6 * D_MODEL), D_MODEL ** -0.5),
        "ada_b": nrm(ks[5], (DEPTH, 6 * D_MODEL), 0.02),
        "norm_g": 1.0 + nrm(ks[6], (DEPTH, 4, D_MODEL), 0.05),
        "ffn_w_up": nrm(ks[7], (DEPTH, D_MODEL, 2 * FFN_HIDDEN), D_MODEL ** -0.5),
        "ffn_conv_w": nrm(ks[8], (DEPTH, FFN_CONV, 2 * FFN_HIDDEN), FFN_CONV ** -0.5),
        "ffn_conv_b": nrm(ks[9], (DEPTH, 2 * FFN_HIDDEN), 0.02),
        "ffn_w_down": nrm(ks[10], (DEPTH, FFN_HIDDEN, D_MODEL), FFN_HIDDEN ** -0.5),
        "ev_w_in": nrm(ks[11], (n_even, D_MODEL, EVEN_IN), D_MODEL ** -0.5),
        "ev_gate_b": gate_b,
        "ev_conv_w": nrm(ks[12], (n_even, ML_CONV, 2 * ML_WIDTH), ML_CONV ** -0.5),
        "ev_conv_b": nrm(ks[13], (n_even, 2 * ML_WIDTH), 0.02),
        "ev_rpb": nrm(ks[14], (n_even, NA_HEADS, 2 * NA_WIN_ROWS - 1, 2 * NA_WIN_COLS - 1), 0.1),
        "ev_ml_norm_g": 1.0 + nrm(ks[16], (n_even, ML_WIDTH), 0.05),
        "ev_w_out": nrm(ks[17], (n_even, EVEN_OUT, D_MODEL), EVEN_OUT ** -0.5),
        "od_w_dq": nrm(ks[18], (n_odd, D_MODEL, MLA_Q_RANK), D_MODEL ** -0.5),
        "od_q_norm_g": 1.0 + nrm(ks[19], (n_odd, MLA_Q_RANK), 0.05),
        "od_w_uq": nrm(ks[20], (n_odd, MLA_Q_RANK, MLA_HEADS * MLA_QK_DIM), MLA_Q_RANK ** -0.5),
        "od_w_dkv": nrm(ks[21], (n_odd, D_MODEL, MLA_KV_RANK + MLA_ROPE), D_MODEL ** -0.5),
        "od_kv_norm_g": 1.0 + nrm(ks[22], (n_odd, MLA_KV_RANK), 0.05),
        "od_w_ukv": nrm(ks[23], (n_odd, MLA_KV_RANK, MLA_HEADS * (MLA_NOPE + MLA_V)), MLA_KV_RANK ** -0.5),
        "od_w_o": nrm(ks[24], (n_odd, MLA_HEADS * MLA_V, D_MODEL), (MLA_HEADS * MLA_V) ** -0.5),
    }

def second_block(x, c, ctx, c_ctx, ada_w, ada_b, norm_g, ffn_w_up, ffn_conv_w, ffn_conv_b, ffn_w_down,
              ev_w_in, ev_gate_b, ev_conv_w, ev_conv_b, ev_rpb, ev_ml_norm_g, ev_w_out,
              od_w_dq, od_q_norm_g, od_w_uq, od_w_dkv, od_kv_norm_g, od_w_ukv, od_w_o):
    t = x.shape[1]
    pos = jnp.arange(t)
    row = pos // GRID_W
    col = pos % GRID_W
    silu_c = jax.nn.silu(c)
    silu_cc = jax.nn.silu(c_ctx)
    xc = ctx
    for l in range(DEPTH):
        ctx_out = l < DEPTH - 1
        mod_x = (silu_c @ ada_w[l] + ada_b[l])[:, None, :]
        mod_c = silu_cc @ ada_w[l] + ada_b[l]
        sh1, sc1, g1, sh2, sc2, g2 = jnp.split(mod_x, 6, axis=-1)
        csh1, csc1, cg1, csh2, csc2, cg2 = jnp.split(mod_c, 6, axis=-1)
        hx = modulate(rms_norm(x, norm_g[l, 0]), sh1, sc1)
        hc = modulate(rms_norm(xc, norm_g[l, 0]), csh1, csc1)
        if l % 2 == 0:
            e = l // 2
            yx, yc = even_mixer(hx, hc, ev_w_in[e], ev_gate_b[e], ev_conv_w[e], ev_conv_b[e],
                                ev_rpb[e], ev_ml_norm_g[e], ev_w_out[e], ctx_out)
        else:
            o = l // 2
            yx, yc = odd_mixer(hx, hc, od_w_dq[o], od_q_norm_g[o], od_w_uq[o], od_w_dkv[o],
                               od_kv_norm_g[o], od_w_ukv[o], od_w_o[o], row, col, ctx_out)
        x = x + g1 * rms_norm(yx, norm_g[l, 1])
        hx = modulate(rms_norm(x, norm_g[l, 2]), sh2, sc2)
        x = x + g2 * rms_norm(conv_ffn(hx, ffn_w_up[l], ffn_conv_w[l], ffn_conv_b[l], ffn_w_down[l]),
                              norm_g[l, 3])
        if ctx_out:
            xc = xc + cg1 * rms_norm(yc, norm_g[l, 1])
            hc = modulate(rms_norm(xc, norm_g[l, 2]), csh2, csc2)
            xc = xc + cg2 * rms_norm(conv_ffn(hc, ffn_w_up[l], ffn_conv_w[l], ffn_conv_b[l], ffn_w_down[l]),
                                     norm_g[l, 3])
    return x


def setup_inputs(seed=0):
    out = dict(first_inputs(seed))
    for name, value in second_inputs(seed + 1).items():
        if name != "x":
            out[name + "_2"] = value
    return out


def reference(
    x, meta, ln_in_g, ln_in_b, ffn1_w13, ffn1_w2, w_in, pool_w, pool_scale, conv_dw, conv_db,
    conv_ln_g, conv_ln_b, conv_pw, ret_gn_g, w_out, ffn2_w13, ffn2_w2, ln_g, ln_b, c_2, ctx_2,
    c_ctx_2, ada_w_2, ada_b_2, norm_g_2, ffn_w_up_2, ffn_conv_w_2, ffn_conv_b_2, ffn_w_down_2,
    ev_w_in_2, ev_gate_b_2, ev_conv_w_2, ev_conv_b_2, ev_rpb_2, ev_ml_norm_g_2, ev_w_out_2,
    od_w_dq_2, od_q_norm_g_2, od_w_uq_2, od_w_dkv_2, od_kv_norm_g_2, od_w_ukv_2, od_w_o_2,
):
    x = first_block(
        x, meta, ln_in_g, ln_in_b, ffn1_w13, ffn1_w2, w_in, pool_w, pool_scale, conv_dw,
        conv_db, conv_ln_g, conv_ln_b, conv_pw, ret_gn_g, w_out, ffn2_w13, ffn2_w2, ln_g, ln_b,
    )
    return second_block(
        x, c_2, ctx_2, c_ctx_2, ada_w_2, ada_b_2, norm_g_2, ffn_w_up_2, ffn_conv_w_2,
        ffn_conv_b_2, ffn_w_down_2, ev_w_in_2, ev_gate_b_2, ev_conv_w_2, ev_conv_b_2, ev_rpb_2,
        ev_ml_norm_g_2, ev_w_out_2, od_w_dq_2, od_q_norm_g_2, od_w_uq_2, od_w_dkv_2,
        od_kv_norm_g_2, od_w_ukv_2, od_w_o_2,
    )


_drawn_inputs = setup_inputs


def setup_inputs(seed=0):
    import zlib

    import numpy as np

    out = dict(_drawn_inputs(seed))
    spreads = {}
    factors = {'pool_scale': 5.704,
     'conv_db': 8.0,
     'conv_ln_g': 5.882,
     'conv_ln_b': 8.0,
     'ret_gn_g': 5.728,
     'ffn_conv_b_2': 4.321,
     'ev_conv_b_2': 8.0,
     'ev_rpb_2': 8.0,
     'od_q_norm_g_2': 8.0,
     'od_kv_norm_g_2': 3.17}
    for name, (base, spread) in spreads.items():
        noise = np.random.default_rng([zlib.crc32(name.encode()), seed]).standard_normal(out[name].shape)
        drawn = base * np.exp(spread * noise) if base else spread * noise
        out[name] = jnp.asarray(drawn.astype(out[name].dtype))
    for name, factor in factors.items():
        out[name] = (out[name] * factor).astype(out[name].dtype)
    return out
```

```python
from contextlib import ExitStack

import numpy as np

import concourse.bass as bass
from concourse import mybir

ALU = mybir.AluOpType
ACT = mybir.ActivationFunctionType
AX = mybir.AxisListType
F32 = mybir.dt.float32

P = 128
D = 1024
CT = D // P
META = 16
SEQ = 256
CTX = 256
L1 = META + SEQ
L2 = CTX + SEQ
X0 = L2 - L1
DEPTH = 2
FT = 22
FF = FT * P
SLOT = FT * P
ALPHA = (2.0 * DEPTH) ** 0.25
TAPS = 31
RH = 4
GRID_W = 64
ROWS = SEQ // GRID_W
NAH, NAD = 8, 64
MLH = 4
MLAH = 16
NEG = -1e30
RPB_PERIOD = 2 * GRID_W - 1
RPB_ROW = GRID_W * RPB_PERIOD
N_START, N_TABLES, N_ODD = 9, 10, 5
N_SET = 11

PAIRS_ADA = 12
PAIRS_UP, PAIRS_DN = FT // 2, CT // 2
PAIRS_FFN = PAIRS_UP + PAIRS_DN
PAIRS_MIX = 8
PAIRS_LAYER = 2 * PAIRS_FFN + PAIRS_MIX
PAIRS_EVEN = 9
PAIRS_ODD = 9

V_LNG, V_LNB, V_PS, V_DW, V_DB, V_CG, V_CB, V_GN = 0, 24, 48, 50, 112, 114, 116, 118
NV = 122


def build(nc, A, out):
    with ExitStack() as ctx:
        def sb(name, shape):
            return ctx.enter_context(nc.sbuf_tensor(name, shape, F32))

        def sem(name):
            return ctx.enter_context(nc.semaphore(name))

        X = sb("X", [P, CT, L2])
        PRE = sb("PRE", [P, CT, L2])
        SQ = sb("SQ", [P, CT, L2])
        RING = sb("RING", [P, 2, SLOT])
        G = sb("G", [P, FT, L2])
        SG = sb("SG", [P, 2, L2])
        RSTD = sb("RSTD", [P, L2])
        VEC = sb("VEC", [P, NV])
        LNIN = sb("LNIN", [P, 2, CT])
        ONES = sb("ONES", [P, 3, P])
        EPS5 = sb("EPS5", [P, 1])
        EPS6 = sb("EPS6", [P, 1])
        SC = sb("SC", [P, CT, 2])
        ADAB = sb("ADAB", [P, DEPTH, 48])
        MOD = sb("MOD", [P, DEPTH, 48, 2])
        NG = sb("NG", [P, DEPTH, 4, CT])
        GIN = sb("GIN", [P, DEPTH, 2, CT, 2])
        GOUT = sb("GOUT", [P, DEPTH, 2, CT, 2])
        BW = 21056
        B = sb("B", [P, BW])
        PS = ctx.enter_context(nc.psum_tensor("PS", [P, 8, 512], F32))

        used = {}

        def carve(region, base, words, shape, **dims):
            at = used.get(region, 0)
            used[region] = at + words
            total = {"G1": FT * L2, "G2": FT * L2, "G3": FT * L2}.get(region, BW)
            assert used[region] <= total, (region, used[region], total)
            v = base[:, at:at + words]
            return v.rearrange(shape, **dims) if shape else v

        GF = G[:, :, :].rearrange("p a b -> p (a b)")
        YM = carve("G1", GF, CT * L1, "p (a b) -> p a b", a=CT)
        QK = carve("G1", GF, 8 * L1, "p (a b) -> p a b", a=8)
        V1 = carve("G1", GF, 3 * 512, "p (a b) -> p a b", a=3)
        OT = carve("G1", GF, 4 * L1, "p (a b) -> p a b", a=4)
        STD4 = carve("G1", GF, 4 * L1, "p (a b) -> p a b", a=4)
        GS = carve("G1", GF, 4 * L1, "p (a b) -> p a b", a=4)
        ST = carve("G1", GF, 2 * 3 * L1, "p (z a b) -> p z a b", z=2, a=3)
        DT = carve("B1", B, RH * 3 * L1, "p (h a b) -> p h a b", h=RH, a=3)
        RC = carve("B1", B, L1, None)
        RS = carve("B1", B, 2 * L1, "p (a b) -> p a b", a=2)
        IC = carve("B1", B, 2 * L1, "p (a b) -> p a b", a=2)
        XP = carve("B1", B, 2 * (16 + L1), "p (a b) -> p a b", a=2)
        PT_ = [carve("B1", B, 2 * (16 + L1), "p (a b) -> p a b", a=2) for _ in range(4)]
        WN = carve("B1", B, 2 * L1, "p (a b) -> p a b", a=2)
        PM = carve("B1", B, 2 * L1, "p (a b) -> p a b", a=2)
        CA = carve("B1", B, 2 * L1, "p (a b) -> p a b", a=2)
        CSG = carve("B1", B, 2 * L1, "p (a b) -> p a b", a=2)
        CP = carve("B1", B, 2 * (TAPS - 1 + L1), "p (a b) -> p a b", a=2)
        ACC = carve("B1", B, 2 * L1, "p (a b) -> p a b", a=2)
        T1 = carve("B1", B, 2 * L1, "p (a b) -> p a b", a=2)
        T2 = carve("B1", B, 2 * L1, "p (a b) -> p a b", a=2)
        CY = carve("B1", B, 2 * L1, "p (a b) -> p a b", a=2)
        CSQ = carve("B1", B, 2 * L1, "p (a b) -> p a b", a=2)
        PW = carve("B1", B, 2 * P, "p (a b) -> p a b", a=2)
        CSTD = carve("B1", B, L1, None)
        IDN = carve("B2", B, P, None)
        YM2 = carve("B2", B, CT * L2, "p (a b) -> p a b", a=CT)
        CB = [carve("B2", B, 2 * 2 * 258, "p (a g b) -> p a g b", a=2, g=2) for _ in range(2)]
        AC = [carve("B2", B, 2 * L2, "p (a g b) -> p a g b", a=2, g=2) for _ in range(2)]
        FCW = [carve("B2", B, FT * 2 * 4, "p (f a c) -> p f a c", f=FT, a=2) for _ in range(2)]
        TM = carve("B2", B, 2 * 512, "p (d w) -> p d w", d=2)
        SS = [TM[:, 0, :], TM[:, 1, :]]
        PR = [carve("B2", B, 512, None) for _ in range(2)]
        PTT = [carve("B2", B, 512, "p (a b) -> p a b", a=4) for _ in range(2)]
        STAT = carve("B2", B, 64, None)
        b2_shared = used["B2"]
        VN = carve("B2", B, 4 * 512, "p (a b) -> p a b", a=4)
        VM = carve("B2", B, 4 * 512, "p (a b) -> p a b", a=4)
        EVW = carve("B2", B, 8 * 4, "p (f c) -> p f c", c=4)
        WG = carve("B2", B, CT * 16, "p (a b) -> p a b", a=CT)
        MASK = carve("B2", B, 2 * 3 * 512, "p (d w) -> p d w", d=2)
        GB = carve("B2", B, 2 * 512, "p (d w) -> p d w", d=2)
        GR = SG
        SEL = carve("B2", B, MLH * P, None)
        GBIAS = carve("B2", B, 16, None)
        GT = carve("B2", B, 64, "p (a b) -> p a b", a=4)
        GE = carve("B2", B, 64, "p (a b) -> p a b", a=4)
        LS = carve("B2", B, 64, "p (a b) -> p a b", a=4)
        NF = carve("B2", B, 32, "p (d t h) -> p d t h", d=2, t=4)
        MLG = carve("B2", B, MLH, None)
        used["B3"] = b2_shared
        WUQ = carve("B3", B, 12 * 2 * P, "p (f k c) -> p f k c", f=12, k=2)
        WUKV = carve("B3", B, 2 * D, None)
        DQ = carve("B3", B, 2 * SEQ, "p (a b) -> p a b", a=2)
        CKV = carve("B3", B, L2, None)
        KPE = carve("B3", B, L2, None)
        RT = carve("B3", B, 2 * SEQ, "p (a b) -> p a b", a=2)
        PERM = carve("B3", B, P, None)
        SW = carve("B3", B, 4 * SEQ, "p (a b) -> p a b", a=4)
        QNG = carve("B3", B, 3, None)
        QT = carve("G3", GF, 12 * SEQ, "p (a b) -> p a b", a=12)
        KN = carve("G3", GF, 8 * L2, "p (a b) -> p a b", a=8)
        VV = carve("G3", GF, 4 * D, "p (a b) -> p a b", a=4)
        SQF = SQ[:, :, :].rearrange("p a b -> p (a b)")
        NU = SQF.rearrange("p (d s t) -> p d s t", d=2, s=4)
        BIAS = PRE[:, :, :].rearrange("p a (q r c) -> p a q r c", q=2, r=ROWS)

        WIN = carve("B2", B, GRID_W, None)

        def item(qk, keys, scale, v, rows, o, bias=None):
            return {"qk": qk, "keys": keys, "scale": scale, "v": v, "rows": rows, "out": o, "bias": bias,
                    "sb": bias is not None}

        def na_item(h, t):
            q = slice(64 * (h % 2), 64 * (h % 2) + 64)
            keys = CTX if t < 2 else L2
            return item([(G[q, h // 2, t * P:(t + 1) * P], G[q, 4 + h // 2, 0:keys])], keys, NAD ** -0.5,
                        lambda j: VN[:, j, h * NAD:(h + 1) * NAD], q, YM2[q, h // 2, t * P:(t + 1) * P],
                        None if t < 2 else BIAS[:, h, t - 2, :, :].rearrange("p r c -> p (r c)"))

        def mla_item(h, t):
            q, r = slice(64 * (h % 2), 64 * (h % 2) + 64), slice(32 * (h % 4), 32 * (h % 4) + 32)
            cols = slice(t * P, (t + 1) * P)
            return item([(QT[q, h // 2, cols], KN[q, h // 2, :]), (QT[r, 8 + h // 4, cols], KPE[r, :])],
                        L2, 96.0 ** -0.5, lambda j: VV[:, j, h * 64:(h + 1) * 64], q,
                        YM2[q, h // 2, CTX + t * P:CTX + (t + 1) * P])

        EVEN_ITEMS = [na_item(h, t) for t in range(4) for h in range(NAH)]
        ODD_ITEMS = [mla_item(h, t) for h in range(MLAH) for t in range(2)]

        GAIN_STEPS = DEPTH * 2 * 5
        ABS_AT = 3
        LS_AT = ABS_AT + 2
        NF_AT = LS_AT + 2
        MLC_AT = NF_AT + 4 * MLH * 10 + 1
        MLY_AT = MLC_AT + 2 + MLH
        EVEN_AT = MLY_AT + NAH + sum(4 if i["sb"] else 2 for i in EVEN_ITEMS)
        ODD_Q_AT = EVEN_AT + 10
        ODD_ROPE_AT = ODD_Q_AT + 6
        ODD_STD_AT = 3

        XL = X[:, :, X0:L2]
        PL = PRE[:, :, 0:L1]
        SL = SQ[:, :, 0:L1]

        w_loaded = [sem("w_loaded0"), sem("w_loaded1")]
        unit_done = [sem("unit_done0"), sem("unit_done1")]
        unit_taken = [sem("unit_taken0"), sem("unit_taken1")]
        start_loaded = sem("start_loaded")
        start_set = sem("start_set")
        vec_loaded = sem("vec_loaded")
        silu_c = sem("silu_c")
        gains_step = sem("gains_step")
        silu_done = [sem("silu_done0"), sem("silu_done1")]
        residual_scaled = sem("residual_scaled")
        ln_mean, ln_centred, ln_squared, ln_var = sem("ln_mean"), sem("ln_centred"), sem("ln_squared"), sem("ln_var")
        ln_std, ln_rstd, ln_scaled, ln_out = sem("ln_std"), sem("ln_rstd"), sem("ln_scaled"), sem("ln_out")
        conv_gate, silu_g = sem("conv_gate"), sem("silu_g")
        mix_step, conv_tap, pool_step = sem("mix_step"), sem("conv_tap"), sem("pool_step")
        ret_scores, ret_decayed, ret_out, ret_copied = (sem("ret_scores"), sem("ret_decayed"), sem("ret_out"),
                                                        sem("ret_copied"))
        cv_mean, cv_squared, cv_var, cv_std, cv_silu = (sem("cv_mean"), sem("cv_squared"), sem("cv_var"),
                                                        sem("cv_std"), sem("cv_silu"))
        gn_stat, gn_squared, gn_std, gn_y = sem("gn_stat"), sem("gn_squared"), sem("gn_std"), sem("gn_y")
        pooled_taken = sem("pooled_taken")
        ctx_loaded, tab_loaded, u_loaded, bias_loaded, odd_loaded = (sem("ctx_loaded"), sem("tab_loaded"),
                                                                     sem("u_loaded"), sem("bias_loaded"),
                                                                     sem("odd_loaded"))
        rm_squared, rm_var, rm_std, rm_rstd, rm_scaled, rm_in, rm_out = (
            sem("rm_squared"), sem("rm_var"), sem("rm_std"), sem("rm_rstd"), sem("rm_scaled"), sem("rm_in"),
            sem("rm_out"))
        side_step = [sem("side_step0"), sem("side_step1")]
        tap_side = [sem("tap_side0"), sem("tap_side1")]
        tap_silu = [sem("tap_silu0"), sem("tap_silu1")]
        tap_prod = [sem("tap_prod0"), sem("tap_prod1")]
        borders_zero = sem("borders_zero")
        vec_step, act_step, pe_step = sem("vec_step"), sem("act_step"), sem("pe_step")
        at_scores, at_max, at_exp, at_probs, at_turned, at_copied, at_pv, at_out = (
            sem("at_scores"), sem("at_max"), sem("at_exp"), sem("at_probs"), sem("at_turned"), sem("at_copied"),
            sem("at_pv"), sem("at_out"))
        ml_bc, ml_bcopied, ml_arg, ml_w, ml_probs, ml_scores, ml_turned, ml_copied, ml_pv, ml_out = (
            sem("ml_bc"), sem("ml_bcopied"), sem("ml_arg"), sem("ml_w"), sem("ml_probs"), sem("ml_scores"),
            sem("ml_turned"), sem("ml_copied"), sem("ml_pv"), sem("ml_out"))
        out_stored = sem("out_stored")
        passed = {e: sem("passed_" + e) for e in ("pool", "vector", "tensor")}

        def lay(l, per, n):
            return n if l is None else l * per + n

        U0 = DEPTH * PAIRS_ADA
        U_FFN_A, U_MIX, U_FFN_B = U0, U0 + PAIRS_FFN, U0 + PAIRS_FFN + PAIRS_MIX
        U_EVEN = U0 + DEPTH * PAIRS_LAYER
        U_FFN2 = [U_EVEN + PAIRS_EVEN, U_EVEN + PAIRS_EVEN + PAIRS_FFN + PAIRS_ODD]
        U_ODD = U_FFN2[0] + PAIRS_FFN
        VIRTUAL = PAIRS_ODD - 3

        class Steps:

            def __init__(self, eng, s, base=0, total=None):
                self.eng, self.s, self.base, self.n, self.total = eng, s, base, 0, total

            def did(self, ins):
                self.n += 1
                ins.then_inc(self.s, 1)
                return ins

            def wait(self, back=0):
                self.eng.wait_ge(self.s, self.base + (self.n - back))

            def link(self, ins):
                self.did(ins)
                self.wait()

            def end(self):
                assert self.total is None or self.n == self.total, (self.n, self.total)

        MIX_STEPS = 18
        POOL_STEPS = 9

        def mm(pe, o, w, x, first, last):
            return pe.matmul(o, w, x, start=first, stop=last)

        block = ctx.enter_context(nc.Block())

        @block.sync
        def _(sp):
            def load(src, u_prev, s, words):
                sp.wait_ge(unit_done[s], u_prev + 1)
                sp.dma_start(RING[:, s, 0:words], src).then_inc(w_loaded[s], 16)

            def ffn_load(up, dn, l, row, u):
                upv = up.rearrange("n p w -> n p w")
                with sp.Fori(0, PAIRS_UP) as i:
                    for s in range(2):
                        r = (l * FT + i * 2 + (row * FT + s)) if l is not None else (i * 2 + (row * FT + s))
                        load(upv[r, :, :], u + i, s, 2 * D)
                with sp.Fori(0, PAIRS_DN) as i:
                    for s in range(2):
                        r = (l * CT + i * 2 + (row * CT + s)) if l is not None else (i * 2 + (row * CT + s))
                        load(dn[r, :, :], u + i + PAIRS_UP, s, SLOT)

            with sp.Fori(0, U0) as i:
                for s in range(2):
                    load(A["ada"][i * 2 + s, :, :], i, s, 2 * D)
            with sp.Fori(0, DEPTH) as l:
                ffn_load(A["up_a"], A["dn_a"], l, 0, l * PAIRS_LAYER + U_FFN_A)
                with sp.Fori(0, PAIRS_MIX) as i:
                    for s in range(2):
                        load(A["mix"][l * (2 * PAIRS_MIX) + i * 2 + s, :, :], l * PAIRS_LAYER + i + U_MIX, s, 2 * D)
                ffn_load(A["up_b"], A["dn_b"], l, 0, l * PAIRS_LAYER + U_FFN_B)
            with sp.Fori(0, PAIRS_EVEN) as i:
                for s in range(2):
                    load(A["even"][i * 2 + s, :, :], i + U_EVEN, s, 2 * D)
            ffn_load(A["up_c"], A["dn_c"], None, 0, U_FFN2[0])
            for n in range(6):
                u_prev = U_ODD + (0 if n < 2 else 1 if n < 4 else PAIRS_ODD - 1)
                load(A["odd"][n, :, :], u_prev, n % 2, 2 * D)
            ffn_load(A["up_c"], A["dn_c"], None, 1, U_FFN2[1])
            sp.wait_ge(rm_out, 8 * 4)
            sp.dma_start(out, X[:, :, CTX:L2]).then_inc(out_stored, 16)
            sp.wait_ge(out_stored, 16)

        @block.gpsimd
        def _(pool):
            for n, v in enumerate((1.0 / D, 1.0 / 256, 1.0 / P)):
                pool.memset(ONES[:, n, :], v).then_inc(start_set, 1)
            pool.memset(EPS5[:, :], 1e-5).then_inc(start_set, 1)
            pool.memset(EPS6[:, :], 1e-6).then_inc(start_set, 1)
            pool.memset(XP[:, :, 0:16], 0.0).then_inc(start_set, 1)
            for t in PT_:
                pool.memset(t[:, :, 0:16], 0.0).then_inc(start_set, 1)
            pool.memset(CP[:, :, 0:TAPS - 1], 0.0).then_inc(start_set, 1)
            pool.wait_ge(start_set, N_SET)

            def scale_residual(norms):
                pool.wait_ge(ln_out, norms)
                pool.sem_inc(passed["pool"], 1)
                pool.tensor_scalar(PL, XL, ALPHA, None, ALU.mult).then_inc(residual_scaled, 1)

            for dst, name in ((SC[:, :, :], "c"), (ADAB[:, :, :], "ada_b"), (PL, "x"), (LNIN[:, :, :], "ln_in"),
                              (NG[:, :, :, :], "norm_g"), (DT, "decay"), (RC, "rope_c"), (RS, "rope_s"), (IC, "inv_count")):
                pool.dma_start(dst, A[name]).then_inc(start_loaded, 16)

            with pool.Fori(0, DEPTH) as l:
                pool.wait_ge(ln_out, l * 24 + 8)
                pool.dma_start(VEC[:, :], A["vec"][l, :, :]).then_inc(vec_loaded, 16)
                pool.dma_start(PW, A["pool_w"][l, :, :, :]).then_inc(vec_loaded, 16)
                scale_residual(l * 24 + 8)
                scale_residual(l * 24 + 16)
                st = Steps(pool, pool_step, l * POOL_STEPS, POOL_STEPS)
                pool.wait_ge(unit_taken[0], l * PAIRS_LAYER + U_MIX + 2)
                src, n = XP, 16 + L1
                for j in range(4):
                    w = 1 << j
                    lo = 2 * w - 1
                    st.link(pool.tensor_tensor(PT_[j][:, :, lo:n], src[:, :, lo:n], src[:, :, lo - w:n - w], ALU.add))
                    src = PT_[j]
                for j in range(4):
                    q = slice(64 * (j % 2), 64 * (j % 2) + 64)
                    st.did(pool.tensor_tensor(WN[q, j // 2, :], PT_[j][q, j // 2, 16:n], IC[q, j // 2, :], ALU.mult))
                st.wait()
                st.did(pool.tensor_tensor(PM, WN, XP[:, :, 16:n], ALU.subtract))
                st.end()
                scale_residual(l * 24 + 24)

            pool.wait_ge(ln_out, 8 * 7)
            pool.dma_start(X[:, :, 0:CTX], A["ctx"]).then_inc(ctx_loaded, 16)
            for dst, name in ((IDN, "ident"), (FCW[0], "fcw0"), (FCW[1], "fcw1"), (EVW, "evw"), (WG, "wg"),
                              (MASK, "mask"), (SEL[0:4, :], "sel"), (WIN, "win"), (GBIAS, "gate_b"), (MLG, "ml_g")):
                pool.dma_start(dst, A[name]).then_inc(tab_loaded, 16)
            for c in CB:
                pool.memset(c[:, :, :, 0:258:257], 0.0).then_inc(borders_zero, 1)
            pool.wait_ge(rm_var, 1)
            pool.dma_start(NU, A["seen"]).then_inc(u_loaded, 16)
            for s in range(2):
                pool.wait_ge(unit_done[s], U_EVEN + 7 + 1)
            pool.wait_ge(pe_step, 1)
            for r in range(ROWS):
                for h in range(NAH):
                    src = bass.AP(A["rpb"].tensor, ((h * 7) + (ROWS - 1 - r)) * RPB_ROW + (GRID_W - 1),
                                  [[RPB_PERIOD - 1, GRID_W], [RPB_ROW, ROWS], [1, GRID_W]])
                    pool.dma_start(BIAS[GRID_W * (r % 2):GRID_W * (r % 2) + GRID_W, h, r // 2, :, :], src)\
                        .then_inc(bias_loaded, 16)
            for s in range(2):
                pool.wait_ge(unit_taken[s], U_EVEN + PAIRS_EVEN + 1)
            for dst, name in ((WUQ, "uq"), (WUKV, "ukv"), (RT, "rope2"), (PERM, "perm"), (QNG, "qkv_g")):
                pool.dma_start(dst, A[name]).then_inc(odd_loaded, 16)

        @block.tensor
        def _(pe):
            pe.wait_ge(start_set, N_SET)
            for s in range(2):
                mm(pe, PS[:, 2 * s, 0:P], ONES[:, 0, :], ONES[:, 1, :], True, True).then_inc(unit_done[s], 1)

            def begin(s, ld, u):
                pe.wait_ge(w_loaded[s], ld * 16 + 16)
                pe.wait_ge(unit_taken[s], u + 1)

            def two_tiles(s, rhs, n):
                for j in range(2):
                    for k in range(CT):
                        last = mm(pe, PS[:, 2 * s + j, 0:n], RING[:, s, (j * CT + k) * P:(j * CT + k + 1) * P],
                                  rhs[:, k, :], k == 0, k == CT - 1)
                return last

            def token_major(s, lhs, tts):
                c0 = 0
                for t, w in enumerate(tts):
                    o = PS[0:w, 2 * s + t // 2, 256 * (t % 2):256 * (t % 2) + 256]
                    for k in range(CT):
                        last = mm(pe, o, lhs[:, k, c0:c0 + w], RING[:, s, k * 256:(k + 1) * 256], k == 0, k == CT - 1)
                    c0 += w
                return last

            def ffn(u, ld, rhs, n, hidden_ready):
                with pe.Fori(0, PAIRS_UP) as i:
                    for s in range(2):
                        begin(s, ld + i, u + i)
                        two_tiles(s, rhs, n).then_inc(unit_done[s], 1)
                for s in range(2):
                    hidden_ready(s)
                pe.sem_inc(passed["tensor"], 1)
                with pe.Fori(0, PAIRS_DN) as i:
                    for s in range(2):
                        begin(s, ld + i + PAIRS_UP, u + i + PAIRS_UP)
                        for k in range(FT):
                            last = mm(pe, PS[:, 2 * s, 0:n], RING[:, s, k * P:(k + 1) * P],
                                      G[:, k, 0:n], k == 0, k == FT - 1)
                        last.then_inc(unit_done[s], 1)

            def layer_norm(l, e, du):
                if du is None:
                    pe.wait_ge(start_loaded, 16 * N_START)
                else:
                    for s in range(2):
                        pe.wait_ge(unit_taken[s], lay(l, PAIRS_LAYER, du + 1))
                for k in range(CT):
                    last = mm(pe, PS[:, 4, 0:L1], ONES[:, 0, :], PL[:, k, :], k == 0, k == CT - 1)
                last.then_inc(ln_mean, 1)
                for c in range(4):
                    pe.wait_ge(ln_squared, lay(l, 12, 4 * e + c + 1))
                    for k in (2 * c, 2 * c + 1):
                        last = mm(pe, PS[:, 5, 0:L1], ONES[:, 0, :], SL[:, k, :], k == 0, k == CT - 1)
                last.then_inc(ln_var, 1)

            pe.wait_ge(silu_c, 1)
            with pe.Fori(0, U0) as i:
                for s in range(2):
                    begin(s, i, i)
                    two_tiles(s, SC, 2).then_inc(unit_done[s], 1)
            layer_norm(None, 0, None)

            def mixer(l):
                u, n = l * PAIRS_LAYER, 0
                pe.wait_ge(ln_out, l * 24 + 16)
                for n in range(9):
                    s = n % 2
                    begin(s, u + (U_MIX + n // 2), u + (U_MIX + n // 2))
                    two_tiles(s, XL, L1).then_inc(unit_done[s], 1)
                for n in (9, 10):
                    s = n % 2
                    begin(s, u + (U_MIX + n // 2), u + (U_MIX + n // 2))
                    token_major(s, XL, (P, P, META)).then_inc(unit_done[s], 1)

                def scores(h):
                    if h == 0:
                        pe.wait_ge(mix_step, l * MIX_STEPS + 12)
                    else:
                        pe.wait_ge(ret_decayed, l * 4 + h)
                    q = slice(64 * (h % 2), 64 * (h % 2) + 64)
                    for jt in range(3):
                        w = P if jt < 2 else META
                        for a in range(2):
                            last = mm(pe, PS[0:w, 4 + jt, 0:L1], QK[q, 4 + 2 * (h // 2) + a, jt * P:jt * P + w],
                                      QK[q, 2 * (h // 2) + a, :], a == 0, a == 1)
                    last.then_inc(ret_scores, 1)

                def values(h):
                    pe.wait_ge(ret_decayed, l * 4 + h + 1)
                    if h == 0:
                        for s in range(2):
                            pe.wait_ge(unit_taken[s], u + (U_MIX + (5 if s else 6) + 1))
                    else:
                        pe.wait_ge(ret_copied, l * 4 + h)
                    for jt in range(3):
                        w = P if jt < 2 else META
                        last = mm(pe, PS[:, 7, 0:L1], V1[0:w, jt, h * P:(h + 1) * P], ST[0:w, h % 2, jt, :],
                                  jt == 0, jt == 2)
                    last.then_inc(ret_out, 1)

                scores(0)
                pe.wait_ge(unit_taken[0], u + (U_MIX + 6 + 1))
                pe.wait_ge(conv_tap, l * 62 + 62)
                for t in range(2):
                    last = mm(pe, PS[:, 0, 0:L1], ONES[:, 1, :], ACC[:, t, :], t == 0, t == 1)
                last.then_inc(cv_mean, 1)
                scores(1)
                values(0)
                pe.wait_ge(cv_squared, l + 1)
                for t in range(2):
                    last = mm(pe, PS[:, 1, 0:L1], ONES[:, 1, :], CSQ[:, t, :], t == 0, t == 1)
                last.then_inc(cv_var, 1)
                scores(2)
                values(1)
                scores(3)
                values(2)
                values(3)
                pe.wait_ge(ret_copied, l * 4 + 4)
                for h in range(RH):
                    last = mm(pe, PS[:, 4 + h, 0:L1], ONES[:, 2, :], OT[:, h, :], True, True)
                last.then_inc(gn_stat, 1)
                begin(1, u + (U_MIX + 5), u + (U_MIX + 5))
                pe.wait_ge(pool_step, l * POOL_STEPS + POOL_STEPS)
                pe.wait_ge(vec_loaded, l * 32 + 32)
                for t in range(2):
                    last = mm(pe, PS[:, 2 + t, 0:L1], PW[:, t, :], PM[:, t, :], True, True)
                last.then_inc(gn_stat, 1)
                pe.wait_ge(pooled_taken, l + 1)
                pe.wait_ge(cv_silu, l * 2 + 2)
                for j in range(2):
                    for k in range(2):
                        last = mm(pe, PS[:, 2 + j, 0:L1], RING[:, 1, (j * 2 + k) * P:(j * 2 + k + 1) * P],
                                  CY[:, k, :], k == 0, k == 1)
                last.then_inc(unit_done[1], 1)
                pe.wait_ge(gn_squared, l + 1)
                for h in range(RH):
                    last = mm(pe, PS[:, 4 + h, 0:L1], ONES[:, 2, :], SL[:, h, :], True, True)
                last.then_inc(gn_stat, 1)
                pe.wait_ge(gn_y, l * 4 + 4)
                pe.wait_ge(unit_taken[1], u + (U_MIX + 6 + 1))
                for n in range(12, 16):
                    s = n % 2
                    begin(s, u + (U_MIX + n // 2), u + (U_MIX + n // 2))
                    two_tiles(s, YM, L1).then_inc(unit_done[s], 1)

            with pe.Fori(0, DEPTH) as l:
                def hidden(off):
                    return lambda s: pe.wait_ge(unit_taken[s], l * PAIRS_LAYER + (off + PAIRS_UP + 1))
                pe.wait_ge(ln_out, l * 24 + 8)
                pe.sem_inc(passed["tensor"], 1)
                ffn(l * PAIRS_LAYER + U_FFN_A, l * PAIRS_LAYER + U_FFN_A, XL, L1, hidden(U_FFN_A))
                layer_norm(l, 1, U_FFN_A + PAIRS_FFN)
                mixer(l)
                layer_norm(l, 2, U_MIX + PAIRS_MIX)
                pe.wait_ge(ln_out, l * 24 + 24)
                pe.sem_inc(passed["tensor"], 1)
                ffn(l * PAIRS_LAYER + U_FFN_B, l * PAIRS_LAYER + U_FFN_B, XL, L1, hidden(U_FFN_B))
                layer_norm(l, 3, U_FFN_B + PAIRS_FFN)

            def rms(e, c0):
                for c in range(4):
                    pe.wait_ge(rm_squared, 4 * e + c + 1)
                    for k in (2 * c, 2 * c + 1):
                        last = mm(pe, PS[:, 4, 0:L2 - c0], ONES[:, 0, :], SQ[:, k, c0:L2], k == 0, k == CT - 1)
                last.then_inc(rm_var, 1)

            def attend(items, base):
                def scores(n):
                    it = items[n]
                    if base + n >= 2:
                        pe.wait_ge(at_max, base + n - 1)
                        pe.wait_ge(at_exp, base + n - 1)
                    o = PS[:, 4 + n % 2, 0:it["keys"]]
                    for j, (a, b) in enumerate(it["qk"]):
                        last = mm(pe, o, a, b, j == 0, j == len(it["qk"]) - 1)
                    last.then_inc(at_scores, 1)

                def turn(n):
                    it = items[n]
                    pe.wait_ge(at_probs, base + n + 1)
                    if base + n >= 1:
                        pe.wait_ge(at_copied, base + n)
                    for j in range(it["keys"] // P):
                        last = pe.transpose(PS[:, 6, j * P:(j + 1) * P], PR[n % 2][:, j * P:(j + 1) * P], IDN)
                    last.then_inc(at_turned, 1)

                def values(n):
                    it = items[n]
                    pe.wait_ge(at_copied, base + n + 1)
                    if base + n >= 1:
                        pe.wait_ge(at_out, base + n)
                    nk = it["keys"] // P
                    for j in range(nk):
                        last = mm(pe, PS[it["rows"], 7, 0:P], it["v"](j), PTT[n % 2][:, j, :], j == 0, j == nk - 1)
                    last.then_inc(at_pv, 1)

                scores(0)
                for n in range(len(items)):
                    if n + 1 < len(items):
                        scores(n + 1)
                    turn(n)
                    if n >= 1:
                        values(n - 1)
                values(len(items) - 1)

            rms(0, 0)
            pe.wait_ge(rm_in, 8)
            for n in range(14):
                s, u = n % 2, U_EVEN + n // 2
                begin(s, u, u)
                (two_tiles(s, PRE, L2) if n < 10 else token_major(s, PRE, (P,) * 4)).then_inc(unit_done[s], 1)
            pe.wait_ge(tab_loaded, 16 * N_TABLES)
            for t in range(4):
                for k in range(CT):
                    last = mm(pe, PS[:, 5, 16 * t:16 * t + 16], PRE[:, k, t * P:(t + 1) * P], WG[:, k, :],
                              k == 0, k == CT - 1)
            last.then_inc(pe_step, 1)
            pe.wait_ge(vec_step, LS_AT)
            pe.wait_ge(u_loaded, 16)
            for d in range(2):
                for st in range(4):
                    mm(pe, PS[0:4, 6 + d, :], LS[:, st, 8 * d + 4:8 * d + 8], NU[:, d, st, :], st == 0, False)
                for st in range(4):
                    mm(pe, PS[0:4, 6 + d, st * P:(st + 1) * P], GT[:, st, 8 * d:8 * d + 4], IDN, False, st == 3)
            for d in range(2):
                for t in range(4):
                    for st in range(4):
                        last = mm(pe, PS[:, 4, 16 * d + 4 * t:16 * d + 4 * t + 4], NU[:, d, st, t * P:(t + 1) * P],
                                  LS[:, st, 8 * d + 4:8 * d + 8], st == 0, st == 3)
            last.then_inc(pe_step, 1)
            pe.wait_ge(vec_step, NF_AT)
            for s in range(2):
                pe.wait_ge(unit_taken[s], U_EVEN + 7 + 1)
                pe.wait_ge(tap_prod[s], 2)
            for h in range(MLH):
                if h >= 1:
                    pe.wait_ge(ml_bcopied, h)
                for d in range(2):
                    last = mm(pe, PS[:, 4 + d, :], SEL[0:4, h * P:(h + 1) * P], GR[0:4, d, :], True, True)
                last.then_inc(ml_bc, 1)
                for t in range(4):
                    n, nk = 4 * h + t, 2 if t < 2 else 4
                    if n >= 1:
                        pe.wait_ge(ml_probs, n)
                    mm(pe, PS[:, 6, 0:nk * P], G[:, 8 + h, t * P:(t + 1) * P], G[:, 12 + h, 0:nk * P], True, True)\
                        .then_inc(ml_scores, 1)
                    pe.wait_ge(ml_probs, n + 1)
                    for j in range(nk):
                        last = pe.transpose(PS[:, 7, j * P:(j + 1) * P], PR[n % 2][:, j * P:(j + 1) * P], IDN)
                    last.then_inc(ml_turned, 1)
                    pe.wait_ge(ml_copied, n + 1)
                    if t == 0 and h >= 1:
                        pe.wait_ge(ml_out, h)
                    for j in range(nk):
                        last = mm(pe, PS[:, 0, t * P:(t + 1) * P], VM[:, j, h * P:(h + 1) * P], PTT[n % 2][:, j, :],
                                  j == 0, j == nk - 1)
                last.then_inc(ml_pv, 1)
            for part in range(2):
                pe.wait_ge(ml_out, 4 + part)
                for h in range(MLH):
                    last = mm(pe, PS[:, 4 + h, :], ONES[:, 2, :], (G[:, 16 + h, :], SQ[:, h, :])[part], True, True)
                last.then_inc(pe_step, 1)
            pe.wait_ge(ml_out, 6)
            attend(EVEN_ITEMS, 0)
            pe.wait_ge(at_out, len(EVEN_ITEMS))
            pe.wait_ge(vec_step, MLY_AT)
            for n in range(14, 18):
                s, u = n % 2, U_EVEN + n // 2
                begin(s, u, u)
                two_tiles(s, YM2, L2).then_inc(unit_done[s], 1)
            rms(1, 0)
            rms(2, 0)
            pe.wait_ge(rm_in, 16)
            ffn(U_FFN2[0], U_FFN2[0], PRE, L2, lambda s: pe.wait_ge(tap_prod[s], 2 + PAIRS_UP))
            rms(3, 0)
            rms(4, 0)
            pe.wait_ge(rm_in, 24)
            u = U_ODD
            begin(0, u, u)
            two_tiles(0, PRE[:, :, CTX:L2], SEQ).then_inc(unit_done[0], 1)
            begin(1, u, u)
            two_tiles(1, PRE, L2).then_inc(unit_done[1], 1)
            pe.wait_ge(odd_loaded, 16 * N_ODD)
            for s in range(2):
                pe.wait_ge(unit_taken[s], u + 2)
            for t in range(2):
                mm(pe, PS[:, 4, 0:SEQ], ONES[:, 1, :], SQ[:, t, 0:SEQ], t == 0, t == 1)
            mm(pe, PS[:, 5, :], ONES[:, 2, :], SQ[:, 2, :], True, True)
            mm(pe, PS[:, 6, 0:SEQ], PERM, KPE[:, CTX:L2], True, True).then_inc(pe_step, 1)
            pe.wait_ge(vec_step, ODD_Q_AT)
            for n in range(4):
                s, u = n % 2, U_ODD + 1 + n // 2
                pe.wait_ge(unit_taken[s], u + 1)
                for j in range(3):
                    for k in range(2):
                        last = mm(pe, PS[:, 2 * s + j // 2, 256 * (j % 2):256 * (j % 2) + 256],
                                  WUQ[:, 3 * n + j, k, :], DQ[:, k, :], k == 0, k == 1)
                last.then_inc(unit_done[s], 1)
            for n in range(4):
                s, u = n % 2, U_ODD + 3 + n // 2
                pe.wait_ge(unit_taken[s], u + 1)
                for j in range(2):
                    last = mm(pe, PS[:, 2 * s + j, :], WUKV[:, (2 * n + j) * P:(2 * n + j + 1) * P], CKV, True, True)
                last.then_inc(unit_done[s], 1)
            for n in range(4):
                s, u = n % 2, U_ODD + 5 + n // 2
                pe.wait_ge(unit_taken[s], u + 1)
                for j in range(2):
                    last = mm(pe, PS[:, 2 * s + j, :], CKV[:, n * P:(n + 1) * P],
                              WUKV[:, D + j * 512:D + (j + 1) * 512], True, True)
                last.then_inc(unit_done[s], 1)
            for s in range(2):
                pe.wait_ge(unit_taken[s], U_ODD + 7 + 1)
            for t in range(4):
                last = mm(pe, PS[:, 4 + t // 2, 256 * (t % 2):256 * (t % 2) + 256], PERM, QT[:, 8 + t, :], True, True)
            last.then_inc(pe_step, 1)
            pe.wait_ge(vec_step, ODD_ROPE_AT)
            attend(ODD_ITEMS, len(EVEN_ITEMS))
            pe.wait_ge(at_out, len(EVEN_ITEMS) + len(ODD_ITEMS))
            for n in range(4):
                s, u = n % 2, U_ODD + 7 + n // 2
                begin(s, U_ODD + 1 + n // 2, u)
                two_tiles(s, YM2[:, :, CTX:L2], SEQ).then_inc(unit_done[s], 1)
            rms(5, CTX)
            rms(6, CTX)
            pe.wait_ge(rm_in, 32)
            ffn(U_FFN2[1], U_FFN2[1] - VIRTUAL, PRE[:, :, CTX:L2], SEQ, lambda s: pe.wait_ge(tap_prod[s], 2 + 2 * PAIRS_UP))
            rms(7, CTX)

        @block.scalar
        def _(act):
            act.wait_ge(start_loaded, 16 * N_START)
            act.activation(SC[:, :, :], SC[:, :, :], ACT.Silu).then_inc(silu_c, 1)

            def layer_norm(l, e, gain, bias):
                for c in range(4):
                    act.wait_ge(ln_centred, lay(l, 12, 4 * e + c + 1))
                    act.activation(SL[:, 2 * c:2 * c + 2, :], PL[:, 2 * c:2 * c + 2, :], ACT.Square)\
                        .then_inc(ln_squared, 1)
                act.wait_ge(ln_var, lay(l, 3, e + 1))
                act.activation(RSTD[:, 0:L1], PS[:, 5, 0:L1], ACT.Sqrt, bias=EPS5[:, 0:1]).then_inc(ln_std, 1)
                for k in range(CT):
                    if k % 2 == 0:
                        act.wait_ge(ln_scaled, lay(l, 12, 4 * e + k // 2 + 1))
                    act.activation(XL[:, k, :], PL[:, k, :], ACT.Identity, scale=gain(k), bias=bias(k))\
                        .then_inc(ln_out, 1)

            def ffn_gate(l, u, f):
                with act.Fori(0, PAIRS_UP) as i:
                    for s in range(2):
                        act.wait_ge(unit_done[s], u + i + 2)
                        act.activation(SG[:, s, 0:L1], PS[:, 2 * s, 0:L1], ACT.Silu).then_inc(silu_done[s], 1)

            layer_norm(None, 0, lambda k: LNIN[:, 0, k:k + 1], lambda k: LNIN[:, 1, k:k + 1])

            with act.Fori(0, DEPTH) as l:
                def vec_norm(e):
                    layer_norm(l, e, lambda k: VEC[:, V_LNG + 8 * (e - 1) + k:V_LNG + 8 * (e - 1) + k + 1],
                               lambda k: VEC[:, V_LNB + 8 * (e - 1) + k:V_LNB + 8 * (e - 1) + k + 1])
                u = l * PAIRS_LAYER
                act.wait_ge(vec_loaded, l * 32 + 32)
                ffn_gate(l, u + U_FFN_A, None)
                vec_norm(1)
                act.wait_ge(unit_done[0], u + (U_MIX + 1 + 2))
                act.activation(CSG, PS[:, 0:2, 0:L1], ACT.Sigmoid).then_inc(conv_gate, 1)
                for n in (7, 8):
                    s = n % 2
                    act.wait_ge(unit_done[s], u + (U_MIX + n // 2 + 2))
                    act.activation(GS[:, 2 * (n - 7):2 * (n - 7) + 2, :], PS[:, 2 * s:2 * s + 2, 0:L1], ACT.Silu)\
                        .then_inc(unit_taken[s], 1)
                for n in (9, 10):
                    s = n % 2
                    act.wait_ge(unit_done[s], u + (U_MIX + n // 2 + 2))
                    c = 256 * (n - 9)
                    act.copy(V1[:, 0:2, c:c + 256], PS[:, 2 * s, :].rearrange("p (a b) -> p a b", a=2))
                    act.copy(V1[0:META, 2, c:c + 256], PS[0:META, 2 * s + 1, 0:256]).then_inc(unit_taken[s], 1)

                def copy_head(h):
                    act.wait_ge(ret_out, l * 4 + h + 1)
                    act.copy(OT[:, h, :], PS[:, 7, 0:L1]).then_inc(ret_copied, 1)

                act.wait_ge(mix_step, l * MIX_STEPS + 13)
                act.activation(CSQ, ACC, ACT.Square).then_inc(cv_squared, 1)
                copy_head(0)
                act.wait_ge(cv_var, l + 1)
                act.activation(CSTD, PS[:, 1, 0:L1], ACT.Sqrt, bias=EPS5[:, 0:1]).then_inc(cv_std, 1)
                for h in range(1, RH):
                    copy_head(h)
                act.wait_ge(mix_step, l * MIX_STEPS + 15)
                for t in range(2):
                    act.activation(CY[:, t, :], ACC[:, t, :], ACT.Silu, scale=VEC[:, V_CG + t:V_CG + t + 1],
                                   bias=VEC[:, V_CB + t:V_CB + t + 1]).then_inc(cv_silu, 1)
                act.wait_ge(mix_step, l * MIX_STEPS + 16)
                act.activation(SL[:, 0:4, :], OT, ACT.Square).then_inc(gn_squared, 1)
                act.wait_ge(gn_stat, l * 3 + 3)
                act.activation(STD4, PS[:, 4:8, 0:L1], ACT.Sqrt, bias=EPS5[:, 0:1]).then_inc(gn_std, 1)
                vec_norm(2)
                ffn_gate(l, u + U_FFN_B, None)
                vec_norm(3)

            st = Steps(act, act_step)

            def rms_stats(e, src, c0, wait_tile):
                for c in range(4):
                    wait_tile(c)
                    act.activation(SQ[:, 2 * c:2 * c + 2, c0:L2], src[:, 2 * c:2 * c + 2, c0:L2], ACT.Square)\
                        .then_inc(rm_squared, 1)
                act.wait_ge(rm_var, e + 1)
                act.activation(RSTD[:, c0:L2], PS[:, 4, 0:L2 - c0], ACT.Sqrt, bias=EPS6[:, 0:1]).then_inc(rm_std, 1)

            def rms_in(e, l, which, c0, wait_tile):
                rms_stats(e, X, c0, wait_tile)
                for k in range(CT):
                    if k % 2 == 0:
                        act.wait_ge(rm_scaled, 4 * e + k // 2 + 1)
                    for g in range(c0 // CTX, 2):
                        cols = slice(g * CTX, (g + 1) * CTX)
                        last = act.activation(PRE[:, k, cols], PRE[:, k, cols], ACT.Identity,
                                              scale=GIN[:, l, which, k, g:g + 1],
                                              bias=MOD[:, l, 24 * which + k, g:g + 1])
                    last.then_inc(rm_in, 1)

            def conv_taps(s, done, free, n, vec, ngrp):
                if free is not None:
                    act.wait_ge(tap_prod[s], free)
                act.wait_ge(unit_done[s], done)
                cb, ac = CB[s], AC[s]
                src = PS[:, 2 * s:2 * s + 2, 0:n]
                if ngrp == 2:
                    for a in range(2):
                        act.copy(cb[:, a, :, 1:257], PS[:, 2 * s + a, :].rearrange("p (g t) -> p g t", g=2))
                else:
                    act.copy(cb[:, :, 1, 1:257], src)
                for a in range(2):
                    o = ac[:, a, :, :] if ngrp == 2 else ac[:, a, 1, :]
                    i = PS[:, 2 * s + a, :].rearrange("p (g t) -> p g t", g=2) if ngrp == 2 else PS[:, 2 * s + a, 0:n]
                    last = act.activation(o, i, ACT.Identity, scale=vec(a, 1), bias=vec(a, 3))
                last.then_inc(unit_taken[s], 1)

            def ffn2(f, u, n, ngrp):
                with act.Fori(0, PAIRS_UP) as i:
                    for s in range(2):
                        conv_taps(s, i + (u + 2), i + (2 + PAIRS_UP * f), n,
                                  lambda a, c: FCW[f].rearrange("p f a c -> p f (a c)")[:, bass.ds(i * 2 + s, 1), 4 * a + c],
                                  ngrp)
                        act.wait_ge(tap_side[s], i + (2 + PAIRS_UP * f + 1))
                        act.activation(SG[:, s, 0:n], AC[s][:, 1, 2 - ngrp:2, :].rearrange("p g t -> p (g t)"),
                                       ACT.Silu).then_inc(tap_silu[s], 1)

            def softmax(items, base):
                for n, it in enumerate(items):
                    b = base + n
                    w = it["keys"]
                    act.wait_ge(at_max, b + 1)
                    if n >= 2:
                        act.wait_ge(at_turned, b - 1)
                    act.activation(PR[n % 2][:, 0:w], SS[n % 2][:, 0:w] if it["sb"] else PS[:, 4 + n % 2, 0:w],
                                   ACT.Exp, bias=STAT[:, 4 + n % 2:5 + n % 2],
                                   scale=1.0 if it["sb"] else it["scale"],
                                   accum_out=STAT[:, 8 + n % 2:9 + n % 2]).then_inc(at_exp, 1)
                    if n >= 1:
                        copy_turned(items, base, n - 1)
                copy_turned(items, base, len(items) - 1)

            def copy_turned(items, base, n):
                act.wait_ge(at_turned, base + n + 1)
                if base + n >= 2:
                    act.wait_ge(at_pv, base + n - 1)
                nk = items[n]["keys"] // P
                act.copy(PTT[n % 2][:, 0:nk, :], PS[:, 6, 0:nk * P].rearrange("p (a b) -> p a b", a=nk))\
                    .then_inc(at_copied, 1)

            def first_tiles(c):
                if c == 0:
                    act.wait_ge(ctx_loaded, 16)
                    act.wait_ge(ln_out, 56)

            def after_pairs(u):
                def wait(c):
                    if c == 0:
                        for s in range(2):
                            act.wait_ge(unit_taken[s], u + 1)
                return wait

            def after_post(e):
                return lambda c: act.wait_ge(rm_out, 8 * e + 2 * c + 2)

            act.wait_ge(gains_step, GAIN_STEPS)
            rms_in(0, 0, 0, 0, first_tiles)
            act.wait_ge(tab_loaded, 16 * N_TABLES)
            act.wait_ge(borders_zero, 2)
            for n in range(4, 8):
                s, j = n % 2, n - 4
                conv_taps(s, U_EVEN + n // 2 + 2, j // 2 or None, L2, lambda a, c: EVW[:, 2 * j + a, c:c + 1], 2)
                act.wait_ge(tap_side[s], j // 2 + 1)
                for a in range(2):
                    last = act.activation(G[:, 8 + 2 * j + a, :], AC[s][:, a, :, :].rearrange("p g t -> p (g t)"),
                                          ACT.Silu)
                last.then_inc(tap_prod[s], 1)
            for n in (8, 9):
                s = n % 2
                act.wait_ge(unit_done[s], U_EVEN + n // 2 + 2)
                act.activation(G[:, 16 + 2 * (n - 8):18 + 2 * (n - 8), :], PS[:, 2 * s:2 * s + 2, :], ACT.Sigmoid)\
                    .then_inc(unit_taken[s], 1)
            for n in range(10, 14):
                s, c = n % 2, 256 * (n % 2)
                act.wait_ge(unit_done[s], U_EVEN + n // 2 + 2)
                act.copy((VN if n < 12 else VM)[:, :, c:c + 256],
                         PS[:, 2 * s:2 * s + 2, :].rearrange("p a (b c) -> p (a b) c", b=2)).then_inc(unit_taken[s], 1)
            act.wait_ge(vec_step, ABS_AT)
            st.link(act.activation(GE, GE, ACT.Exp, scale=-1.0))
            st.did(act.activation(GE, GE, ACT.Ln, bias=1.0))
            for h in range(MLH):
                act.wait_ge(ml_bc, h + 1)
                if h >= 1:
                    act.wait_ge(ml_probs, 4 * h)
                for d in range(2):
                    last = act.copy(GB[:, d, :], PS[:, 4 + d, :])
                last.then_inc(ml_bcopied, 1)
                for t in range(4):
                    n, nk = 4 * h + t, 2 if t < 2 else 4
                    act.wait_ge(ml_arg, n + 1)
                    for d in range(2):
                        act.activation(TM[:, d, 0:nk * P], TM[:, d, 0:nk * P], ACT.Exp, bias=STAT[:, 18 + d:19 + d])
                    act.activation(STAT[:, 20:22], STAT[:, 20:22], ACT.Exp).then_inc(ml_w, 1)
                    act.wait_ge(ml_turned, n + 1)
                    act.copy(PTT[n % 2][:, 0:nk, :], PS[:, 7, 0:nk * P].rearrange("p (a b) -> p a b", a=nk))\
                        .then_inc(ml_copied, 1)
            act.wait_ge(vec_step, MLC_AT)
            act.activation(SQ[:, 0:4, :], G[:, 16:20, :], ACT.Square).then_inc(ml_out, 1)
            act.wait_ge(pe_step, 4)
            act.activation(SQ[:, 4:8, :], PS[:, 4:8, :], ACT.Sqrt, bias=EPS6[:, 0:1]).then_inc(ml_out, 1)
            softmax(EVEN_ITEMS, 0)
            for n in range(14, 18):
                s, k = n % 2, 2 * (n - 14)
                act.wait_ge(unit_done[s], U_EVEN + n // 2 + 2)
                act.copy(PRE[:, k:k + 2, :], PS[:, 2 * s:2 * s + 2, :]).then_inc(unit_taken[s], 1)
            rms_stats(1, PRE, 0, after_pairs(U_EVEN + PAIRS_EVEN))
            rms_in(2, 0, 1, 0, after_post(0))
            ffn2(0, U_FFN2[0], L2, 2)
            rms_stats(3, PRE, 0, after_pairs(U_FFN2[0] + PAIRS_FFN))
            rms_in(4, 1, 0, 0, after_post(1))
            act.wait_ge(unit_done[0], U_ODD + 2)
            act.copy(DQ, PS[:, 0:2, 0:SEQ])
            act.activation(SQ[:, 0:2, 0:SEQ], PS[:, 0:2, 0:SEQ], ACT.Square).then_inc(unit_taken[0], 1)
            act.wait_ge(unit_done[1], U_ODD + 2)
            act.wait_ge(odd_loaded, 16 * N_ODD)
            act.copy(CKV, PS[:, 2, :])
            act.copy(KPE, PS[:, 3, :])
            act.activation(SQ[:, 2, :], PS[:, 2, :], ACT.Square).then_inc(unit_taken[1], 1)
            act.wait_ge(pe_step, 5)
            act.activation(SQ[:, 3, 0:SEQ], PS[:, 4, 0:SEQ], ACT.Sqrt, bias=EPS6[:, 0:1])
            st.did(act.activation(SQ[:, 4, :], PS[:, 5, :], ACT.Sqrt, bias=EPS6[:, 0:1]))
            for n in range(4):
                s = n % 2
                act.wait_ge(unit_done[s], U_ODD + 1 + n // 2 + 2)
                act.copy(QT[:, 3 * n:3 * n + 2, :], PS[:, 2 * s, :].rearrange("p (a b) -> p a b", a=2))
                act.copy(QT[:, 3 * n + 2, :], PS[:, 2 * s + 1, 0:SEQ]).then_inc(unit_taken[s], 1)
            for n in range(4):
                s = n % 2
                act.wait_ge(unit_done[s], U_ODD + 3 + n // 2 + 2)
                act.copy(KN[:, 2 * n:2 * n + 2, :], PS[:, 2 * s:2 * s + 2, :]).then_inc(unit_taken[s], 1)
            for n in range(4):
                s = n % 2
                act.wait_ge(unit_done[s], U_ODD + 5 + n // 2 + 2)
                act.copy(VV[:, n, :].rearrange("p (a b) -> p a b", a=2), PS[:, 2 * s:2 * s + 2, :])\
                    .then_inc(unit_taken[s], 1)
            softmax(ODD_ITEMS, len(EVEN_ITEMS))
            for n in range(4):
                s, k = n % 2, 2 * n
                act.wait_ge(unit_done[s], U_ODD + 7 + n // 2 + 2)
                act.copy(PRE[:, k:k + 2, CTX:L2], PS[:, 2 * s:2 * s + 2, 0:SEQ]).then_inc(unit_taken[s], 1)
            rms_stats(5, PRE, CTX, after_pairs(U_ODD + PAIRS_ODD))
            rms_in(6, 1, 1, CTX, after_post(2))
            ffn2(1, U_FFN2[1], SEQ, 1)
            rms_stats(7, PRE, CTX, after_pairs(U_FFN2[1] + PAIRS_FFN))

        @block.vector
        def _(v):
            for s in range(2):
                v.memset(SG[:, s, :], 0.0).then_inc(unit_taken[s], 1)
            v.wait_ge(start_loaded, 16 * N_START)
            with v.Fori(0, PAIRS_ADA) as i:
                for s in range(2):
                    v.wait_ge(unit_done[s], i + 2)
                    v.tensor_tensor(MOD[:, 0, bass.ds(i * 4 + 2 * s, 2), :], PS[:, 2 * s:2 * s + 2, 0:2],
                                    ADAB[:, 0, bass.ds(i * 4 + 2 * s, 2)].rearrange("p (a o) -> p a o", o=1)
                                    .to_broadcast([P, 2, 2]), ALU.add).then_inc(unit_taken[s], 1)
            with v.Fori(0, PAIRS_ADA) as i:
                for s in range(2):
                    v.wait_ge(unit_done[s], i + (PAIRS_ADA + 2))
                    v.tensor_tensor(MOD[:, 1, bass.ds(i * 4 + 2 * s, 2), :], PS[:, 2 * s:2 * s + 2, 0:2],
                                    ADAB[:, 1, bass.ds(i * 4 + 2 * s, 2)].rearrange("p (a o) -> p a o", o=1)
                                    .to_broadcast([P, 2, 2]), ALU.add).then_inc(unit_taken[s], 1)
            for s in range(2):
                v.wait_ge(unit_taken[s], U0 + 1)
            gst = Steps(v, gains_step)
            for l in range(DEPTH):
                for w in range(2):
                    m = MOD[:, l, 24 * w:24 * w + 24, :]
                    gst.did(v.tensor_scalar(GIN[:, l, w, :, :], m[:, 8:16, :], 1.0, None, ALU.add))
                    for g in range(2):
                        gst.did(v.tensor_tensor(GOUT[:, l, w, :, g], m[:, 16:24, g], NG[:, l, 2 * w + 1, :], ALU.mult))
            gst.wait()
            for l in range(DEPTH):
                for w in range(2):
                    for g in range(2):
                        gst.did(v.tensor_tensor(GIN[:, l, w, :, g], GIN[:, l, w, :, g], NG[:, l, 2 * w, :], ALU.mult))
            assert gst.n == GAIN_STEPS

            def bc(t, n):
                return t.rearrange("p (o n) -> p o n", o=1).to_broadcast([P, n, t.shape[-1]])

            def layer_norm(l, e):
                v.wait_ge(ln_mean, lay(l, 3, e + 1))
                for c in range(4):
                    q = PL[:, 2 * c:2 * c + 2, :]
                    v.tensor_tensor(q, q, bc(PS[:, 4, 0:L1], 2), ALU.subtract).then_inc(ln_centred, 1)
                v.wait_ge(ln_std, lay(l, 3, e + 1))
                v.reciprocal(RSTD[:, 0:L1], RSTD[:, 0:L1]).then_inc(ln_rstd, 1)
                v.wait_ge(ln_rstd, lay(l, 3, e + 1))
                for c in range(4):
                    q = PL[:, 2 * c:2 * c + 2, :]
                    v.tensor_tensor(q, q, bc(RSTD[:, 0:L1], 2), ALU.mult).then_inc(ln_scaled, 1)

            def ffn_half(l, u, f):
                with v.Fori(0, PAIRS_UP) as i:
                    for s in range(2):
                        v.wait_ge(silu_done[s], l * (2 * PAIRS_UP) + i + (f * PAIRS_UP + 1))
                        v.tensor_tensor(G[:, bass.ds(i * 2 + s, 1), 0:L1],
                                        SG[:, s, 0:L1].rearrange("p (o n) -> p o n", o=1),
                                        PS[:, 2 * s + 1, 0:L1].rearrange("p (o n) -> p o n", o=1), ALU.mult)\
                            .then_inc(unit_taken[s], 1)
                v.wait_ge(residual_scaled, l * 3 + (1 if f == 0 else 3))
                v.sem_inc(passed["vector"], 1)
                with v.Fori(0, PAIRS_DN) as i:
                    for s in range(2):
                        v.wait_ge(unit_done[s], u + i + (PAIRS_UP + 2))
                        q = PL[:, bass.ds(i * 2 + s, 1), :]
                        v.scalar_tensor_tensor(q, PS[:, 2 * s, 0:L1].rearrange("p (o n) -> p o n", o=1), 0.5, q,
                                               ALU.mult, ALU.add).then_inc(unit_taken[s], 1)

            layer_norm(None, 0)

            with v.Fori(0, DEPTH) as l:
                u = l * PAIRS_LAYER
                ffn_half(l, u + U_FFN_A, 0)
                layer_norm(l, 1)
                st = Steps(v, mix_step, l * MIX_STEPS, MIX_STEPS)

                def taken(n):
                    s = n % 2
                    v.wait_ge(unit_done[s], u + (U_MIX + n // 2 + 2))
                    return s, PS[:, 2 * s:2 * s + 2, 0:L1]

                s, b = taken(0)
                v.tensor_copy(XP[:, :, 16:16 + L1], b).then_inc(unit_taken[s], 1)
                s, b = taken(1)
                v.tensor_copy(CA, b).then_inc(unit_taken[s], 1)
                v.wait_ge(conv_gate, l + 1)
                v.wait_ge(unit_taken[1], u + (U_MIX + 2))
                v.tensor_tensor(CP[:, :, TAPS - 1:TAPS - 1 + L1], CA, CSG, ALU.mult).then_inc(unit_taken[0], 1)
                v.wait_ge(unit_taken[0], u + (U_MIX + 3))
                v.wait_ge(vec_loaded, l * 32 + 32)

                def taps(a, b):
                    for t in range(a, b):
                        for j in range(2):
                            w = VEC[:, V_DW + 2 * t + j:V_DW + 2 * t + j + 1]
                            if t == 0:
                                ins = v.tensor_scalar(ACC[:, j, :], CP[:, j, 0:L1], w,
                                                      VEC[:, V_DB + j:V_DB + j + 1], ALU.mult, ALU.add)
                            else:
                                v.wait_ge(conv_tap, l * 62 + (2 * t + j - 1))
                                ins = v.scalar_tensor_tensor(ACC[:, j, :], CP[:, j, t:t + L1], w, ACC[:, j, :],
                                                             ALU.mult, ALU.add)
                            ins.then_inc(conv_tap, 1)

                def rotate(n):
                    s, b = taken(n)
                    if st.n:
                        st.wait()
                    st.did(v.tensor_tensor(T1, b, bc(RC, 2), ALU.mult))
                    st.did(v.tensor_tensor(T2[:, 0, :], PS[:, 2 * s + 1, 0:L1], RS[:, 0, :], ALU.mult))
                    v.tensor_tensor(T2[:, 1, :], PS[:, 2 * s, 0:L1], RS[:, 1, :], ALU.mult)\
                        .then_inc(unit_taken[s], 1)
                    v.wait_ge(unit_taken[s], u + (U_MIX + n // 2 + 2))
                    st.wait()
                    st.did(v.tensor_tensor(QK[:, 2 * (n - 3):2 * (n - 3) + 2, :], T1, T2, ALU.add))

                for j, n in enumerate((3, 4, 5, 6)):
                    taps(8 * j, min(8 * j + 8, TAPS))
                    rotate(n)

                def decay(h):
                    v.wait_ge(ret_scores, l * 4 + h + 1)
                    if h >= 2:
                        v.wait_ge(ret_out, l * 4 + h - 1)
                    v.tensor_tensor(ST[:, h % 2, 0:2, :], PS[:, 4:6, 0:L1], DT[:, h, 0:2, :], ALU.mult)
                    v.tensor_tensor(ST[0:META, h % 2, 2, :], PS[0:META, 6, 0:L1], DT[0:META, h, 2, :], ALU.mult)\
                        .then_inc(ret_decayed, 1)

                decay(0)
                v.wait_ge(cv_mean, l + 1)
                st.did(v.tensor_tensor(ACC, ACC, bc(PS[:, 0, 0:L1], 2), ALU.subtract))
                decay(1)
                decay(2)
                v.wait_ge(cv_std, l + 1)
                st.link(v.reciprocal(CSTD, CSTD))
                st.did(v.tensor_tensor(ACC, ACC, bc(CSTD, 2), ALU.mult))
                decay(3)
                v.wait_ge(gn_stat, l * 3 + 1)
                st.did(v.tensor_tensor(OT, OT, PS[:, 4:8, 0:L1], ALU.subtract))
                v.wait_ge(gn_stat, l * 3 + 2)
                for t in range(2):
                    last = v.tensor_scalar(YM[:, t, :], PS[:, 2 + t, 0:L1], VEC[:, V_PS + t:V_PS + t + 1], None,
                                           ALU.mult)
                last.then_inc(pooled_taken, 1)
                s, b = taken(11)
                v.tensor_copy(YM[:, 2:4, :], b).then_inc(unit_taken[s], 1)
                v.wait_ge(gn_std, l + 1)
                st.link(v.reciprocal(STD4, STD4))
                st.link(v.tensor_tensor(OT, OT, STD4, ALU.mult))
                for h in range(RH):
                    v.scalar_tensor_tensor(YM[:, 4 + h, :], OT[:, h, :], VEC[:, V_GN + h:V_GN + h + 1], GS[:, h, :],
                                           ALU.mult, ALU.mult).then_inc(gn_y, 1)
                v.wait_ge(residual_scaled, l * 3 + 2)
                for n in range(12, 16):
                    s, b = taken(n)
                    q = PL[:, 2 * (n - 12):2 * (n - 12) + 2, :]
                    ins = v.tensor_tensor(q, b, q, ALU.add)
                    ins.then_inc(unit_taken[s], 1)
                st.end()
                layer_norm(l, 2)
                ffn_half(l, u + U_FFN_B, 1)
                layer_norm(l, 3)

            st = Steps(v, vec_step)

            def rms_scale(e, src, c0):
                v.wait_ge(rm_std, e + 1)
                v.reciprocal(RSTD[:, c0:L2], RSTD[:, c0:L2]).then_inc(rm_rstd, 1)
                v.wait_ge(rm_rstd, e + 1)
                for c in range(4):
                    v.tensor_tensor(PRE[:, 2 * c:2 * c + 2, c0:L2], src[:, 2 * c:2 * c + 2, c0:L2],
                                    bc(RSTD[:, c0:L2], 2), ALU.mult).then_inc(rm_scaled, 1)

            def rms_post(e, l, which, c0):
                rms_scale(e, PRE, c0)
                for k in range(CT):
                    if k % 2 == 0:
                        v.wait_ge(rm_scaled, 4 * e + k // 2 + 1)
                    for g in range(c0 // CTX, 2):
                        cols = slice(g * CTX, (g + 1) * CTX)
                        last = v.scalar_tensor_tensor(X[:, k, cols], PRE[:, k, cols], GOUT[:, l, which, k, g:g + 1],
                                                      X[:, k, cols], ALU.mult, ALU.add)
                    last.then_inc(rm_out, 1)

            def side_taps(s, mid, vec, ngrp):
                v.wait_ge(unit_taken[s], mid)
                for a in range(2):
                    for c in (0, 2):
                        ac, cb = AC[s][:, a, :, :], CB[s][:, a, :, :]
                        if ngrp == 1:
                            ac, cb = ac[:, 1:2, :], cb[:, 1:2, :]
                        if c == 2:
                            st_side[s].wait()
                        ins = v.scalar_tensor_tensor(ac, cb[:, :, c:c + 256], vec(a, c), ac, ALU.mult, ALU.add)
                        if c == 0:
                            st_side[s].did(ins)
                        elif a == 0:
                            st_side[s].did(ins)
                ins.then_inc(tap_side[s], 1)

            class LoopSteps:
                def __init__(self, s):
                    self.s, self.base, self.n = s, 0, 0

                def did(self, ins):
                    self.n += 1
                    ins.then_inc(self.s, 1)

                def wait(self):
                    v.wait_ge(self.s, self.base + self.n)

            st_side = [LoopSteps(side_step[0]), LoopSteps(side_step[1])]

            def ffn2(f, u, n, ngrp):
                for s in range(2):
                    base0 = 3 * (2 + PAIRS_UP * f)
                    st_side[s].base, st_side[s].n = base0, 0
                with v.Fori(0, PAIRS_UP) as i:
                    for s in range(2):
                        st_side[s].base = i * 3 + base0
                        st_side[s].n = 0
                        side_taps(s, i + (u + 2),
                                  lambda a, c: FCW[f].rearrange("p f a c -> p f (a c)")[:, bass.ds(i * 2 + s, 1), 4 * a + c],
                                  ngrp)
                        v.wait_ge(tap_silu[s], i + (PAIRS_UP * f + 1))
                        v.tensor_tensor(G[:, bass.ds(i * 2 + s, 1), 0:n],
                                        AC[s][:, 0:1, 2 - ngrp:2, :].rearrange("p o g t -> p o (g t)"),
                                        SG[:, s, 0:n].rearrange("p (o n) -> p o n", o=1), ALU.mult)\
                            .then_inc(tap_prod[s], 1)
                with v.Fori(0, PAIRS_DN) as i:
                    for s in range(2):
                        v.wait_ge(unit_done[s], i + (u + PAIRS_UP + 2))
                        v.tensor_scalar(PRE[:, bass.ds(i * 2 + s, 1), L2 - n:L2],
                                        PS[:, 2 * s, 0:n].rearrange("p (o n) -> p o n", o=1), 1.0, None, ALU.mult)\
                            .then_inc(unit_taken[s], 1)

            def attend(items, base):
                def top(n):
                    it, b = items[n], base + n
                    w = it["keys"]
                    v.wait_ge(at_scores, b + 1)
                    src = PS[:, 4 + n % 2, 0:w]
                    if it["sb"]:
                        if n >= 2:
                            v.wait_ge(at_exp, b - 1)
                        st.did(v.tensor_scalar(SS[n % 2][:, 0:CTX], src[:, 0:CTX], it["scale"], None, ALU.mult))
                        st.did(v.scalar_tensor_tensor(SS[n % 2][:, CTX:L2], src[:, CTX:L2], it["scale"], it["bias"],
                                                      ALU.mult, ALU.add))
                        st.wait()
                        src = SS[n % 2][:, 0:w]
                    st.link(v.tensor_reduce(STAT[:, n % 2:n % 2 + 1], src, AX.X, ALU.max))
                    v.tensor_scalar(STAT[:, 4 + n % 2:5 + n % 2], STAT[:, n % 2:n % 2 + 1],
                                    -1.0 if it["sb"] else -it["scale"], None, ALU.mult).then_inc(at_max, 1)

                def norm(n):
                    it, b = items[n], base + n
                    v.wait_ge(at_exp, b + 1)
                    st.link(v.reciprocal(STAT[:, 12 + n % 2:13 + n % 2], STAT[:, 8 + n % 2:9 + n % 2]))
                    q = PR[n % 2][:, 0:it["keys"]]
                    v.tensor_scalar(q, q, STAT[:, 12 + n % 2:13 + n % 2], None, ALU.mult).then_inc(at_probs, 1)

                def place(n):
                    it, b = items[n], base + n
                    v.wait_ge(at_pv, b + 1)
                    v.tensor_copy(it["out"], PS[it["rows"], 7, 0:P]).then_inc(at_out, 1)

                top(0)
                for n in range(len(items)):
                    if n + 1 < len(items):
                        top(n + 1)
                    norm(n)
                    if n >= 2:
                        place(n - 2)
                for n in range(len(items) - 2, len(items)):
                    place(n)

            v.wait_ge(gains_step, GAIN_STEPS)
            rms_scale(0, X, 0)
            for n in range(4):
                s = n % 2
                v.wait_ge(unit_done[s], U_EVEN + n // 2 + 2)
                v.tensor_copy(G[:, 2 * n:2 * n + 2, :], PS[:, 2 * s:2 * s + 2, :]).then_inc(unit_taken[s], 1)
            for n in range(4, 8):
                s, j = n % 2, n - 4
                st_side[s].base, st_side[s].n = 3 * (j // 2), 0
                side_taps(s, U_EVEN + n // 2 + 2, lambda a, c: EVW[:, 2 * j + a, c:c + 1], 2)
            v.wait_ge(pe_step, 1)
            v.wait_ge(tab_loaded, 16 * N_TABLES)
            st.link(v.tensor_tensor(GT, PS[:, 5, 0:64].rearrange("p (a b) -> p a b", a=4), bc(GBIAS, 4), ALU.add))
            st.link(v.tensor_scalar(GE, GT, -1.0, None, ALU.mult))
            st.did(v.tensor_tensor(GE, GE, GT, ALU.max))
            assert st.n == ABS_AT
            st.link(v.tensor_scalar(LS, GT, 0.0, None, ALU.min))
            v.wait_ge(act_step, 2)
            st.did(v.tensor_tensor(LS, LS, GE, ALU.subtract))
            assert st.n == LS_AT
            v.wait_ge(pe_step, 2)
            st.did(v.tensor_copy(GR[0:4, :, :], PS[0:4, 6:8, :]))
            st.did(v.tensor_copy(NF, PS[:, 4, 0:32].rearrange("p (d t h) -> p d t h", d=2, t=4)))
            assert st.n == NF_AT
            for h in range(MLH):
                for t in range(4):
                    n, nk = 4 * h + t, 2 if t < 2 else 4
                    w = nk * P
                    if t == 0:
                        v.wait_ge(ml_bcopied, h + 1)
                    m0 = (0, 256, 512, 1024)[t]
                    st.wait()
                    for d in range(2):
                        st.did(v.tensor_tensor_reduce(TM[:, d, 0:w], GB[:, d, 0:w], MASK[:, d, m0:m0 + w], 1.0, -3e38,
                                                      ALU.add, ALU.max, STAT[:, 16 + d:17 + d]))
                    st.wait()
                    st.did(v.tensor_scalar(STAT[:, 18:20], STAT[:, 16:18], -1.0, None, ALU.mult))
                    v.tensor_tensor(STAT[:, 20:22], NF[:, :, t, h], STAT[:, 16:18], ALU.subtract).then_inc(ml_arg, 1)
                    v.wait_ge(ml_scores, n + 1)
                    v.wait_ge(ml_w, n + 1)
                    for d in range(2):
                        st.did(v.tensor_tensor_reduce(TM[:, d, 0:w], TM[:, d, 0:w], PS[:, 6, 0:w], 128.0 ** -0.5, 0.0,
                                                      ALU.mult, ALU.add, STAT[:, 22 + d:23 + d]))
                    st.wait()
                    st.link(v.tensor_scalar(STAT[:, 24:26], STAT[:, 22:24], -1.0, None, ALU.mult))
                    st.link(v.tensor_tensor(STAT[:, 24:26], STAT[:, 24:26], STAT[:, 22:24], ALU.max))
                    st.link(v.tensor_tensor(STAT[:, 24:26], STAT[:, 24:26], STAT[:, 20:22], ALU.max))
                    st.link(v.reciprocal(STAT[:, 26:28], STAT[:, 24:26]))
                    if n >= 2:
                        v.wait_ge(ml_turned, n - 1)
                    st.link(v.tensor_scalar(PR[n % 2][:, 0:w], TM[:, 0, 0:w], STAT[:, 26:27], None, ALU.mult))
                    v.scalar_tensor_tensor(PR[n % 2][:, 0:w], TM[:, 1, 0:w], STAT[:, 27:28], PR[n % 2][:, 0:w],
                                           ALU.mult, ALU.add).then_inc(ml_probs, 1)
                    v.wait_ge(ml_probs, n + 1)
                v.wait_ge(ml_pv, h + 1)
                v.tensor_tensor(G[:, 16 + h, :], G[:, 16 + h, :], PS[:, 0, :], ALU.mult).then_inc(ml_out, 1)
            v.wait_ge(pe_step, 3)
            st.did(v.tensor_tensor(G[:, 16:20, :], G[:, 16:20, :], PS[:, 4:8, :], ALU.subtract))
            assert st.n == MLC_AT, st.n
            v.wait_ge(ml_out, 6)
            st.link(v.reciprocal(SQ[:, 4:8, :], SQ[:, 4:8, :]))
            st.link(v.tensor_tensor(G[:, 16:20, :], G[:, 16:20, :], SQ[:, 4:8, :], ALU.mult))
            for h in range(MLH):
                st.did(v.tensor_scalar(YM2[:, 4 + h, :], G[:, 16 + h, :], MLG[:, h:h + 1], None, ALU.mult))
            assert st.n == MLY_AT, st.n
            v.wait_ge(bias_loaded, 16 * ROWS * NAH)
            for h in range(NAH):
                q = BIAS[:, h, :, :, :].rearrange("p q r c -> p (q r) c")
                st.did(v.tensor_tensor(q, q, bc(WIN, 8), ALU.add))
            st.wait()
            attend(EVEN_ITEMS, 0)
            rms_post(1, 0, 0, 0)
            rms_scale(2, X, 0)
            ffn2(0, U_FFN2[0], L2, 2)
            rms_post(3, 0, 1, 0)
            rms_scale(4, X, 0)
            v.wait_ge(act_step, ODD_STD_AT)
            v.wait_ge(odd_loaded, 16 * N_ODD)
            st.did(v.reciprocal(SQ[:, 3, 0:SEQ], SQ[:, 3, 0:SEQ]))
            st.link(v.reciprocal(SQ[:, 4, :], SQ[:, 4, :]))
            st.did(v.tensor_tensor(DQ, DQ, bc(SQ[:, 3, 0:SEQ], 2), ALU.mult))
            st.did(v.tensor_tensor(CKV, CKV, SQ[:, 4, :], ALU.mult))
            st.did(v.tensor_tensor(KPE[:, CTX:L2], KPE[:, CTX:L2], RT[:, 0, :], ALU.mult))
            st.did(v.tensor_tensor(SW[:, 0, :], PS[:, 6, 0:SEQ], RT[:, 1, :], ALU.mult))
            st.wait()
            for t in range(2):
                st.did(v.tensor_scalar(DQ[:, t, :], DQ[:, t, :], QNG[:, t:t + 1], None, ALU.mult))
            st.did(v.tensor_scalar(CKV, CKV, QNG[:, 2:3], None, ALU.mult))
            st.did(v.tensor_tensor(KPE[:, CTX:L2], KPE[:, CTX:L2], SW[:, 0, :], ALU.add))
            assert st.n == ODD_Q_AT, st.n
            v.wait_ge(pe_step, 6)
            st.wait()
            for t in range(4):
                st.did(v.tensor_tensor(SW[:, t, :], PS[:, 4 + t // 2, 256 * (t % 2):256 * (t % 2) + 256], RT[:, 1, :],
                                       ALU.mult))
            q = QT[:, 8:12, :]
            st.link(v.tensor_tensor(q, q, bc(RT[:, 0, :], 4), ALU.mult))
            st.did(v.tensor_tensor(q, q, SW, ALU.add))
            assert st.n == ODD_ROPE_AT, st.n
            attend(ODD_ITEMS, len(EVEN_ITEMS))
            rms_post(5, 1, 0, CTX)
            rms_scale(6, X, CTX)
            ffn2(1, U_FFN2[1], SEQ, 1)
            rms_post(7, 1, 1, CTX)


def feature_major(a):
    return a.T.reshape(-1, P, a.shape[0]).transpose(1, 0, 2)


def columns(v):
    t = v.reshape(v.shape[:-1] + (-1, P))
    return np.moveaxis(t, -1, 0)


def tile_pairs(w):
    f = w.shape[1] // (2 * P)
    return w.reshape(CT, P, f, 2, P).transpose(2, 1, 3, 0, 4).reshape(f, P, 2 * D)


def wide(w):
    f = w.shape[1] // 256
    return w.reshape(CT, P, f, 256).transpose(2, 1, 0, 3).reshape(f, P, 2 * D)


def up_units(w):
    h = w.shape[1] // 2
    w = np.pad(w.reshape(D, 2, h), ((0, 0), (0, 0), (0, FF - h)))
    return w.reshape(CT, P, 2, FT, P).transpose(3, 1, 2, 0, 4).reshape(FT, P, 2 * D)


def down_units(w):
    w = np.pad(w, ((0, FF - w.shape[0]), (0, 0)))
    return w.reshape(FT, P, CT, P).transpose(2, 1, 0, 3).reshape(CT, P, SLOT)


def shape_tables():
    t = {}
    pos = np.arange(L1)
    half = 64
    ang = pos[None, :] * (10000.0 ** (-np.arange(0, 128, 2) / 128.0))[:, None]
    ang = np.concatenate([ang, ang], 0)
    t["rope_c"] = np.cos(ang)
    t["rope_s"] = np.stack([-np.sin(ang), np.sin(ang)], 1)
    decay = np.zeros((P, RH, 3, L1))
    chunk = (pos + (-META) % 64) // 64
    for h in range(RH):
        gamma = 1.0 - 2.0 ** (-5.0 - h)
        m = gamma ** np.abs(pos[None, :] - pos[:, None]) * (chunk[:, None] <= chunk[None, :]) * 128.0 ** -0.5
        for j in range(3):
            rows = m[j * P:(j + 1) * P]
            decay[:len(rows), h, j] = rows
    t["decay"] = decay
    cnt = np.zeros((P, 2, L1))
    for g, w in enumerate((2, 4, 8, 16)):
        cnt[64 * (g % 2):64 * (g % 2) + 64, g // 2] = 1.0 / np.minimum(pos + 1, w)
    t["inv_count"] = cnt
    t["ident"] = np.eye(P)
    s = np.arange(L2)
    is_ctx = s < CTX
    fwd = s[:, None] <= s[None, :]
    bwd = np.where(is_ctx[:, None], np.where(is_ctx[None, :], s[:, None] >= s[None, :], True),
                   np.where(is_ctx[None, :], False, s[:, None] >= s[None, :]))
    seen = np.stack([fwd, bwd]).astype(np.float64)
    t["seen"] = (-seen).reshape(2, 4, P, L2).transpose(2, 0, 1, 3)
    mask = np.where(seen > 0, 0.0, NEG)
    parts = [mask[:, 0:w, q * P:(q + 1) * P].transpose(2, 0, 1) for q, w in ((0, CTX), (1, CTX), (2, L2), (3, L2))]
    t["mask"] = np.concatenate(parts, 2)
    sel = np.zeros((MLH, MLH, P))
    for h in range(MLH):
        sel[h, h] = 1.0
    t["sel"] = sel.reshape(MLH, MLH * P)
    col = np.arange(GRID_W)
    cs = np.clip(col - 8, 0, GRID_W - 16)
    inside = (col[None, :] >= cs[:, None]) & (col[None, :] < cs[:, None] + 16)
    t["win"] = np.tile(np.where(inside, 0.0, NEG), (2, 1))
    d = np.arange(P) % 32
    x = np.arange(SEQ)
    where = np.where((d < 16)[:, None], (x // GRID_W)[None, :], (x % GRID_W)[None, :])
    ang = where * (10000.0 ** (-(d % 8) / 8.0))[:, None]
    t["rope2"] = np.stack([np.cos(ang), np.where((d % 16 < 8)[:, None], -np.sin(ang), np.sin(ang))], 1)
    perm = np.zeros((P, P))
    perm[np.arange(P), np.arange(P) ^ 8] = 1.0
    t["perm"] = perm
    return {k: np.ascontiguousarray(v, dtype=np.float32) for k, v in t.items()}


def lay_out(i):
    cat = np.concatenate
    a = {}
    a["x"] = feature_major(cat([i["meta"], i["x"][0]], 0))
    a["ctx"] = feature_major(i["ctx_2"][0])
    a["c"] = columns(np.stack([i["c_ctx_2"], i["c_2"][0]])).transpose(0, 2, 1)
    a["ln_in"] = columns(np.stack([i["ln_in_g"], i["ln_in_b"]]))
    a["ada"] = cat([tile_pairs(w) for w in i["ada_w_2"]], 0)
    a["ada_b"] = columns(i["ada_b_2"])
    a["norm_g"] = columns(i["norm_g_2"])
    for key, n in (("a", "ffn1"), ("b", "ffn2")):
        a["up_" + key] = cat([up_units(w) for w in i[n + "_w13"]], 0)
        a["dn_" + key] = cat([down_units(w) for w in i[n + "_w2"]], 0)
    a["up_c"] = cat([up_units(w) for w in i["ffn_w_up_2"]], 0)
    a["dn_c"] = cat([down_units(w) for w in i["ffn_w_down_2"]], 0)
    halves = np.array([[h * P + a_ * 64 + e for h in (2 * g, 2 * g + 1) for e in range(64)]
                       for g in range(2) for a_ in range(2)]).reshape(-1)
    mix, vec, pw = [], [], []
    for l in range(DEPTH):
        w = i["w_in"][l]
        pws = i["conv_pw"][l].reshape(2, P, 2, P).transpose(1, 2, 0, 3).reshape(P, 512)
        mix.append(cat([tile_pairs(w[:, 0:768]), tile_pairs(w[:, 768:1280][:, halves]),
                        tile_pairs(w[:, 1280:1792][:, halves]), tile_pairs(w[:, 2304:2816]), wide(w[:, 1792:2304]),
                        np.pad(pws, ((0, 0), (0, 2 * D - 512)))[None], tile_pairs(i["w_out"][l])], 0))
        dw = columns(i["conv_dw"][l]).reshape(P, 2 * TAPS)
        vec.append(cat([columns(i["ln_g"][l]).reshape(P, 24), columns(i["ln_b"][l]).reshape(P, 24),
                        columns(i["pool_scale"][l]), dw, columns(i["conv_db"][l]), columns(i["conv_ln_g"][l]),
                        columns(i["conv_ln_b"][l]), columns(i["ret_gn_g"][l])], 1))
        g4 = i["pool_w"][l]
        blocks = np.zeros((P, 2, P), np.float32)
        for g in range(4):
            q = slice(64 * (g % 2), 64 * (g % 2) + 64)
            blocks[q, g // 2, q] = g4[g]
        pw.append(blocks)
    a["mix"], a["vec"], a["pool_w"] = cat(mix, 0), np.stack(vec), np.stack(pw)
    w = i["ev_w_in_2"][0]
    a["even"] = cat([tile_pairs(w[:, 0:1024]), tile_pairs(w[:, 1536:2560]), tile_pairs(w[:, 3072:3584]),
                     wide(w[:, 1024:1536]), wide(w[:, 2560:3072]), tile_pairs(i["ev_w_out_2"][0])], 0)
    a["wg"] = w[:, 3584:3600].reshape(CT, P, 16).transpose(1, 0, 2)
    a["gate_b"] = np.tile(i["ev_gate_b_2"], (P, 1))
    a["ml_g"] = columns(i["ev_ml_norm_g_2"][0])

    def taps(w, b, lead):
        t = columns(cat([w, b[None]], 0)).transpose(0, 2, 1)
        return t if lead is None else t.reshape(P, 2, -1, 4).transpose(0, 2, 1, 3)
    a["evw"] = taps(i["ev_conv_w_2"][0], i["ev_conv_b_2"][0], None)
    for l in range(DEPTH):
        a[f"fcw{l}"] = taps(i["ffn_conv_w_2"][l], i["ffn_conv_b_2"][l], 2)
    r = i["ev_rpb_2"][0][:, 8 - ROWS:7 + ROWS]
    r = np.pad(r, ((0, 0), (0, 0), (GRID_W - 16, GRID_W - 16)))
    a["rpb"] = np.tile(r, (1, 1, GRID_W))
    kv = i["od_w_dkv_2"][0]
    a["odd"] = cat([tile_pairs(i["od_w_dq_2"][0]), tile_pairs(cat([kv[:, 0:128]] + [kv[:, 128:160]] * 4, 1)),
                    tile_pairs(i["od_w_o_2"][0])], 0)
    uq = i["od_w_uq_2"][0].reshape(256, MLAH, 96)
    uq = cat([uq[:, :, 0:64].reshape(256, 1024), uq[:, :, 64:96].reshape(256, 512)], 1)
    a["uq"] = uq.reshape(2, P, 12, P).transpose(1, 2, 0, 3)
    ukv = i["od_w_ukv_2"][0].reshape(128, MLAH, 128)
    a["ukv"] = cat([ukv[:, :, 0:64].reshape(128, 1024), ukv[:, :, 64:128].reshape(128, 1024)], 1)
    a["qkv_g"] = cat([columns(i["od_q_norm_g_2"][0]), columns(i["od_kv_norm_g_2"][0])], 1)
    a.update(shape_tables())
    return {k: np.ascontiguousarray(v) for k, v in a.items()}


def kernel(**inputs):
    import concourse.bacc as bacc
    from concourse.bass_utils import run_bass_kernel_spmd

    nc = bacc.Bacc("TRN2", target_bir_lowering=False, num_devices=1)
    arrays = {"in_" + k: v for k, v in lay_out({k: np.asarray(v) for k, v in inputs.items()}).items()}
    A = {k[3:]: nc.dram_tensor(k, v.shape, F32, kind="ExternalInput").ap() for k, v in arrays.items()}
    out = nc.dram_tensor("out", (P, CT, SEQ), F32, kind="ExternalOutput").ap()
    build(nc, A, out)
    r = run_bass_kernel_spmd(nc, [arrays], core_ids=[0]).results[0]["out"]
    return np.ascontiguousarray(r.transpose(1, 0, 2).reshape(D, SEQ).T)[None]
```

```python
from contextlib import ExitStack

import numpy as np

import concourse.bass as bass
from concourse import mybir

ALU = mybir.AluOpType
ACT = mybir.ActivationFunctionType
AX = mybir.AxisListType
F32 = mybir.dt.float32

P = 128
D = 1024
CT = D // P
META = 16
SEQ = 256
CTX = 256
L1 = META + SEQ
L2 = CTX + SEQ
X0 = L2 - L1
DEPTH = 2
FT = 22
FF = FT * P
ACT_TILES = 5
SLOT = FT * P
ALPHA = (2.0 * DEPTH) ** 0.25
TAPS = 31
RH = 4
GRID_W = 64
ROWS = SEQ // GRID_W
NAH, NAD = 8, 64
MLH = 4
MLAH = 16
NEG = -1e30
RPB_PERIOD = 2 * GRID_W - 1
RPB_ROW = GRID_W * RPB_PERIOD
N_START, N_TABLES, N_ODD = 9, 10, 5
N_SET = 12

ADA_UNITS = 12
PAIRS_UP, PAIRS_DN = FT // 2, CT // 2
PAIRS_FFN = PAIRS_UP + PAIRS_DN
PAIRS_MIX = 8
PAIRS_LAYER = 2 * PAIRS_FFN + PAIRS_MIX
PAIRS_EVEN = 9
PAIRS_ODD = 9

V_LNG, V_LNB, V_PS, V_DW, V_DB, V_CG, V_CB, V_GN = 0, 24, 48, 50, 112, 114, 116, 118
NV = 122


def build(nc, A, out):
    with ExitStack() as ctx:
        def sb(name, shape):
            return ctx.enter_context(nc.sbuf_tensor(name, shape, F32))

        def sem(name):
            return ctx.enter_context(nc.semaphore(name))

        X = sb("X", [P, CT, L2])
        PRE = sb("PRE", [P, CT, L2])
        SQ = sb("SQ", [P, CT, L2])
        RING = sb("RING", [P, 2, SLOT])
        G = sb("G", [P, FT, L2])
        SG = sb("SG", [P, 2, L2])
        RSTD = sb("RSTD", [P, L2])
        VEC = sb("VEC", [P, NV])
        LNIN = sb("LNIN", [P, 2, CT])
        ONES = sb("ONES", [P, 3, P])
        ONE = sb("ONE", [P, 1])
        EPS5 = sb("EPS5", [P, 1])
        EPS6 = sb("EPS6", [P, 1])
        SC = sb("SC", [P, CT, 2])
        ADAB = sb("ADAB", [P, DEPTH * 48])
        MODF = sb("MOD", [P, DEPTH * 48, 2])
        MOD = MODF[:, :, :].rearrange("p (l m) g -> p l m g", l=DEPTH)
        NG = sb("NG", [P, DEPTH, 4, CT])
        GIN = sb("GIN", [P, DEPTH, 2, CT, 2])
        GOUT = sb("GOUT", [P, DEPTH, 2, CT, 2])
        BW = 21056
        B = sb("B", [P, BW])
        PS = ctx.enter_context(nc.psum_tensor("PS", [P, 8, 512], F32))

        used = {}

        def carve(region, base, words, shape, **dims):
            at = used.get(region, 0)
            used[region] = at + words
            total = {"G1": FT * L2, "G2": FT * L2, "G3": FT * L2}.get(region, BW)
            assert used[region] <= total, (region, used[region], total)
            v = base[:, at:at + words]
            return v.rearrange(shape, **dims) if shape else v

        SUMS = SG
        GF = G[:, :, :].rearrange("p a b -> p (a b)")
        YM = carve("G1", GF, CT * L1, "p (a b) -> p a b", a=CT)
        QK = carve("G1", GF, 8 * L1, "p (a b) -> p a b", a=8)
        V1 = carve("G1", GF, 3 * 512, "p (a b) -> p a b", a=3)
        OT = carve("G1", GF, 4 * L1, "p (a b) -> p a b", a=4)
        STD4 = carve("G1", GF, 4 * L1, "p (a b) -> p a b", a=4)
        GS = carve("G1", GF, 4 * L1, "p (a b) -> p a b", a=4)
        ST = carve("G1", GF, 2 * 3 * L1, "p (z a b) -> p z a b", z=2, a=3)
        DT = carve("B1", B, RH * 3 * L1, "p (h a b) -> p h a b", h=RH, a=3)
        RC = carve("B1", B, L1, None)
        RS = carve("B1", B, 2 * L1, "p (a b) -> p a b", a=2)
        IC = carve("B1", B, 2 * L1, "p (a b) -> p a b", a=2)
        XP = carve("B1", B, 2 * (16 + L1), "p (a b) -> p a b", a=2)
        PT_ = [carve("B1", B, 2 * (16 + L1), "p (a b) -> p a b", a=2) for _ in range(4)]
        WN = carve("B1", B, 2 * L1, "p (a b) -> p a b", a=2)
        PM = carve("B1", B, 2 * L1, "p (a b) -> p a b", a=2)
        CA = carve("B1", B, 2 * L1, "p (a b) -> p a b", a=2)
        CSG = carve("B1", B, 2 * L1, "p (a b) -> p a b", a=2)
        CP = carve("B1", B, 2 * (TAPS - 1 + L1), "p (a b) -> p a b", a=2)
        ACC = carve("B1", B, 2 * L1, "p (a b) -> p a b", a=2)
        T1 = carve("B1", B, 2 * L1, "p (a b) -> p a b", a=2)
        T2 = carve("B1", B, 2 * L1, "p (a b) -> p a b", a=2)
        CY = carve("B1", B, 2 * L1, "p (a b) -> p a b", a=2)
        CSQ = carve("B1", B, 2 * L1, "p (a b) -> p a b", a=2)
        PW = carve("B1", B, 2 * P, "p (a b) -> p a b", a=2)
        CSTD = carve("B1", B, L1, None)
        AW = carve("B1", B, 2 * D, "p (j k c) -> p j k c", j=2, k=CT)
        AP_ = carve("B1", B, 2 * 2 * P, "p (g j c) -> p g j c", g=2, j=2)
        IDN = carve("B2", B, P, None)
        YM2 = carve("B2", B, CT * L2, "p (a b) -> p a b", a=CT)
        CB = [carve("B2", B, 2 * 2 * 258, "p (a g b) -> p a g b", a=2, g=2) for _ in range(2)]
        AC = [carve("B2", B, 2 * L2, "p (a g b) -> p a g b", a=2, g=2) for _ in range(2)]
        FCW = [carve("B2", B, FT * 2 * 4, "p (f a c) -> p f a c", f=FT, a=2) for _ in range(2)]
        TM = carve("B2", B, 2 * 512, "p (d w) -> p d w", d=2)
        SS = [TM[:, 0, :], TM[:, 1, :]]
        PR = [carve("B2", B, 512, None) for _ in range(2)]
        PTT = [carve("B2", B, 512, "p (a b) -> p a b", a=4) for _ in range(2)]
        STAT = carve("B2", B, 64, None)
        b2_shared = used["B2"]
        VN = carve("B2", B, 4 * 512, "p (a b) -> p a b", a=4)
        VM = carve("B2", B, 4 * 512, "p (a b) -> p a b", a=4)
        EVW = carve("B2", B, 8 * 4, "p (f c) -> p f c", c=4)
        WG = carve("B2", B, CT * 16, "p (a b) -> p a b", a=CT)
        MASK = carve("B2", B, 2 * 3 * 512, "p (d w) -> p d w", d=2)
        GB = carve("B2", B, 2 * 512, "p (d w) -> p d w", d=2)
        GR = SG
        SEL = carve("B2", B, MLH * P, None)
        GBIAS = carve("B2", B, 16, None)
        GT = carve("B2", B, 64, "p (a b) -> p a b", a=4)
        GE = carve("B2", B, 64, "p (a b) -> p a b", a=4)
        LS = carve("B2", B, 64, "p (a b) -> p a b", a=4)
        NF = carve("B2", B, 32, "p (d t h) -> p d t h", d=2, t=4)
        MLG = carve("B2", B, MLH, None)
        used["B3"] = b2_shared
        WUQ = carve("B3", B, 12 * 2 * P, "p (f k c) -> p f k c", f=12, k=2)
        WUKV = carve("B3", B, 2 * D, None)
        DQ = carve("B3", B, 2 * SEQ, "p (a b) -> p a b", a=2)
        CKV = carve("B3", B, L2, None)
        KPE = carve("B3", B, L2, None)
        RT = carve("B3", B, 2 * SEQ, "p (a b) -> p a b", a=2)
        PERM = carve("B3", B, P, None)
        SW = carve("B3", B, 4 * SEQ, "p (a b) -> p a b", a=4)
        QNG = carve("B3", B, 3, None)
        QT = carve("G3", GF, 12 * SEQ, "p (a b) -> p a b", a=12)
        KN = carve("G3", GF, 8 * L2, "p (a b) -> p a b", a=8)
        VV = carve("G3", GF, 4 * D, "p (a b) -> p a b", a=4)
        SQF = SQ[:, :, :].rearrange("p a b -> p (a b)")
        NU = SQF.rearrange("p (d s t) -> p d s t", d=2, s=4)
        BIAS = PRE[:, :, :].rearrange("p a (q r c) -> p a q r c", q=2, r=ROWS)

        WIN = carve("B2", B, GRID_W, None)

        def item(qk, keys, scale, v, rows, o, bias=None):
            return {"qk": qk, "keys": keys, "scale": scale, "v": v, "rows": rows, "out": o, "bias": bias,
                    "sb": bias is not None}

        def na_item(h, t):
            q = slice(64 * (h % 2), 64 * (h % 2) + 64)
            keys = CTX if t < 2 else L2
            return item([(G[q, h // 2, t * P:(t + 1) * P], G[q, 4 + h // 2, 0:keys])], keys, NAD ** -0.5,
                        lambda j: VN[:, j, h * NAD:(h + 1) * NAD], q, YM2[q, h // 2, t * P:(t + 1) * P],
                        None if t < 2 else BIAS[:, h, t - 2, :, :].rearrange("p r c -> p (r c)"))

        def mla_item(h, t):
            q, r = slice(64 * (h % 2), 64 * (h % 2) + 64), slice(32 * (h % 4), 32 * (h % 4) + 32)
            cols = slice(t * P, (t + 1) * P)
            return item([(QT[q, h // 2, cols], KN[q, h // 2, :]), (QT[r, 8 + h // 4, cols], KPE[r, :])],
                        L2, 96.0 ** -0.5, lambda j: VV[:, j, h * 64:(h + 1) * 64], q,
                        YM2[q, h // 2, CTX + t * P:CTX + (t + 1) * P])

        EVEN_ITEMS = [na_item(h, t) for t in range(4) for h in range(NAH)]
        ODD_ITEMS = [mla_item(h, t) for h in range(MLAH) for t in range(2)]

        GAIN_STEPS = DEPTH * 2 * 5
        ABS_AT = 3
        LS_AT = ABS_AT + 2
        NF_AT = LS_AT + 2
        MLC_AT = NF_AT + 4 * MLH * 10 + 1
        MLY_AT = MLC_AT + 2 + MLH
        EVEN_AT = MLY_AT + NAH + sum(4 if i["sb"] else 2 for i in EVEN_ITEMS) + 1
        ODD_Q_AT = EVEN_AT + 11
        ODD_ROPE_AT = ODD_Q_AT + 6
        ODD_STD_AT = 3

        XL = X[:, :, X0:L2]
        PL = PRE[:, :, 0:L1]
        SL = SQ[:, :, 0:L1]

        w_loaded = [sem("w_loaded0"), sem("w_loaded1")]
        unit_done = [sem("unit_done0"), sem("unit_done1")]
        unit_taken = [sem("unit_taken0"), sem("unit_taken1")]
        start_loaded = sem("start_loaded")
        start_set = sem("start_set")
        vec_loaded = sem("vec_loaded")
        silu_c = sem("silu_c")
        ada_loaded, ada_summed, ada_done, ada_taken = (sem("ada_loaded"), sem("ada_summed"), sem("ada_done"),
                                                       sem("ada_taken"))
        ada_step, ada_last_loaded = sem("ada_step"), sem("ada_last_loaded")
        gains_step = sem("gains_step")
        silu_done = [sem("silu_done0"), sem("silu_done1")]
        residual_scaled = sem("residual_scaled")
        ln_mean, ln_centred, ln_squared, ln_var = sem("ln_mean"), sem("ln_centred"), sem("ln_squared"), sem("ln_var")
        ln_std, ln_rstd, ln_scaled, ln_out = sem("ln_std"), sem("ln_rstd"), sem("ln_scaled"), sem("ln_out")
        sum_added, sum_squared = sem("sum_added"), sem("sum_squared")
        conv_gate, silu_g = sem("conv_gate"), sem("silu_g")
        mix_step, conv_tap, pool_step = sem("mix_step"), sem("conv_tap"), sem("pool_step")
        ret_scores, ret_decayed, ret_out, ret_copied = (sem("ret_scores"), sem("ret_decayed"), sem("ret_out"),
                                                        sem("ret_copied"))
        cv_mean, cv_squared, cv_var, cv_std, cv_silu = (sem("cv_mean"), sem("cv_squared"), sem("cv_var"),
                                                        sem("cv_std"), sem("cv_silu"))
        gn_stat, gn_squared, gn_std, gn_y = sem("gn_stat"), sem("gn_squared"), sem("gn_std"), sem("gn_y")
        pooled_taken = sem("pooled_taken")
        ctx_loaded, tab_loaded, u_loaded, bias_loaded, odd_loaded = (sem("ctx_loaded"), sem("tab_loaded"),
                                                                     sem("u_loaded"), sem("bias_loaded"),
                                                                     sem("odd_loaded"))
        rm_squared, rm_var, rm_std, rm_rstd, rm_scaled, rm_in, rm_out = (
            sem("rm_squared"), sem("rm_var"), sem("rm_std"), sem("rm_rstd"), sem("rm_scaled"), sem("rm_in"),
            sem("rm_out"))
        side_step = [sem("side_step0"), sem("side_step1")]
        tap_side = [sem("tap_side0"), sem("tap_side1")]
        tap_silu = [sem("tap_silu0"), sem("tap_silu1")]
        tap_prod = [sem("tap_prod0"), sem("tap_prod1")]
        borders_zero = sem("borders_zero")
        vec_step, act_step, pe_step = sem("vec_step"), sem("act_step"), sem("pe_step")
        at_scores, at_max, at_exp, at_probs, at_turned, at_copied, at_pv, at_out = (
            sem("at_scores"), sem("at_max"), sem("at_exp"), sem("at_probs"), sem("at_turned"), sem("at_copied"),
            sem("at_pv"), sem("at_out"))
        ml_bc, ml_bcopied, ml_arg, ml_w, ml_probs, ml_scores, ml_turned, ml_copied, ml_pv, ml_out = (
            sem("ml_bc"), sem("ml_bcopied"), sem("ml_arg"), sem("ml_w"), sem("ml_probs"), sem("ml_scores"),
            sem("ml_turned"), sem("ml_copied"), sem("ml_pv"), sem("ml_out"))
        out_stored = sem("out_stored")
        passed = {e: sem("passed_" + e) for e in ("pool", "vector", "tensor")}

        def lay(l, per, n):
            return n if l is None else l * per + n

        U_FFN_A, U_MIX, U_FFN_B = 0, PAIRS_FFN, PAIRS_FFN + PAIRS_MIX
        U_EVEN = DEPTH * PAIRS_LAYER
        U_FFN2 = [U_EVEN + PAIRS_EVEN, U_EVEN + PAIRS_EVEN + PAIRS_FFN + PAIRS_ODD]
        U_ODD = U_FFN2[0] + PAIRS_FFN
        VIRTUAL = PAIRS_ODD - 3

        class Steps:

            def __init__(self, eng, s, base=0, total=None):
                self.eng, self.s, self.base, self.n, self.total = eng, s, base, 0, total

            def did(self, ins):
                self.n += 1
                ins.then_inc(self.s, 1)
                return ins

            def wait(self, back=0):
                self.eng.wait_ge(self.s, self.base + (self.n - back))

            def link(self, ins):
                self.did(ins)
                self.wait()

            def end(self):
                assert self.total is None or self.n == self.total, (self.n, self.total)

        MIX_STEPS = 18
        POOL_STEPS = 9

        def mm(pe, o, w, x, first, last):
            return pe.matmul(o, w, x, start=first, stop=last)

        block = ctx.enter_context(nc.Block())

        @block.sync
        def _(sp):
            def load(src, u_prev, s, words):
                sp.wait_ge(unit_done[s], u_prev + 1)
                sp.dma_start(RING[:, s, 0:words], src).then_inc(w_loaded[s], 16)

            def ffn_load(up, dn, l, row, u, ada=None):
                with sp.Fori(0, PAIRS_UP) as i:
                    for s in range(2):
                        r = (l * FT + i * 2 + (row * FT + s)) if l is not None else (i * 2 + (row * FT + s))
                        load(up[r, :, :], u + i, s, 2 * D)
                        if s == 0 and ada is not None:
                            ada_load(ada + i)
                with sp.Fori(0, PAIRS_DN) as i:
                    for s in range(2):
                        r = (l * CT + i * 2 + (row * CT + s)) if l is not None else (i * 2 + (row * CT + s))
                        load(dn[r, :, :], u + i + PAIRS_UP, s, SLOT)

            def ada_load(n):
                sp.wait_ge(ada_summed, n + 1)
                sp.dma_start(AW, A["ada"][n, :, :].rearrange("p (j k c) -> p j k c", j=2, k=CT)).then_inc(ada_loaded, 16)

            with sp.Fori(0, DEPTH) as l:
                ffn_load(A["up_a"], A["dn_a"], l, 0, l * PAIRS_LAYER + U_FFN_A, l * (2 * ADA_UNITS))
                with sp.Fori(0, PAIRS_MIX) as i:
                    for s in range(2):
                        load(A["mix"][l * (2 * PAIRS_MIX) + i * 2 + s, :, :], l * PAIRS_LAYER + i + U_MIX, s, 2 * D)
                ffn_load(A["up_b"], A["dn_b"], l, 0, l * PAIRS_LAYER + U_FFN_B, l * (2 * ADA_UNITS) + ADA_UNITS)
            with sp.Fori(0, PAIRS_EVEN) as i:
                for s in range(2):
                    load(A["even"][i * 2 + s, :, :], i + U_EVEN, s, 2 * D)
            ffn_load(A["up_c"], A["dn_c"], None, 0, U_FFN2[0])
            for n in range(6):
                u_prev = U_ODD + (0 if n < 2 else 1 if n < 4 else PAIRS_ODD - 1)
                load(A["odd"][n, :, :], u_prev, n % 2, 2 * D)
            ffn_load(A["up_c"], A["dn_c"], None, 1, U_FFN2[1])
            sp.wait_ge(rm_out, 4 * 4)
            sp.dma_start(out, X[:, :, CTX:L2]).then_inc(out_stored, 16)
            sp.wait_ge(out_stored, 16)

        @block.gpsimd
        def _(pool):
            for n, v in enumerate((1.0 / D, 1.0 / 256, 1.0 / P)):
                pool.memset(ONES[:, n, :], v).then_inc(start_set, 1)
            pool.memset(ONE[:, :], 1.0).then_inc(start_set, 1)
            pool.memset(EPS5[:, :], 1e-5).then_inc(start_set, 1)
            pool.memset(EPS6[:, :], 1e-6).then_inc(start_set, 1)
            pool.memset(XP[:, :, 0:16], 0.0).then_inc(start_set, 1)
            for t in PT_:
                pool.memset(t[:, :, 0:16], 0.0).then_inc(start_set, 1)
            pool.memset(CP[:, :, 0:TAPS - 1], 0.0).then_inc(start_set, 1)
            pool.wait_ge(start_set, N_SET)

            def scale_residual(norms):
                pool.wait_ge(ln_out, norms)
                pool.sem_inc(passed["pool"], 1)
                pool.tensor_scalar(PL, XL, ALPHA, None, ALU.mult).then_inc(residual_scaled, 1)

            for dst, name in ((SC[:, :, :], "c"), (ADAB[:, :], "ada_b"), (PL, "x"), (LNIN[:, :, :], "ln_in"),
                              (NG[:, :, :, :], "norm_g"), (DT, "decay"), (RC, "rope_c"), (RS, "rope_s"), (IC, "inv_count")):
                pool.dma_start(dst, A[name]).then_inc(start_loaded, 16)

            def ada_load(n):
                pool.wait_ge(ada_summed, n + 1)
                pool.dma_start(AW, A["ada"][n, :, :].rearrange("p (j k c) -> p j k c", j=2, k=CT))\
                    .then_inc(ada_last_loaded, 16)

            with pool.Fori(0, DEPTH) as l:
                pool.wait_ge(ln_out, l * 24 + 8)
                pool.dma_start(VEC[:, :], A["vec"][l, :, :]).then_inc(vec_loaded, 16)
                pool.dma_start(PW, A["pool_w"][l, :, :, :]).then_inc(vec_loaded, 16)
                scale_residual(l * 24 + 8)
                ada_load(l * (2 * ADA_UNITS) + (ADA_UNITS - 1))
                scale_residual(l * 24 + 16)
                st = Steps(pool, pool_step, l * POOL_STEPS, POOL_STEPS)
                pool.wait_ge(unit_taken[0], l * PAIRS_LAYER + U_MIX + 2)
                src, n = XP, 16 + L1
                for j in range(4):
                    w = 1 << j
                    lo = 2 * w - 1
                    st.link(pool.tensor_tensor(PT_[j][:, :, lo:n], src[:, :, lo:n], src[:, :, lo - w:n - w], ALU.add))
                    src = PT_[j]
                for j in range(4):
                    q = slice(64 * (j % 2), 64 * (j % 2) + 64)
                    st.did(pool.tensor_tensor(WN[q, j // 2, :], PT_[j][q, j // 2, 16:n], IC[q, j // 2, :], ALU.mult))
                st.wait()
                st.did(pool.tensor_tensor(PM, WN, XP[:, :, 16:n], ALU.subtract))
                st.end()
                scale_residual(l * 24 + 24)
                ada_load(l * (2 * ADA_UNITS) + (2 * ADA_UNITS - 1))

            pool.wait_ge(ln_out, 8 * 7)
            pool.dma_start(X[:, :, 0:CTX], A["ctx"]).then_inc(ctx_loaded, 16)
            for dst, name in ((IDN, "ident"), (FCW[0], "fcw0"), (FCW[1], "fcw1"), (EVW, "evw"), (WG, "wg"),
                              (MASK, "mask"), (SEL[0:4, :], "sel"), (WIN, "win"), (GBIAS, "gate_b"), (MLG, "ml_g")):
                pool.dma_start(dst, A[name]).then_inc(tab_loaded, 16)
            for c in CB:
                pool.memset(c[:, :, :, 0:258:257], 0.0).then_inc(borders_zero, 1)
            pool.wait_ge(rm_var, 1)
            pool.dma_start(NU, A["seen"]).then_inc(u_loaded, 16)
            for s in range(2):
                pool.wait_ge(unit_done[s], U_EVEN + 7 + 1)
            pool.wait_ge(pe_step, 1)
            for r in range(ROWS):
                for h in range(NAH):
                    src = bass.AP(A["rpb"].tensor, ((h * 7) + (ROWS - 1 - r)) * RPB_ROW + (GRID_W - 1),
                                  [[RPB_PERIOD - 1, GRID_W], [RPB_ROW, ROWS], [1, GRID_W]])
                    pool.dma_start(BIAS[GRID_W * (r % 2):GRID_W * (r % 2) + GRID_W, h, r // 2, :, :], src)\
                        .then_inc(bias_loaded, 16)
            for s in range(2):
                pool.wait_ge(unit_taken[s], U_EVEN + PAIRS_EVEN + 1)
            for dst, name in ((WUQ, "uq"), (WUKV, "ukv"), (RT, "rope2"), (PERM, "perm"), (QNG, "qkv_g")):
                pool.dma_start(dst, A[name]).then_inc(odd_loaded, 16)

        @block.tensor
        def _(pe):
            pe.wait_ge(start_set, N_SET)
            for s in range(2):
                mm(pe, PS[:, 2 * s, 0:P], ONES[:, 0, :], ONES[:, 1, :], True, True).then_inc(unit_done[s], 1)
            mm(pe, PS[:, 6, 0:P], ONES[:, 0, :], ONES[:, 1, :], True, True).then_inc(ada_done, 1)

            def begin(s, ld, u):
                pe.wait_ge(w_loaded[s], ld * 16 + 16)
                pe.wait_ge(unit_taken[s], u + 1)

            def two_tiles(s, rhs, n):
                for j in range(2):
                    for k in range(CT):
                        last = mm(pe, PS[:, 2 * s + j, 0:n], RING[:, s, (j * CT + k) * P:(j * CT + k + 1) * P],
                                  rhs[:, k, :], k == 0, k == CT - 1)
                return last

            def token_major(s, lhs, tts):
                c0 = 0
                for t, w in enumerate(tts):
                    o = PS[0:w, 2 * s + t // 2, 256 * (t % 2):256 * (t % 2) + 256]
                    for k in range(CT):
                        last = mm(pe, o, lhs[:, k, c0:c0 + w], RING[:, s, k * 256:(k + 1) * 256], k == 0, k == CT - 1)
                    c0 += w
                return last

            def ada_unit(n):
                pe.wait_ge(ada_summed, n + 2)
                pe.wait_ge(ada_taken, n + 1)
                for j in range(2):
                    for g in range(2):
                        last = mm(pe, PS[:, 6, 2 * j + g:2 * j + g + 1], AP_[:, g, j, :], ONE[:, :], True, True)
                last.then_inc(ada_done, 1)

            def ffn(u, ld, rhs, n, hidden_ready, ada=None):
                with pe.Fori(0, PAIRS_UP) as i:
                    for s in range(2):
                        begin(s, ld + i, u + i)
                        two_tiles(s, rhs, n).then_inc(unit_done[s], 1)
                    if ada is not None:
                        ada_unit(ada + i)
                def down(s, i, late=0):
                    begin(s, ld + i + PAIRS_UP, u + i + PAIRS_UP)
                    for k in range(FT):
                        if late and k == FT - late:
                            for z in range(2):
                                hidden_ready(z, 1)
                        last = mm(pe, PS[:, 2 * s, 0:n], RING[:, s, k * P:(k + 1) * P], G[:, k, 0:n], k == 0,
                                  k == FT - 1)
                    last.then_inc(unit_done[s], 1)

                for s in range(2):
                    hidden_ready(s, 0)
                down(0, 0, 2)
                down(1, 0)
                with pe.Fori(1, PAIRS_DN) as i:
                    for s in range(2):
                        down(s, i)
                if ada is not None:
                    ada_unit(ada + (ADA_UNITS - 1))

            def layer_norm(l, e, du):
                if du is None:
                    pe.wait_ge(start_loaded, 16 * N_START)
                else:
                    for s in range(2):
                        pe.wait_ge(unit_taken[s], lay(l, PAIRS_LAYER, du + 1))
                src, nt = (PL, CT) if du is None else (SUMS[:, :, 0:L1], 2)
                for k in range(nt):
                    last = mm(pe, PS[:, 4, 0:L1], ONES[:, 0, :], src[:, k, :], k == 0, k == nt - 1)
                last.then_inc(ln_mean, 1)
                for c in range(4):
                    pe.wait_ge(ln_squared, lay(l, 12, 4 * e + c + 1))
                    for k in (2 * c, 2 * c + 1):
                        last = mm(pe, PS[:, 5, 0:L1], ONES[:, 0, :], SL[:, k, :], k == 0, k == CT - 1)
                last.then_inc(ln_var, 1)

            layer_norm(None, 0, None)

            def mixer(l):
                u, n = l * PAIRS_LAYER, 0
                pe.wait_ge(ln_out, l * 24 + 16)
                for n in range(9):
                    s = n % 2
                    begin(s, u + (U_MIX + n // 2), u + (U_MIX + n // 2))
                    two_tiles(s, XL, L1).then_inc(unit_done[s], 1)
                for n in (9, 10):
                    s = n % 2
                    begin(s, u + (U_MIX + n // 2), u + (U_MIX + n // 2))
                    token_major(s, XL, (P, P, META)).then_inc(unit_done[s], 1)

                def scores(h):
                    if h == 0:
                        pe.wait_ge(mix_step, l * MIX_STEPS + 12)
                    else:
                        pe.wait_ge(ret_decayed, l * 4 + h)
                    q = slice(64 * (h % 2), 64 * (h % 2) + 64)
                    for jt in range(3):
                        w = P if jt < 2 else META
                        for a in range(2):
                            last = mm(pe, PS[0:w, 4 + jt, 0:L1], QK[q, 4 + 2 * (h // 2) + a, jt * P:jt * P + w],
                                      QK[q, 2 * (h // 2) + a, :], a == 0, a == 1)
                    last.then_inc(ret_scores, 1)

                def values(h):
                    pe.wait_ge(ret_decayed, l * 4 + h + 1)
                    if h == 0:
                        for s in range(2):
                            pe.wait_ge(unit_taken[s], u + (U_MIX + (5 if s else 6) + 1))
                    else:
                        pe.wait_ge(ret_copied, l * 4 + h)
                    for jt in range(3):
                        w = P if jt < 2 else META
                        last = mm(pe, PS[:, 7, 0:L1], V1[0:w, jt, h * P:(h + 1) * P], ST[0:w, h % 2, jt, :],
                                  jt == 0, jt == 2)
                    last.then_inc(ret_out, 1)

                scores(0)
                pe.wait_ge(unit_taken[0], u + (U_MIX + 6 + 1))
                pe.wait_ge(conv_tap, l * 62 + 62)
                for t in range(2):
                    last = mm(pe, PS[:, 0, 0:L1], ONES[:, 1, :], ACC[:, t, :], t == 0, t == 1)
                last.then_inc(cv_mean, 1)
                scores(1)
                values(0)
                pe.wait_ge(cv_squared, l + 1)
                for t in range(2):
                    last = mm(pe, PS[:, 1, 0:L1], ONES[:, 1, :], CSQ[:, t, :], t == 0, t == 1)
                last.then_inc(cv_var, 1)
                scores(2)
                values(1)
                scores(3)
                values(2)
                values(3)
                pe.wait_ge(ret_copied, l * 4 + 4)
                for h in range(RH):
                    last = mm(pe, PS[:, 4 + h, 0:L1], ONES[:, 2, :], OT[:, h, :], True, True)
                last.then_inc(gn_stat, 1)
                begin(1, u + (U_MIX + 5), u + (U_MIX + 5))
                pe.wait_ge(pool_step, l * POOL_STEPS + POOL_STEPS)
                pe.wait_ge(vec_loaded, l * 32 + 32)
                for t in range(2):
                    last = mm(pe, PS[:, 2 + t, 0:L1], PW[:, t, :], PM[:, t, :], True, True)
                last.then_inc(gn_stat, 1)
                pe.wait_ge(pooled_taken, l + 1)
                pe.wait_ge(cv_silu, l * 2 + 2)
                for j in range(2):
                    for k in range(2):
                        last = mm(pe, PS[:, 2 + j, 0:L1], RING[:, 1, (j * 2 + k) * P:(j * 2 + k + 1) * P],
                                  CY[:, k, :], k == 0, k == 1)
                last.then_inc(unit_done[1], 1)
                pe.wait_ge(gn_squared, l + 1)
                for h in range(RH):
                    last = mm(pe, PS[:, 4 + h, 0:L1], ONES[:, 2, :], SL[:, h, :], True, True)
                last.then_inc(gn_stat, 1)
                pe.wait_ge(gn_y, l * 4 + 4)
                pe.wait_ge(unit_taken[1], u + (U_MIX + 6 + 1))
                for n in range(12, 16):
                    s = n % 2
                    begin(s, u + (U_MIX + n // 2), u + (U_MIX + n // 2))
                    two_tiles(s, YM, L1).then_inc(unit_done[s], 1)

            with pe.Fori(0, DEPTH) as l:
                def hidden(off):
                    return lambda s, last: pe.wait_ge(unit_taken[s], l * PAIRS_LAYER + (off + PAIRS_UP + last))
                pe.wait_ge(ln_out, l * 24 + 8)
                pe.sem_inc(passed["tensor"], 1)
                ffn(l * PAIRS_LAYER + U_FFN_A, l * PAIRS_LAYER + U_FFN_A, XL, L1, hidden(U_FFN_A),
                    l * (2 * ADA_UNITS))
                layer_norm(l, 1, U_FFN_A + PAIRS_FFN)
                mixer(l)
                layer_norm(l, 2, U_MIX + PAIRS_MIX)
                pe.wait_ge(ln_out, l * 24 + 24)
                pe.sem_inc(passed["tensor"], 1)
                ffn(l * PAIRS_LAYER + U_FFN_B, l * PAIRS_LAYER + U_FFN_B, XL, L1, hidden(U_FFN_B),
                    l * (2 * ADA_UNITS) + ADA_UNITS)
                layer_norm(l, 3, U_FFN_B + PAIRS_FFN)

            def rms(e, c0):
                for c in range(4):
                    pe.wait_ge(rm_squared, 2 * e + c + 1)
                    for k in (2 * c, 2 * c + 1):
                        last = mm(pe, PS[:, 4, 0:L2 - c0], ONES[:, 0, :], SQ[:, k, c0:L2], k == 0, k == CT - 1)
                last.then_inc(rm_var, 1)

            def rms_sums(e, c0, u):
                for s in range(2):
                    pe.wait_ge(unit_taken[s], u + 1)
                for s in range(2):
                    last = mm(pe, PS[:, 4, 0:L2 - c0], ONES[:, 0, :], SUMS[:, s, c0:L2], s == 0, s == 1)
                last.then_inc(rm_var, 1)

            def attend(items, base):
                def scores(n):
                    it = items[n]
                    if base + n >= 4:
                        pe.wait_ge(at_max, base + n - 3)
                        pe.wait_ge(at_exp, base + n - 3)
                    o = PS[:, n % 4, 0:it["keys"]]
                    for j, (a, b) in enumerate(it["qk"]):
                        last = mm(pe, o, a, b, j == 0, j == len(it["qk"]) - 1)
                    last.then_inc(at_scores, 1)

                def turn(n):
                    it = items[n]
                    pe.wait_ge(at_probs, base + n + 1)
                    if base + n >= 2:
                        pe.wait_ge(at_copied, base + n - 1)
                    for j in range(it["keys"] // P):
                        last = pe.transpose(PS[:, 4 + n % 2, j * P:(j + 1) * P], PR[n % 2][:, j * P:(j + 1) * P], IDN)
                    last.then_inc(at_turned, 1)

                def values(n):
                    it = items[n]
                    pe.wait_ge(at_copied, base + n + 1)
                    if base + n >= 2:
                        pe.wait_ge(at_out, base + n - 1)
                    nk = it["keys"] // P
                    for j in range(nk):
                        last = mm(pe, PS[it["rows"], 6 + n % 2, 0:P], it["v"](j), PTT[n % 2][:, j, :], j == 0, j == nk - 1)
                    last.then_inc(at_pv, 1)

                scores(0)
                scores(1)
                for n in range(len(items)):
                    if n + 2 < len(items):
                        scores(n + 2)
                    turn(n)
                    if n >= 1:
                        values(n - 1)
                values(len(items) - 1)

            rms(0, 0)
            pe.wait_ge(rm_in, 8)
            for n in range(14):
                s, u = n % 2, U_EVEN + n // 2
                begin(s, u, u)
                (two_tiles(s, PRE, L2) if n < 10 else token_major(s, PRE, (P,) * 4)).then_inc(unit_done[s], 1)
            pe.wait_ge(tab_loaded, 16 * N_TABLES)
            for t in range(4):
                for k in range(CT):
                    last = mm(pe, PS[:, 5, 16 * t:16 * t + 16], PRE[:, k, t * P:(t + 1) * P], WG[:, k, :],
                              k == 0, k == CT - 1)
            last.then_inc(pe_step, 1)
            pe.wait_ge(vec_step, LS_AT)
            pe.wait_ge(u_loaded, 16)
            for d in range(2):
                for st in range(4):
                    mm(pe, PS[0:4, 6 + d, :], LS[:, st, 8 * d + 4:8 * d + 8], NU[:, d, st, :], st == 0, False)
                for st in range(4):
                    mm(pe, PS[0:4, 6 + d, st * P:(st + 1) * P], GT[:, st, 8 * d:8 * d + 4], IDN, False, st == 3)
            for d in range(2):
                for t in range(4):
                    for st in range(4):
                        last = mm(pe, PS[:, 4, 16 * d + 4 * t:16 * d + 4 * t + 4], NU[:, d, st, t * P:(t + 1) * P],
                                  LS[:, st, 8 * d + 4:8 * d + 8], st == 0, st == 3)
            last.then_inc(pe_step, 1)
            pe.wait_ge(vec_step, NF_AT)
            for s in range(2):
                pe.wait_ge(unit_taken[s], U_EVEN + 7 + 1)
                pe.wait_ge(tap_prod[s], 2)
            for h in range(MLH):
                if h >= 1:
                    pe.wait_ge(ml_bcopied, h)
                for d in range(2):
                    last = mm(pe, PS[:, 4 + d, :], SEL[0:4, h * P:(h + 1) * P], GR[0:4, d, :], True, True)
                last.then_inc(ml_bc, 1)
                for t in range(4):
                    n, nk = 4 * h + t, 2 if t < 2 else 4
                    if n >= 1:
                        pe.wait_ge(ml_probs, n)
                    mm(pe, PS[:, 6, 0:nk * P], G[:, 8 + h, t * P:(t + 1) * P], G[:, 12 + h, 0:nk * P], True, True)\
                        .then_inc(ml_scores, 1)
                    pe.wait_ge(ml_probs, n + 1)
                    for j in range(nk):
                        last = pe.transpose(PS[:, 7, j * P:(j + 1) * P], PR[n % 2][:, j * P:(j + 1) * P], IDN)
                    last.then_inc(ml_turned, 1)
                    pe.wait_ge(ml_copied, n + 1)
                    if t == 0 and h >= 1:
                        pe.wait_ge(ml_out, h)
                    for j in range(nk):
                        last = mm(pe, PS[:, 0, t * P:(t + 1) * P], VM[:, j, h * P:(h + 1) * P], PTT[n % 2][:, j, :],
                                  j == 0, j == nk - 1)
                last.then_inc(ml_pv, 1)
            for part in range(2):
                pe.wait_ge(ml_out, 4 + part)
                for h in range(MLH):
                    last = mm(pe, PS[:, 4 + h, :], ONES[:, 2, :], (G[:, 16 + h, :], SQ[:, h, :])[part], True, True)
                last.then_inc(pe_step, 1)
            pe.wait_ge(ml_out, 6)
            attend(EVEN_ITEMS, 0)
            pe.wait_ge(at_out, len(EVEN_ITEMS))
            pe.wait_ge(vec_step, MLY_AT)
            for n in range(14, 18):
                s, u = n % 2, U_EVEN + n // 2
                begin(s, u, u)
                two_tiles(s, YM2, L2).then_inc(unit_done[s], 1)
            rms_sums(1, 0, U_EVEN + PAIRS_EVEN)
            rms(2, 0)
            pe.wait_ge(rm_in, 16)
            ffn(U_FFN2[0], U_FFN2[0], PRE, L2, lambda s, last: pe.wait_ge(tap_prod[s], 1 + PAIRS_UP + last))
            rms_sums(3, 0, U_FFN2[0] + PAIRS_FFN)
            rms(4, 0)
            pe.wait_ge(rm_in, 24)
            u = U_ODD
            begin(0, u, u)
            two_tiles(0, PRE[:, :, CTX:L2], SEQ).then_inc(unit_done[0], 1)
            begin(1, u, u)
            two_tiles(1, PRE, L2).then_inc(unit_done[1], 1)
            pe.wait_ge(odd_loaded, 16 * N_ODD)
            for s in range(2):
                pe.wait_ge(unit_taken[s], u + 2)
            for t in range(2):
                mm(pe, PS[:, 4, 0:SEQ], ONES[:, 1, :], SQ[:, t, 0:SEQ], t == 0, t == 1)
            mm(pe, PS[:, 5, :], ONES[:, 2, :], SQ[:, 2, :], True, True)
            mm(pe, PS[:, 6, 0:SEQ], PERM, KPE[:, CTX:L2], True, True).then_inc(pe_step, 1)
            pe.wait_ge(vec_step, ODD_Q_AT)
            for n in range(4):
                s, u = n % 2, U_ODD + 1 + n // 2
                pe.wait_ge(unit_taken[s], u + 1)
                for j in range(3):
                    for k in range(2):
                        last = mm(pe, PS[:, 2 * s + j // 2, 256 * (j % 2):256 * (j % 2) + 256],
                                  WUQ[:, 3 * n + j, k, :], DQ[:, k, :], k == 0, k == 1)
                last.then_inc(unit_done[s], 1)
            for n in range(4):
                s, u = n % 2, U_ODD + 3 + n // 2
                pe.wait_ge(unit_taken[s], u + 1)
                for j in range(2):
                    last = mm(pe, PS[:, 2 * s + j, :], WUKV[:, (2 * n + j) * P:(2 * n + j + 1) * P], CKV, True, True)
                last.then_inc(unit_done[s], 1)
            for n in range(4):
                s, u = n % 2, U_ODD + 5 + n // 2
                pe.wait_ge(unit_taken[s], u + 1)
                for j in range(2):
                    last = mm(pe, PS[:, 2 * s + j, :], CKV[:, n * P:(n + 1) * P],
                              WUKV[:, D + j * 512:D + (j + 1) * 512], True, True)
                last.then_inc(unit_done[s], 1)
            for s in range(2):
                pe.wait_ge(unit_taken[s], U_ODD + 7 + 1)
            for t in range(4):
                last = mm(pe, PS[:, 4 + t // 2, 256 * (t % 2):256 * (t % 2) + 256], PERM, QT[:, 8 + t, :], True, True)
            last.then_inc(pe_step, 1)
            pe.wait_ge(vec_step, ODD_ROPE_AT)
            attend(ODD_ITEMS, len(EVEN_ITEMS))
            pe.wait_ge(at_out, len(EVEN_ITEMS) + len(ODD_ITEMS))
            for n in range(4):
                s, u = n % 2, U_ODD + 7 + n // 2
                begin(s, U_ODD + 1 + n // 2, u)
                two_tiles(s, YM2[:, :, CTX:L2], SEQ).then_inc(unit_done[s], 1)
            rms_sums(5, CTX, U_ODD + PAIRS_ODD)
            rms(6, CTX)
            pe.wait_ge(rm_in, 32)
            ffn(U_FFN2[1], U_FFN2[1] - VIRTUAL, PRE[:, :, CTX:L2], SEQ, 
                lambda s, last: pe.wait_ge(tap_prod[s], 1 + 2 * PAIRS_UP + last))
            rms_sums(7, CTX, U_FFN2[1] + PAIRS_FFN)

        @block.scalar
        def _(act):
            act.wait_ge(start_loaded, 16 * N_START)
            act.activation(SC[:, :, :], SC[:, :, :], ACT.Silu).then_inc(silu_c, 1)

            def layer_norm(l, e, gain, bias):
                for c in range(4):
                    act.wait_ge(ln_centred, lay(l, 12, 4 * e + c + 1))
                    act.activation(SL[:, 2 * c:2 * c + 2, :], PL[:, 2 * c:2 * c + 2, :], ACT.Square)\
                        .then_inc(ln_squared, 1)
                act.wait_ge(ln_var, lay(l, 3, e + 1))
                act.activation(RSTD[:, 0:L1], PS[:, 5, 0:L1], ACT.Sqrt, bias=EPS5[:, 0:1]).then_inc(ln_std, 1)
                for k in range(ACT_TILES):
                    if k % 2 == 0:
                        act.wait_ge(ln_scaled, lay(l, 12, 4 * e + k // 2 + 1))
                    act.activation(XL[:, k, :], PL[:, k, :], ACT.Identity, scale=gain(k), bias=bias(k))\
                        .then_inc(ln_out, 1)

            def ffn_gate(l, u, f):
                with act.Fori(0, PAIRS_UP) as i:
                    for s in range(2):
                        act.wait_ge(unit_done[s], u + i + 2)
                        act.activation(SG[:, s, 0:L1], PS[:, 2 * s, 0:L1], ACT.Silu).then_inc(silu_done[s], 1)

            layer_norm(None, 0, lambda k: LNIN[:, 0, k:k + 1], lambda k: LNIN[:, 1, k:k + 1])

            with act.Fori(0, DEPTH) as l:
                def vec_norm(e):
                    layer_norm(l, e, lambda k: VEC[:, V_LNG + 8 * (e - 1) + k:V_LNG + 8 * (e - 1) + k + 1],
                               lambda k: VEC[:, V_LNB + 8 * (e - 1) + k:V_LNB + 8 * (e - 1) + k + 1])
                u = l * PAIRS_LAYER
                act.wait_ge(vec_loaded, l * 32 + 32)
                ffn_gate(l, u + U_FFN_A, None)
                vec_norm(1)
                act.wait_ge(unit_done[0], u + (U_MIX + 1 + 2))
                act.activation(CSG, PS[:, 0:2, 0:L1], ACT.Sigmoid).then_inc(conv_gate, 1)
                for n in (7, 8):
                    s = n % 2
                    act.wait_ge(unit_done[s], u + (U_MIX + n // 2 + 2))
                    act.activation(GS[:, 2 * (n - 7):2 * (n - 7) + 2, :], PS[:, 2 * s:2 * s + 2, 0:L1], ACT.Silu)\
                        .then_inc(unit_taken[s], 1)
                for n in (9, 10):
                    s = n % 2
                    act.wait_ge(unit_done[s], u + (U_MIX + n // 2 + 2))
                    c = 256 * (n - 9)
                    act.copy(V1[:, 0:2, c:c + 256], PS[:, 2 * s, :].rearrange("p (a b) -> p a b", a=2))
                    act.copy(V1[0:META, 2, c:c + 256], PS[0:META, 2 * s + 1, 0:256]).then_inc(unit_taken[s], 1)

                def copy_head(h):
                    act.wait_ge(ret_out, l * 4 + h + 1)
                    act.copy(OT[:, h, :], PS[:, 7, 0:L1]).then_inc(ret_copied, 1)

                act.wait_ge(mix_step, l * MIX_STEPS + 13)
                act.activation(CSQ, ACC, ACT.Square).then_inc(cv_squared, 1)
                copy_head(0)
                act.wait_ge(cv_var, l + 1)
                act.activation(CSTD, PS[:, 1, 0:L1], ACT.Sqrt, bias=EPS5[:, 0:1]).then_inc(cv_std, 1)
                for h in range(1, RH):
                    copy_head(h)
                act.wait_ge(mix_step, l * MIX_STEPS + 15)
                for t in range(2):
                    act.activation(CY[:, t, :], ACC[:, t, :], ACT.Silu, scale=VEC[:, V_CG + t:V_CG + t + 1],
                                   bias=VEC[:, V_CB + t:V_CB + t + 1]).then_inc(cv_silu, 1)
                act.wait_ge(mix_step, l * MIX_STEPS + 16)
                act.activation(SL[:, 0:4, :], OT, ACT.Square).then_inc(gn_squared, 1)
                act.wait_ge(gn_stat, l * 3 + 3)
                act.activation(STD4, PS[:, 4:8, 0:L1], ACT.Sqrt, bias=EPS5[:, 0:1]).then_inc(gn_std, 1)
                vec_norm(2)
                ffn_gate(l, u + U_FFN_B, None)
                vec_norm(3)

            st = Steps(act, act_step)

            def rms_std(e, c0):
                act.wait_ge(rm_var, e + 1)
                act.activation(RSTD[:, c0:L2], PS[:, 4, 0:L2 - c0], ACT.Sqrt, bias=EPS6[:, 0:1]).then_inc(rm_std, 1)

            def rms_in(e, l, which, c0, wait_tile):
                for c in range(4):
                    wait_tile(c)
                    act.activation(SQ[:, 2 * c:2 * c + 2, c0:L2], X[:, 2 * c:2 * c + 2, c0:L2], ACT.Square)\
                        .then_inc(rm_squared, 1)
                rms_std(e, c0)
                for k in range(ACT_TILES):
                    if k % 2 == 0:
                        act.wait_ge(rm_scaled, 4 * e + k // 2 + 1)
                    for g in range(c0 // CTX, 2):
                        cols = slice(g * CTX, (g + 1) * CTX)
                        last = act.activation(PRE[:, k, cols], PRE[:, k, cols], ACT.Identity,
                                              scale=GIN[:, l, which, k, g:g + 1],
                                              bias=MOD[:, l, 24 * which + k, g:g + 1])
                    last.then_inc(rm_in, 1)

            def projected(u, c0):
                for n in range(4):
                    s = n % 2
                    act.wait_ge(unit_done[s], u + n // 2 + 2)
                    act.activation(SQ[:, 2 * n:2 * n + 2, c0:L2], PS[:, 2 * s:2 * s + 2, 0:L2 - c0], ACT.Square)\
                        .then_inc(sum_squared, 1)

            def conv_taps(s, done, free, n, vec, ngrp):
                if free is not None:
                    act.wait_ge(tap_prod[s], free)
                act.wait_ge(unit_done[s], done)
                cb, ac = CB[s], AC[s]
                src = PS[:, 2 * s:2 * s + 2, 0:n]
                if ngrp == 2:
                    for a in range(2):
                        act.copy(cb[:, a, :, 1:257], PS[:, 2 * s + a, :].rearrange("p (g t) -> p g t", g=2))
                else:
                    act.copy(cb[:, :, 1, 1:257], src)
                for a in range(2):
                    o = ac[:, a, :, :] if ngrp == 2 else ac[:, a, 1, :]
                    i = PS[:, 2 * s + a, :].rearrange("p (g t) -> p g t", g=2) if ngrp == 2 else PS[:, 2 * s + a, 0:n]
                    last = act.activation(o, i, ACT.Identity, scale=vec(a, 1), bias=vec(a, 3))
                last.then_inc(unit_taken[s], 1)

            def ffn2(f, u, n, ngrp):
                with act.Fori(0, PAIRS_UP) as i:
                    for s in range(2):
                        conv_taps(s, i + (u + 2), i + (2 + PAIRS_UP * f), n,
                                  lambda a, c: FCW[f].rearrange("p f a c -> p f (a c)")[:, bass.ds(i * 2 + s, 1), 4 * a + c],
                                  ngrp)
                        act.wait_ge(tap_side[s], i + (2 + PAIRS_UP * f + 1))
                        act.activation(SG[:, s, 0:n], AC[s][:, 1, 2 - ngrp:2, :].rearrange("p g t -> p (g t)"),
                                       ACT.Silu).then_inc(tap_silu[s], 1)
                with act.Fori(0, PAIRS_DN) as i:
                    for s in range(2):
                        act.wait_ge(unit_done[s], i + (u + PAIRS_UP + 2))
                        act.activation(SQ[:, bass.ds(i * 2 + s, 1), L2 - n:L2],
                                       PS[:, 2 * s, 0:n].rearrange("p (o n) -> p o n", o=1), ACT.Square)\
                            .then_inc(sum_squared, 1)

            def softmax(items, base):
                for n, it in enumerate(items):
                    b = base + n
                    w = it["keys"]
                    act.wait_ge(at_max, b + 1)
                    if n >= 2:
                        act.wait_ge(at_turned, b - 1)
                    act.activation(PR[n % 2][:, 0:w], SS[n % 2][:, 0:w] if it["sb"] else PS[:, n % 4, 0:w],
                                   ACT.Exp, bias=STAT[:, 4 + n % 2:5 + n % 2],
                                   scale=1.0 if it["sb"] else it["scale"],
                                   accum_out=STAT[:, 8 + n % 2:9 + n % 2]).then_inc(at_exp, 1)
                    if n >= 1:
                        copy_turned(items, base, n - 1)
                copy_turned(items, base, len(items) - 1)

            def copy_turned(items, base, n):
                act.wait_ge(at_turned, base + n + 1)
                if base + n >= 2:
                    act.wait_ge(at_pv, base + n - 1)
                nk = items[n]["keys"] // P
                act.copy(PTT[n % 2][:, 0:nk, :], PS[:, 4 + n % 2, 0:nk * P].rearrange("p (a b) -> p a b", a=nk))\
                    .then_inc(at_copied, 1)

            def first_tiles(c):
                if c == 0:
                    act.wait_ge(ctx_loaded, 16)
                    act.wait_ge(ln_out, 56)

            def after_post(e):
                return lambda c: act.wait_ge(rm_out, 4 * e + c + 1)

            act.wait_ge(gains_step, GAIN_STEPS)
            rms_in(0, 0, 0, 0, first_tiles)
            act.wait_ge(tab_loaded, 16 * N_TABLES)
            act.wait_ge(borders_zero, 2)
            for n in range(4, 8):
                s, j = n % 2, n - 4
                conv_taps(s, U_EVEN + n // 2 + 2, j // 2 or None, L2, lambda a, c: EVW[:, 2 * j + a, c:c + 1], 2)
                act.wait_ge(tap_side[s], j // 2 + 1)
                for a in range(2):
                    last = act.activation(G[:, 8 + 2 * j + a, :], AC[s][:, a, :, :].rearrange("p g t -> p (g t)"),
                                          ACT.Silu)
                last.then_inc(tap_prod[s], 1)
            for n in (8, 9):
                s = n % 2
                act.wait_ge(unit_done[s], U_EVEN + n // 2 + 2)
                act.activation(G[:, 16 + 2 * (n - 8):18 + 2 * (n - 8), :], PS[:, 2 * s:2 * s + 2, :], ACT.Sigmoid)\
                    .then_inc(unit_taken[s], 1)
            for n in range(10, 14):
                s, c = n % 2, 256 * (n % 2)
                act.wait_ge(unit_done[s], U_EVEN + n // 2 + 2)
                act.copy((VN if n < 12 else VM)[:, :, c:c + 256],
                         PS[:, 2 * s:2 * s + 2, :].rearrange("p a (b c) -> p (a b) c", b=2)).then_inc(unit_taken[s], 1)
            act.wait_ge(vec_step, ABS_AT)
            st.link(act.activation(GE, GE, ACT.Exp, scale=-1.0))
            st.did(act.activation(GE, GE, ACT.Ln, bias=1.0))
            for h in range(MLH):
                act.wait_ge(ml_bc, h + 1)
                if h >= 1:
                    act.wait_ge(ml_probs, 4 * h)
                for d in range(2):
                    last = act.copy(GB[:, d, :], PS[:, 4 + d, :])
                last.then_inc(ml_bcopied, 1)
                for t in range(4):
                    n, nk = 4 * h + t, 2 if t < 2 else 4
                    act.wait_ge(ml_arg, n + 1)
                    for d in range(2):
                        act.activation(TM[:, d, 0:nk * P], TM[:, d, 0:nk * P], ACT.Exp, bias=STAT[:, 18 + d:19 + d])
                    act.activation(STAT[:, 20:22], STAT[:, 20:22], ACT.Exp).then_inc(ml_w, 1)
                    act.wait_ge(ml_turned, n + 1)
                    act.copy(PTT[n % 2][:, 0:nk, :], PS[:, 7, 0:nk * P].rearrange("p (a b) -> p a b", a=nk))\
                        .then_inc(ml_copied, 1)
            act.wait_ge(vec_step, MLC_AT)
            act.activation(SQ[:, 0:4, :], G[:, 16:20, :], ACT.Square).then_inc(ml_out, 1)
            act.wait_ge(pe_step, 4)
            act.activation(SQ[:, 4:8, :], PS[:, 4:8, :], ACT.Sqrt, bias=EPS6[:, 0:1]).then_inc(ml_out, 1)
            softmax(EVEN_ITEMS, 0)
            projected(U_EVEN + 7, 0)
            rms_std(1, 0)
            rms_in(2, 0, 1, 0, after_post(0))
            ffn2(0, U_FFN2[0], L2, 2)
            rms_std(3, 0)
            rms_in(4, 1, 0, 0, after_post(1))
            act.wait_ge(unit_done[0], U_ODD + 2)
            act.copy(DQ, PS[:, 0:2, 0:SEQ])
            act.activation(SQ[:, 0:2, 0:SEQ], PS[:, 0:2, 0:SEQ], ACT.Square).then_inc(unit_taken[0], 1)
            act.wait_ge(unit_done[1], U_ODD + 2)
            act.wait_ge(odd_loaded, 16 * N_ODD)
            act.copy(CKV, PS[:, 2, :])
            act.copy(KPE, PS[:, 3, :])
            act.activation(SQ[:, 2, :], PS[:, 2, :], ACT.Square).then_inc(unit_taken[1], 1)
            act.wait_ge(pe_step, 5)
            act.activation(SQ[:, 3, 0:SEQ], PS[:, 4, 0:SEQ], ACT.Sqrt, bias=EPS6[:, 0:1])
            st.did(act.activation(SQ[:, 4, :], PS[:, 5, :], ACT.Sqrt, bias=EPS6[:, 0:1]))
            for n in range(4):
                s = n % 2
                act.wait_ge(unit_done[s], U_ODD + 1 + n // 2 + 2)
                act.copy(QT[:, 3 * n:3 * n + 2, :], PS[:, 2 * s, :].rearrange("p (a b) -> p a b", a=2))
                act.copy(QT[:, 3 * n + 2, :], PS[:, 2 * s + 1, 0:SEQ]).then_inc(unit_taken[s], 1)
            for n in range(4):
                s = n % 2
                act.wait_ge(unit_done[s], U_ODD + 3 + n // 2 + 2)
                act.copy(KN[:, 2 * n:2 * n + 2, :], PS[:, 2 * s:2 * s + 2, :]).then_inc(unit_taken[s], 1)
            for n in range(4):
                s = n % 2
                act.wait_ge(unit_done[s], U_ODD + 5 + n // 2 + 2)
                act.copy(VV[:, n, :].rearrange("p (a b) -> p a b", a=2), PS[:, 2 * s:2 * s + 2, :])\
                    .then_inc(unit_taken[s], 1)
            softmax(ODD_ITEMS, len(EVEN_ITEMS))
            projected(U_ODD + 7, CTX)
            rms_std(5, CTX)
            rms_in(6, 1, 1, CTX, after_post(2))
            ffn2(1, U_FFN2[1], SEQ, 1)
            rms_std(7, CTX)

        @block.vector
        def _(v):
            for s in range(2):
                v.memset(SG[:, s, :], 0.0).then_inc(unit_taken[s], 1)
            v.wait_ge(start_loaded, 16 * N_START)
            v.memset(MODF[:, :, :], 0.0).then_inc(ada_taken, 1)
            v.memset(AP_, 0.0).then_inc(ada_summed, 1)

            def ada_sum(n, loaded, loads):
                v.wait_ge(loaded, loads)
                v.wait_ge(ada_done, n + 1)
                for k in range(CT):
                    for g in range(2):
                        c = SC[:, k, g:g + 1]
                        if k == 0:
                            ins = v.tensor_scalar(AP_[:, g, :, :], AW[:, :, k, :], c, None, ALU.mult)
                        else:
                            v.wait_ge(ada_step, n * (2 * CT) + (2 * k - 1 + g))
                            ins = v.scalar_tensor_tensor(AP_[:, g, :, :], AW[:, :, k, :], c, AP_[:, g, :, :],
                                                         ALU.mult, ALU.add)
                        if k == CT - 1 and g == 1:
                            ins.then_inc(ada_summed, 1)
                        else:
                            ins.then_inc(ada_step, 1)
                v.sem_inc(ada_step, 1)

            def ada_take(n):
                v.wait_ge(ada_done, n + 2)
                v.tensor_tensor(MODF[:, bass.ds(n * 2, 2), :], PS[:, 6, 0:4].rearrange("p (a b) -> p a b", a=2),
                                ADAB[:, bass.ds(n * 2, 2)].rearrange("p (a o) -> p a o", o=1).to_broadcast([P, 2, 2]),
                                ALU.add).then_inc(ada_taken, 1)

            def bc(t, n):
                return t.rearrange("p (o n) -> p o n", o=1).to_broadcast([P, n, t.shape[-1]])

            def layer_norm(l, e, gain, bias):
                v.wait_ge(ln_mean, lay(l, 3, e + 1))
                for c in range(4):
                    q = PL[:, 2 * c:2 * c + 2, :]
                    v.tensor_tensor(q, q, bc(PS[:, 4, 0:L1], 2), ALU.subtract).then_inc(ln_centred, 1)
                v.wait_ge(ln_std, lay(l, 3, e + 1))
                v.reciprocal(RSTD[:, 0:L1], RSTD[:, 0:L1]).then_inc(ln_rstd, 1)
                v.wait_ge(ln_rstd, lay(l, 3, e + 1))
                for c in range(4):
                    q = PL[:, 2 * c:2 * c + 2, :]
                    v.tensor_tensor(q, q, bc(RSTD[:, 0:L1], 2), ALU.mult).then_inc(ln_scaled, 1)
                v.wait_ge(ln_scaled, lay(l, 12, 4 * e + 4))
                for k in range(ACT_TILES, CT):
                    v.tensor_scalar(XL[:, k, :], PL[:, k, :], gain(k), bias(k), ALU.mult, ALU.add).then_inc(ln_out, 1)

            def ffn_half(l, u, f, ada):
                with v.Fori(0, PAIRS_UP) as i:
                    for s in range(2):
                        v.wait_ge(silu_done[s], l * (2 * PAIRS_UP) + i + (f * PAIRS_UP + 1))
                        v.tensor_tensor(G[:, bass.ds(i * 2 + s, 1), 0:L1],
                                        SG[:, s, 0:L1].rearrange("p (o n) -> p o n", o=1),
                                        PS[:, 2 * s + 1, 0:L1].rearrange("p (o n) -> p o n", o=1), ALU.mult)\
                            .then_inc(unit_taken[s], 1)
                        if s == 0:
                            ada_sum(ada + i, ada_loaded, l * (32 * PAIRS_UP) + i * 16 + (f * PAIRS_UP * 16 + 16))
                        else:
                            ada_take(ada + i)
                ada_sum(ada + (ADA_UNITS - 1), ada_last_loaded, l * 32 + (16 * f + 16))
                v.wait_ge(residual_scaled, l * 3 + (1 if f == 0 else 3))
                v.memset(SUMS[:, :, 0:L1], 0.0).then_inc(sum_added, 1)
                with v.Fori(0, PAIRS_DN) as i:
                    for s in range(2):
                        v.wait_ge(unit_done[s], u + i + (PAIRS_UP + 2))
                        q = PL[:, bass.ds(i * 2 + s, 1), :]
                        v.scalar_tensor_tensor(q, PS[:, 2 * s, 0:L1].rearrange("p (o n) -> p o n", o=1), 0.5, q,
                                               ALU.mult, ALU.add).then_inc(sum_added, 1)
                        v.wait_ge(sum_added, l * 23 + i * 2 + (14 * f + 2 + s))
                        t = SUMS[:, s:s + 1, 0:L1]
                        v.tensor_tensor(t, t, q, ALU.add).then_inc(unit_taken[s], 1)
                ada_take(ada + (ADA_UNITS - 1))

            layer_norm(None, 0, lambda k: LNIN[:, 0, k:k + 1], lambda k: LNIN[:, 1, k:k + 1])
            v.wait_ge(silu_c, 1)
            v.sem_inc(passed["vector"], 1)

            with v.Fori(0, DEPTH) as l:
                u = l * PAIRS_LAYER

                def vec_norm(e):
                    layer_norm(l, e, lambda k: VEC[:, V_LNG + 8 * (e - 1) + k:V_LNG + 8 * (e - 1) + k + 1],
                               lambda k: VEC[:, V_LNB + 8 * (e - 1) + k:V_LNB + 8 * (e - 1) + k + 1])
                ffn_half(l, u + U_FFN_A, 0, l * (2 * ADA_UNITS))
                v.wait_ge(vec_loaded, l * 32 + 32)
                vec_norm(1)
                st = Steps(v, mix_step, l * MIX_STEPS, MIX_STEPS)

                def taken(n):
                    s = n % 2
                    v.wait_ge(unit_done[s], u + (U_MIX + n // 2 + 2))
                    return s, PS[:, 2 * s:2 * s + 2, 0:L1]

                s, b = taken(0)
                v.tensor_copy(XP[:, :, 16:16 + L1], b).then_inc(unit_taken[s], 1)
                s, b = taken(1)
                v.tensor_copy(CA, b).then_inc(unit_taken[s], 1)
                v.wait_ge(conv_gate, l + 1)
                v.wait_ge(unit_taken[1], u + (U_MIX + 2))
                v.tensor_tensor(CP[:, :, TAPS - 1:TAPS - 1 + L1], CA, CSG, ALU.mult).then_inc(unit_taken[0], 1)
                v.wait_ge(unit_taken[0], u + (U_MIX + 3))
                v.wait_ge(vec_loaded, l * 32 + 32)

                def taps(a, b):
                    for t in range(a, b):
                        for j in range(2):
                            w = VEC[:, V_DW + 2 * t + j:V_DW + 2 * t + j + 1]
                            if t == 0:
                                ins = v.tensor_scalar(ACC[:, j, :], CP[:, j, 0:L1], w,
                                                      VEC[:, V_DB + j:V_DB + j + 1], ALU.mult, ALU.add)
                            else:
                                v.wait_ge(conv_tap, l * 62 + (2 * t + j - 1))
                                ins = v.scalar_tensor_tensor(ACC[:, j, :], CP[:, j, t:t + L1], w, ACC[:, j, :],
                                                             ALU.mult, ALU.add)
                            ins.then_inc(conv_tap, 1)

                def rotate(n):
                    s, b = taken(n)
                    if st.n:
                        st.wait()
                    st.did(v.tensor_tensor(T1, b, bc(RC, 2), ALU.mult))
                    st.did(v.tensor_tensor(T2[:, 0, :], PS[:, 2 * s + 1, 0:L1], RS[:, 0, :], ALU.mult))
                    v.tensor_tensor(T2[:, 1, :], PS[:, 2 * s, 0:L1], RS[:, 1, :], ALU.mult)\
                        .then_inc(unit_taken[s], 1)
                    v.wait_ge(unit_taken[s], u + (U_MIX + n // 2 + 2))
                    st.wait()
                    st.did(v.tensor_tensor(QK[:, 2 * (n - 3):2 * (n - 3) + 2, :], T1, T2, ALU.add))

                for j, n in enumerate((3, 4, 5, 6)):
                    taps(8 * j, min(8 * j + 8, TAPS))
                    rotate(n)

                def decay(h):
                    v.wait_ge(ret_scores, l * 4 + h + 1)
                    if h >= 2:
                        v.wait_ge(ret_out, l * 4 + h - 1)
                    v.tensor_tensor(ST[:, h % 2, 0:2, :], PS[:, 4:6, 0:L1], DT[:, h, 0:2, :], ALU.mult)
                    v.tensor_tensor(ST[0:META, h % 2, 2, :], PS[0:META, 6, 0:L1], DT[0:META, h, 2, :], ALU.mult)\
                        .then_inc(ret_decayed, 1)

                decay(0)
                v.wait_ge(cv_mean, l + 1)
                st.did(v.tensor_tensor(ACC, ACC, bc(PS[:, 0, 0:L1], 2), ALU.subtract))
                decay(1)
                decay(2)
                v.wait_ge(cv_std, l + 1)
                st.link(v.reciprocal(CSTD, CSTD))
                st.did(v.tensor_tensor(ACC, ACC, bc(CSTD, 2), ALU.mult))
                decay(3)
                v.wait_ge(gn_stat, l * 3 + 1)
                st.did(v.tensor_tensor(OT, OT, PS[:, 4:8, 0:L1], ALU.subtract))
                v.wait_ge(gn_stat, l * 3 + 2)
                for t in range(2):
                    last = v.tensor_scalar(YM[:, t, :], PS[:, 2 + t, 0:L1], VEC[:, V_PS + t:V_PS + t + 1], None,
                                           ALU.mult)
                last.then_inc(pooled_taken, 1)
                s, b = taken(11)
                v.tensor_copy(YM[:, 2:4, :], b).then_inc(unit_taken[s], 1)
                v.wait_ge(gn_std, l + 1)
                st.link(v.reciprocal(STD4, STD4))
                st.link(v.tensor_tensor(OT, OT, STD4, ALU.mult))
                for h in range(RH):
                    v.scalar_tensor_tensor(YM[:, 4 + h, :], OT[:, h, :], VEC[:, V_GN + h:V_GN + h + 1], GS[:, h, :],
                                           ALU.mult, ALU.mult).then_inc(gn_y, 1)
                v.wait_ge(residual_scaled, l * 3 + 2)
                sums = SUMS[:, :, 0:L1]
                v.memset(sums, 0.0).then_inc(sum_added, 1)
                for n in range(12, 16):
                    s, b = taken(n)
                    q = PL[:, 2 * (n - 12):2 * (n - 12) + 2, :]
                    v.tensor_tensor(q, b, q, ALU.add).then_inc(sum_added, 1)
                    v.wait_ge(sum_added, l * 23 + (n - 12 + 11))
                    v.tensor_tensor(sums, sums, q, ALU.add).then_inc(unit_taken[s], 1)
                st.end()
                vec_norm(2)
                ffn_half(l, u + U_FFN_B, 1, l * (2 * ADA_UNITS) + ADA_UNITS)
                vec_norm(3)

            v.wait_ge(ada_taken, 4 * ADA_UNITS + 1)
            gst = Steps(v, gains_step)
            for l in range(DEPTH):
                for w in range(2):
                    m = MOD[:, l, 24 * w:24 * w + 24, :]
                    gst.did(v.tensor_scalar(GIN[:, l, w, :, :], m[:, 8:16, :], 1.0, None, ALU.add))
                    for g in range(2):
                        gst.did(v.tensor_tensor(GOUT[:, l, w, :, g], m[:, 16:24, g], NG[:, l, 2 * w + 1, :], ALU.mult))
            gst.wait()
            for l in range(DEPTH):
                for w in range(2):
                    for g in range(2):
                        gst.did(v.tensor_tensor(GIN[:, l, w, :, g], GIN[:, l, w, :, g], NG[:, l, 2 * w, :], ALU.mult))
            assert gst.n == GAIN_STEPS

            st = Steps(v, vec_step)

            def rms_rstd(e, c0):
                v.wait_ge(rm_std, e + 1)
                v.reciprocal(RSTD[:, c0:L2], RSTD[:, c0:L2]).then_inc(rm_rstd, 1)
                v.wait_ge(rm_rstd, e + 1)

            def rms_in(e, l, which, c0):
                rms_rstd(e, c0)
                for c in range(4):
                    v.tensor_tensor(PRE[:, 2 * c:2 * c + 2, c0:L2], X[:, 2 * c:2 * c + 2, c0:L2],
                                    bc(RSTD[:, c0:L2], 2), ALU.mult).then_inc(rm_scaled, 1)
                v.wait_ge(rm_scaled, 4 * e + 4)
                for k in range(ACT_TILES, CT):
                    for g in range(c0 // CTX, 2):
                        cols = slice(g * CTX, (g + 1) * CTX)
                        last = v.tensor_scalar(PRE[:, k, cols], PRE[:, k, cols], GIN[:, l, which, k, g:g + 1],
                                               MOD[:, l, 24 * which + k, g:g + 1], ALU.mult, ALU.add)
                    last.then_inc(rm_in, 1)

            def rms_post(e, c0):
                rms_rstd(e, c0)
                for c in range(5):
                    if c < 4:
                        q = PRE[:, 2 * c:2 * c + 2, c0:L2]
                        v.tensor_tensor(q, q, bc(RSTD[:, c0:L2], 2), ALU.mult).then_inc(rm_scaled, 1)
                    if c >= 1:
                        k = 2 * c - 2
                        v.wait_ge(rm_scaled, 4 * e + c)
                        v.tensor_tensor(X[:, k:k + 2, c0:L2], X[:, k:k + 2, c0:L2], PRE[:, k:k + 2, c0:L2], ALU.add)\
                            .then_inc(rm_out, 1)

            def projected(u, l, c0, squared):
                sums = SUMS[:, :, c0:L2]
                st.link(v.memset(sums, 0.0))
                for n in range(4):
                    s = n % 2
                    v.wait_ge(sum_squared, squared + n + 1)
                    for a in range(2):
                        for g in range(c0 // CTX, 2):
                            v.tensor_scalar(PRE[:, 2 * n + a, g * CTX:(g + 1) * CTX],
                                            PS[:, 2 * s + a, g * CTX - c0:(g + 1) * CTX - c0],
                                            GOUT[:, l, 0, 2 * n + a, g:g + 1], None, ALU.mult)
                    if n >= 1:
                        v.wait_ge(unit_taken[1 - s], u + (n - 1) // 2 + 2)
                    v.tensor_tensor(sums, sums, SQ[:, 2 * n:2 * n + 2, c0:L2], ALU.add).then_inc(unit_taken[s], 1)

            def side_taps(s, mid, vec, ngrp):
                v.wait_ge(unit_taken[s], mid)
                for a in range(2):
                    for c in (0, 2):
                        ac, cb = AC[s][:, a, :, :], CB[s][:, a, :, :]
                        if ngrp == 1:
                            ac, cb = ac[:, 1:2, :], cb[:, 1:2, :]
                        if c == 2:
                            st_side[s].wait()
                        ins = v.scalar_tensor_tensor(ac, cb[:, :, c:c + 256], vec(a, c), ac, ALU.mult, ALU.add)
                        if c == 0:
                            st_side[s].did(ins)
                        elif a == 0:
                            st_side[s].did(ins)
                ins.then_inc(tap_side[s], 1)

            class LoopSteps:
                def __init__(self, s):
                    self.s, self.base, self.n = s, 0, 0

                def did(self, ins):
                    self.n += 1
                    ins.then_inc(self.s, 1)

                def wait(self):
                    v.wait_ge(self.s, self.base + self.n)

            st_side = [LoopSteps(side_step[0]), LoopSteps(side_step[1])]

            def ffn2(f, u, n, ngrp, squared):
                for s in range(2):
                    base0 = 3 * (2 + PAIRS_UP * f)
                    st_side[s].base, st_side[s].n = base0, 0
                with v.Fori(0, PAIRS_UP) as i:
                    for s in range(2):
                        st_side[s].base = i * 3 + base0
                        st_side[s].n = 0
                        side_taps(s, i + (u + 2),
                                  lambda a, c: FCW[f].rearrange("p f a c -> p f (a c)")[:, bass.ds(i * 2 + s, 1), 4 * a + c],
                                  ngrp)
                        v.wait_ge(tap_silu[s], i + (PAIRS_UP * f + 1))
                        v.tensor_tensor(G[:, bass.ds(i * 2 + s, 1), 0:n],
                                        AC[s][:, 0:1, 2 - ngrp:2, :].rearrange("p o g t -> p o (g t)"),
                                        SG[:, s, 0:n].rearrange("p (o n) -> p o n", o=1), ALU.mult)\
                            .then_inc(tap_prod[s], 1)
                c0 = L2 - n
                for s in range(2):
                    v.wait_ge(tap_prod[s], 2 + PAIRS_UP * (f + 1))
                st.did(v.memset(SUMS[:, :, c0:L2], 0.0))
                st.wait()
                with v.Fori(0, PAIRS_DN) as i:
                    for s in range(2):
                        v.wait_ge(sum_squared, i * 2 + (squared + s + 1))
                        for g in range(c0 // CTX, 2):
                            v.tensor_scalar(PRE[:, bass.ds(i * 2 + s, 1), g * CTX:(g + 1) * CTX],
                                            PS[:, 2 * s, g * CTX - c0:(g + 1) * CTX - c0]
                                            .rearrange("p (o n) -> p o n", o=1),
                                            GOUT[:, f, 1, bass.ds(i * 2 + s, 1), g], None, ALU.mult)
                        t = SUMS[:, s:s + 1, c0:L2]
                        v.tensor_tensor(t, t, SQ[:, bass.ds(i * 2 + s, 1), c0:L2], ALU.add).then_inc(unit_taken[s], 1)

            def attend(items, base):
                def top(n):
                    it, b = items[n], base + n
                    w = it["keys"]
                    v.wait_ge(at_scores, b + 1)
                    src = PS[:, n % 4, 0:w]
                    if it["sb"]:
                        if n >= 2:
                            v.wait_ge(at_exp, b - 1)
                        st.did(v.tensor_scalar(SS[n % 2][:, 0:CTX], src[:, 0:CTX], it["scale"], None, ALU.mult))
                        st.did(v.scalar_tensor_tensor(SS[n % 2][:, CTX:L2], src[:, CTX:L2], it["scale"], it["bias"],
                                                      ALU.mult, ALU.add))
                        st.wait()
                        src = SS[n % 2][:, 0:w]
                    st.link(v.tensor_reduce(STAT[:, n % 2:n % 2 + 1], src, AX.X, ALU.max))
                    v.tensor_scalar(STAT[:, 4 + n % 2:5 + n % 2], STAT[:, n % 2:n % 2 + 1],
                                    -1.0 if it["sb"] else -it["scale"], None, ALU.mult).then_inc(at_max, 1)

                def norm(n):
                    it, b = items[n], base + n
                    v.wait_ge(at_exp, b + 1)
                    st.link(v.reciprocal(STAT[:, 12 + n % 2:13 + n % 2], STAT[:, 8 + n % 2:9 + n % 2]))
                    q = PR[n % 2][:, 0:it["keys"]]
                    v.tensor_scalar(q, q, STAT[:, 12 + n % 2:13 + n % 2], None, ALU.mult).then_inc(at_probs, 1)

                def place(n):
                    it, b = items[n], base + n
                    v.wait_ge(at_pv, b + 1)
                    v.tensor_copy(it["out"], PS[it["rows"], 6 + n % 2, 0:P]).then_inc(at_out, 1)

                top(0)
                top(1)
                for n in range(len(items)):
                    norm(n)
                    if n + 2 < len(items):
                        top(n + 2)
                    if n >= 2:
                        place(n - 2)
                for n in range(len(items) - 2, len(items)):
                    place(n)

            v.wait_ge(gains_step, GAIN_STEPS)
            rms_in(0, 0, 0, 0)
            for n in range(4):
                s = n % 2
                v.wait_ge(unit_done[s], U_EVEN + n // 2 + 2)
                v.tensor_copy(G[:, 2 * n:2 * n + 2, :], PS[:, 2 * s:2 * s + 2, :]).then_inc(unit_taken[s], 1)
            for n in range(4, 8):
                s, j = n % 2, n - 4
                st_side[s].base, st_side[s].n = 3 * (j // 2), 0
                side_taps(s, U_EVEN + n // 2 + 2, lambda a, c: EVW[:, 2 * j + a, c:c + 1], 2)
            v.wait_ge(pe_step, 1)
            v.wait_ge(tab_loaded, 16 * N_TABLES)
            st.link(v.tensor_tensor(GT, PS[:, 5, 0:64].rearrange("p (a b) -> p a b", a=4), bc(GBIAS, 4), ALU.add))
            st.link(v.tensor_scalar(GE, GT, -1.0, None, ALU.mult))
            st.did(v.tensor_tensor(GE, GE, GT, ALU.max))
            assert st.n == ABS_AT
            st.link(v.tensor_scalar(LS, GT, 0.0, None, ALU.min))
            v.wait_ge(act_step, 2)
            st.did(v.tensor_tensor(LS, LS, GE, ALU.subtract))
            assert st.n == LS_AT
            v.wait_ge(pe_step, 2)
            st.did(v.tensor_copy(GR[0:4, :, :], PS[0:4, 6:8, :]))
            st.did(v.tensor_copy(NF, PS[:, 4, 0:32].rearrange("p (d t h) -> p d t h", d=2, t=4)))
            assert st.n == NF_AT
            for h in range(MLH):
                for t in range(4):
                    n, nk = 4 * h + t, 2 if t < 2 else 4
                    w = nk * P
                    if t == 0:
                        v.wait_ge(ml_bcopied, h + 1)
                    m0 = (0, 256, 512, 1024)[t]
                    st.wait()
                    for d in range(2):
                        st.did(v.tensor_tensor_reduce(TM[:, d, 0:w], GB[:, d, 0:w], MASK[:, d, m0:m0 + w], 1.0, -3e38,
                                                      ALU.add, ALU.max, STAT[:, 16 + d:17 + d]))
                    st.wait()
                    st.did(v.tensor_scalar(STAT[:, 18:20], STAT[:, 16:18], -1.0, None, ALU.mult))
                    v.tensor_tensor(STAT[:, 20:22], NF[:, :, t, h], STAT[:, 16:18], ALU.subtract).then_inc(ml_arg, 1)
                    v.wait_ge(ml_scores, n + 1)
                    v.wait_ge(ml_w, n + 1)
                    for d in range(2):
                        st.did(v.tensor_tensor_reduce(TM[:, d, 0:w], TM[:, d, 0:w], PS[:, 6, 0:w], 128.0 ** -0.5, 0.0,
                                                      ALU.mult, ALU.add, STAT[:, 22 + d:23 + d]))
                    st.wait()
                    st.link(v.tensor_scalar(STAT[:, 24:26], STAT[:, 22:24], -1.0, None, ALU.mult))
                    st.link(v.tensor_tensor(STAT[:, 24:26], STAT[:, 24:26], STAT[:, 22:24], ALU.max))
                    st.link(v.tensor_tensor(STAT[:, 24:26], STAT[:, 24:26], STAT[:, 20:22], ALU.max))
                    st.link(v.reciprocal(STAT[:, 26:28], STAT[:, 24:26]))
                    if n >= 2:
                        v.wait_ge(ml_turned, n - 1)
                    st.link(v.tensor_scalar(PR[n % 2][:, 0:w], TM[:, 0, 0:w], STAT[:, 26:27], None, ALU.mult))
                    v.scalar_tensor_tensor(PR[n % 2][:, 0:w], TM[:, 1, 0:w], STAT[:, 27:28], PR[n % 2][:, 0:w],
                                           ALU.mult, ALU.add).then_inc(ml_probs, 1)
                    v.wait_ge(ml_probs, n + 1)
                v.wait_ge(ml_pv, h + 1)
                v.tensor_tensor(G[:, 16 + h, :], G[:, 16 + h, :], PS[:, 0, :], ALU.mult).then_inc(ml_out, 1)
            v.wait_ge(pe_step, 3)
            st.did(v.tensor_tensor(G[:, 16:20, :], G[:, 16:20, :], PS[:, 4:8, :], ALU.subtract))
            assert st.n == MLC_AT, st.n
            v.wait_ge(ml_out, 6)
            st.link(v.reciprocal(SQ[:, 4:8, :], SQ[:, 4:8, :]))
            st.link(v.tensor_tensor(G[:, 16:20, :], G[:, 16:20, :], SQ[:, 4:8, :], ALU.mult))
            for h in range(MLH):
                st.did(v.tensor_scalar(YM2[:, 4 + h, :], G[:, 16 + h, :], MLG[:, h:h + 1], None, ALU.mult))
            assert st.n == MLY_AT, st.n
            v.wait_ge(bias_loaded, 16 * ROWS * NAH)
            for h in range(NAH):
                q = BIAS[:, h, :, :, :].rearrange("p q r c -> p (q r) c")
                st.did(v.tensor_tensor(q, q, bc(WIN, 8), ALU.add))
            st.wait()
            attend(EVEN_ITEMS, 0)
            projected(U_EVEN + 7, 0, 0, 0)
            rms_post(1, 0)
            rms_in(2, 0, 1, 0)
            ffn2(0, U_FFN2[0], L2, 2, 4)
            rms_post(3, 0)
            rms_in(4, 1, 0, 0)
            v.wait_ge(act_step, ODD_STD_AT)
            v.wait_ge(odd_loaded, 16 * N_ODD)
            st.did(v.reciprocal(SQ[:, 3, 0:SEQ], SQ[:, 3, 0:SEQ]))
            st.link(v.reciprocal(SQ[:, 4, :], SQ[:, 4, :]))
            st.did(v.tensor_tensor(DQ, DQ, bc(SQ[:, 3, 0:SEQ], 2), ALU.mult))
            st.did(v.tensor_tensor(CKV, CKV, SQ[:, 4, :], ALU.mult))
            st.did(v.tensor_tensor(KPE[:, CTX:L2], KPE[:, CTX:L2], RT[:, 0, :], ALU.mult))
            st.did(v.tensor_tensor(SW[:, 0, :], PS[:, 6, 0:SEQ], RT[:, 1, :], ALU.mult))
            st.wait()
            for t in range(2):
                st.did(v.tensor_scalar(DQ[:, t, :], DQ[:, t, :], QNG[:, t:t + 1], None, ALU.mult))
            st.did(v.tensor_scalar(CKV, CKV, QNG[:, 2:3], None, ALU.mult))
            st.did(v.tensor_tensor(KPE[:, CTX:L2], KPE[:, CTX:L2], SW[:, 0, :], ALU.add))
            assert st.n == ODD_Q_AT, st.n
            v.wait_ge(pe_step, 6)
            st.wait()
            for t in range(4):
                st.did(v.tensor_tensor(SW[:, t, :], PS[:, 4 + t // 2, 256 * (t % 2):256 * (t % 2) + 256], RT[:, 1, :],
                                       ALU.mult))
            q = QT[:, 8:12, :]
            st.link(v.tensor_tensor(q, q, bc(RT[:, 0, :], 4), ALU.mult))
            st.did(v.tensor_tensor(q, q, SW, ALU.add))
            assert st.n == ODD_ROPE_AT, st.n
            attend(ODD_ITEMS, len(EVEN_ITEMS))
            projected(U_ODD + 7, 1, CTX, 12)
            rms_post(5, CTX)
            rms_in(6, 1, 1, CTX)
            ffn2(1, U_FFN2[1], SEQ, 1, 16)
            rms_post(7, CTX)


def feature_major(a):
    return a.T.reshape(-1, P, a.shape[0]).transpose(1, 0, 2)


def columns(v):
    t = v.reshape(v.shape[:-1] + (-1, P))
    return np.moveaxis(t, -1, 0)


def tile_pairs(w):
    f = w.shape[1] // (2 * P)
    return w.reshape(CT, P, f, 2, P).transpose(2, 1, 3, 0, 4).reshape(f, P, 2 * D)


def wide(w):
    f = w.shape[1] // 256
    return w.reshape(CT, P, f, 256).transpose(2, 1, 0, 3).reshape(f, P, 2 * D)


def up_units(w):
    h = w.shape[1] // 2
    w = np.pad(w.reshape(D, 2, h), ((0, 0), (0, 0), (0, FF - h)))
    return w.reshape(CT, P, 2, FT, P).transpose(3, 1, 2, 0, 4).reshape(FT, P, 2 * D)


def down_units(w):
    w = np.pad(w, ((0, FF - w.shape[0]), (0, 0)))
    return w.reshape(FT, P, CT, P).transpose(2, 1, 0, 3).reshape(CT, P, SLOT)


def shape_tables():
    t = {}
    pos = np.arange(L1)
    half = 64
    ang = pos[None, :] * (10000.0 ** (-np.arange(0, 128, 2) / 128.0))[:, None]
    ang = np.concatenate([ang, ang], 0)
    t["rope_c"] = np.cos(ang)
    t["rope_s"] = np.stack([-np.sin(ang), np.sin(ang)], 1)
    decay = np.zeros((P, RH, 3, L1))
    chunk = (pos + (-META) % 64) // 64
    for h in range(RH):
        gamma = 1.0 - 2.0 ** (-5.0 - h)
        m = gamma ** np.abs(pos[None, :] - pos[:, None]) * (chunk[:, None] <= chunk[None, :]) * 128.0 ** -0.5
        for j in range(3):
            rows = m[j * P:(j + 1) * P]
            decay[:len(rows), h, j] = rows
    t["decay"] = decay
    cnt = np.zeros((P, 2, L1))
    for g, w in enumerate((2, 4, 8, 16)):
        cnt[64 * (g % 2):64 * (g % 2) + 64, g // 2] = 1.0 / np.minimum(pos + 1, w)
    t["inv_count"] = cnt
    t["ident"] = np.eye(P)
    s = np.arange(L2)
    is_ctx = s < CTX
    fwd = s[:, None] <= s[None, :]
    bwd = np.where(is_ctx[:, None], np.where(is_ctx[None, :], s[:, None] >= s[None, :], True),
                   np.where(is_ctx[None, :], False, s[:, None] >= s[None, :]))
    seen = np.stack([fwd, bwd]).astype(np.float64)
    t["seen"] = (-seen).reshape(2, 4, P, L2).transpose(2, 0, 1, 3)
    mask = np.where(seen > 0, 0.0, NEG)
    parts = [mask[:, 0:w, q * P:(q + 1) * P].transpose(2, 0, 1) for q, w in ((0, CTX), (1, CTX), (2, L2), (3, L2))]
    t["mask"] = np.concatenate(parts, 2)
    sel = np.zeros((MLH, MLH, P))
    for h in range(MLH):
        sel[h, h] = 1.0
    t["sel"] = sel.reshape(MLH, MLH * P)
    col = np.arange(GRID_W)
    cs = np.clip(col - 8, 0, GRID_W - 16)
    inside = (col[None, :] >= cs[:, None]) & (col[None, :] < cs[:, None] + 16)
    t["win"] = np.tile(np.where(inside, 0.0, NEG), (2, 1))
    d = np.arange(P) % 32
    x = np.arange(SEQ)
    where = np.where((d < 16)[:, None], (x // GRID_W)[None, :], (x % GRID_W)[None, :])
    ang = where * (10000.0 ** (-(d % 8) / 8.0))[:, None]
    t["rope2"] = np.stack([np.cos(ang), np.where((d % 16 < 8)[:, None], -np.sin(ang), np.sin(ang))], 1)
    perm = np.zeros((P, P))
    perm[np.arange(P), np.arange(P) ^ 8] = 1.0
    t["perm"] = perm
    return {k: np.ascontiguousarray(v, dtype=np.float32) for k, v in t.items()}


def lay_out(i):
    cat = np.concatenate
    a = {}
    a["x"] = feature_major(cat([i["meta"], i["x"][0]], 0))
    a["ctx"] = feature_major(i["ctx_2"][0])
    a["c"] = columns(np.stack([i["c_ctx_2"], i["c_2"][0]])).transpose(0, 2, 1)
    a["ln_in"] = columns(np.stack([i["ln_in_g"], i["ln_in_b"]]))
    a["ada"] = cat([tile_pairs(w) for w in i["ada_w_2"]], 0)
    a["ada_b"] = columns(i["ada_b_2"]).reshape(P, DEPTH * 48)
    a["norm_g"] = columns(i["norm_g_2"])
    for key, n in (("a", "ffn1"), ("b", "ffn2")):
        a["up_" + key] = cat([up_units(w) for w in i[n + "_w13"]], 0)
        a["dn_" + key] = cat([down_units(w) for w in i[n + "_w2"]], 0)
    a["up_c"] = cat([up_units(w) for w in i["ffn_w_up_2"]], 0)
    a["dn_c"] = cat([down_units(w) for w in i["ffn_w_down_2"]], 0)
    halves = np.array([[h * P + a_ * 64 + e for h in (2 * g, 2 * g + 1) for e in range(64)]
                       for g in range(2) for a_ in range(2)]).reshape(-1)
    mix, vec, pw = [], [], []
    for l in range(DEPTH):
        w = i["w_in"][l]
        pws = i["conv_pw"][l].reshape(2, P, 2, P).transpose(1, 2, 0, 3).reshape(P, 512)
        mix.append(cat([tile_pairs(w[:, 0:768]), tile_pairs(w[:, 768:1280][:, halves]),
                        tile_pairs(w[:, 1280:1792][:, halves]), tile_pairs(w[:, 2304:2816]), wide(w[:, 1792:2304]),
                        np.pad(pws, ((0, 0), (0, 2 * D - 512)))[None], tile_pairs(i["w_out"][l])], 0))
        dw = columns(i["conv_dw"][l]).reshape(P, 2 * TAPS)
        vec.append(cat([columns(i["ln_g"][l]).reshape(P, 24), columns(i["ln_b"][l]).reshape(P, 24),
                        columns(i["pool_scale"][l]), dw, columns(i["conv_db"][l]), columns(i["conv_ln_g"][l]),
                        columns(i["conv_ln_b"][l]), columns(i["ret_gn_g"][l])], 1))
        g4 = i["pool_w"][l]
        blocks = np.zeros((P, 2, P), np.float32)
        for g in range(4):
            q = slice(64 * (g % 2), 64 * (g % 2) + 64)
            blocks[q, g // 2, q] = g4[g]
        pw.append(blocks)
    a["mix"], a["vec"], a["pool_w"] = cat(mix, 0), np.stack(vec), np.stack(pw)
    w = i["ev_w_in_2"][0]
    a["even"] = cat([tile_pairs(w[:, 0:1024]), tile_pairs(w[:, 1536:2560]), tile_pairs(w[:, 3072:3584]),
                     wide(w[:, 1024:1536]), wide(w[:, 2560:3072]), tile_pairs(i["ev_w_out_2"][0])], 0)
    a["wg"] = w[:, 3584:3600].reshape(CT, P, 16).transpose(1, 0, 2)
    a["gate_b"] = np.tile(i["ev_gate_b_2"], (P, 1))
    a["ml_g"] = columns(i["ev_ml_norm_g_2"][0])

    def taps(w, b, lead):
        t = columns(cat([w, b[None]], 0)).transpose(0, 2, 1)
        return t if lead is None else t.reshape(P, 2, -1, 4).transpose(0, 2, 1, 3)
    a["evw"] = taps(i["ev_conv_w_2"][0], i["ev_conv_b_2"][0], None)
    for l in range(DEPTH):
        a[f"fcw{l}"] = taps(i["ffn_conv_w_2"][l], i["ffn_conv_b_2"][l], 2)
    r = i["ev_rpb_2"][0][:, 8 - ROWS:7 + ROWS]
    r = np.pad(r, ((0, 0), (0, 0), (GRID_W - 16, GRID_W - 16)))
    a["rpb"] = np.tile(r, (1, 1, GRID_W))
    kv = i["od_w_dkv_2"][0]
    a["odd"] = cat([tile_pairs(i["od_w_dq_2"][0]), tile_pairs(cat([kv[:, 0:128]] + [kv[:, 128:160]] * 4, 1)),
                    tile_pairs(i["od_w_o_2"][0])], 0)
    uq = i["od_w_uq_2"][0].reshape(256, MLAH, 96)
    uq = cat([uq[:, :, 0:64].reshape(256, 1024), uq[:, :, 64:96].reshape(256, 512)], 1)
    a["uq"] = uq.reshape(2, P, 12, P).transpose(1, 2, 0, 3)
    ukv = i["od_w_ukv_2"][0].reshape(128, MLAH, 128)
    a["ukv"] = cat([ukv[:, :, 0:64].reshape(128, 1024), ukv[:, :, 64:128].reshape(128, 1024)], 1)
    a["qkv_g"] = cat([columns(i["od_q_norm_g_2"][0]), columns(i["od_kv_norm_g_2"][0])], 1)
    a.update(shape_tables())
    return {k: np.ascontiguousarray(v) for k, v in a.items()}


def kernel(**inputs):
    import concourse.bacc as bacc
    from concourse.bass_utils import run_bass_kernel_spmd

    nc = bacc.Bacc("TRN2", target_bir_lowering=False, num_devices=1)
    arrays = {"in_" + k: v for k, v in lay_out({k: np.asarray(v) for k, v in inputs.items()}).items()}
    A = {k[3:]: nc.dram_tensor(k, v.shape, F32, kind="ExternalInput").ap() for k, v in arrays.items()}
    out = nc.dram_tensor("out", (P, CT, SEQ), F32, kind="ExternalOutput").ap()
    build(nc, A, out)
    r = run_bass_kernel_spmd(nc, [arrays], core_ids=[0]).results[0]["out"]
    return np.ascontiguousarray(r.transpose(1, 0, 2).reshape(D, SEQ).T)[None]
```

```python
from contextlib import ExitStack

import numpy as np

import concourse.bass as bass
from concourse import mybir

ALU = mybir.AluOpType
ACT = mybir.ActivationFunctionType
AX = mybir.AxisListType
F32 = mybir.dt.float32
F32R = mybir.dt.float32r

P = 128
D = 1024
CT = D // P
META = 16
SEQ = 256
CTX = 256
L1 = META + SEQ
L2 = CTX + SEQ
X0 = L2 - L1
DEPTH = 2
FT = 22
FF = FT * P
ACT_TILES = 5
SLOT = FT * P
ALPHA = (2.0 * DEPTH) ** 0.25
TAPS = 31
RH = 4
GRID_W = 64
ROWS = SEQ // GRID_W
NAH, NAD = 8, 64
MLH = 4
MLAH = 16
NEG = -1e30
RPB_PERIOD = 2 * GRID_W - 1
RPB_ROW = GRID_W * RPB_PERIOD
N_X, N_START, N_TABLES, N_ODD = 3, 6, 9, 5
SPLIT_EVEN = 10
N_SET = 12

ADA_UNITS = 12
PAIRS_UP, PAIRS_DN = FT // 2, CT // 2
PAIRS_FFN = PAIRS_UP + PAIRS_DN
PAIRS_MIX = 8
PAIRS_LAYER = 2 * PAIRS_FFN + PAIRS_MIX
PAIRS_EVEN = 9
PAIRS_ODD = 9

V_LNG, V_LNB, V_PS, V_DW, V_DB, V_CG, V_CB, V_GN = 0, 24, 48, 50, 112, 114, 116, 118
NV = 122


def build(nc, A, out):
    with ExitStack() as ctx:
        def sb(name, shape):
            return ctx.enter_context(nc.sbuf_tensor(name, shape, F32))

        def sem(name):
            return ctx.enter_context(nc.semaphore(name))

        X = sb("X", [P, CT, L2])
        with ExitStack() as over:
            XLO, XHI = (over.enter_context(nc.sbuf_tensor(n, [P, CT, L2], F32R)) for n in ("XLO", "XHI"))
        PRE = sb("PRE", [P, CT, L2])
        SQ = sb("SQ", [P, CT, L2])
        RING = sb("RING", [P, 2, SLOT])
        G = sb("G", [P, FT, L2])
        SG = sb("SG", [P, 2, L2])
        RSTD = sb("RSTD", [P, L2])
        VEC = sb("VEC", [P, NV])
        LNIN = sb("LNIN", [P, 2, CT])
        ONES = sb("ONES", [P, 3, P])
        ONE = sb("ONE", [P, 1])
        EPS5 = sb("EPS5", [P, 1])
        EPS6 = sb("EPS6", [P, 1])
        SC = sb("SC", [P, CT, 2])
        ADAB = sb("ADAB", [P, DEPTH * 48])
        MODF = sb("MOD", [P, DEPTH * 48, 2])
        MOD = MODF[:, :, :].rearrange("p (l m) g -> p l m g", l=DEPTH)
        NG = sb("NG", [P, DEPTH, 4, CT])
        GIN = sb("GIN", [P, DEPTH, 2, CT, 2])
        GOUT = sb("GOUT", [P, DEPTH, 2, CT, 2])
        BW = 21056
        B2_SHARED = 11824
        with ExitStack() as over:
            over.enter_context(nc.sbuf_tensor("B_IDN", [P, P], F32R))
            XLO2 = over.enter_context(nc.sbuf_tensor("XLO2", [P, CT, L2], F32R))
            over.enter_context(nc.sbuf_tensor("B_SHARED", [P, B2_SHARED - P - CT * L2], F32R))
            WHI, WLO = (over.enter_context(nc.sbuf_tensor(n, [P, 2, 2 * D], F32R)) for n in ("WHI", "WLO"))
        B = sb("B", [P, BW])
        PS = ctx.enter_context(nc.psum_tensor("PS", [P, 8, 512], F32))

        used = {}

        def carve(region, base, words, shape, **dims):
            at = used.get(region, 0)
            used[region] = at + words
            total = {"G1": FT * L2, "G2": FT * L2, "G3": FT * L2}.get(region, BW)
            assert used[region] <= total, (region, used[region], total)
            v = base[:, at:at + words]
            return v.rearrange(shape, **dims) if shape else v

        SUMS = SG
        GF = G[:, :, :].rearrange("p a b -> p (a b)")
        YM = carve("G1", GF, CT * L1, "p (a b) -> p a b", a=CT)
        QK = carve("G1", GF, 8 * L1, "p (a b) -> p a b", a=8)
        V1 = carve("G1", GF, 3 * 512, "p (a b) -> p a b", a=3)
        OT = carve("G1", GF, 4 * L1, "p (a b) -> p a b", a=4)
        STD4 = carve("G1", GF, 4 * L1, "p (a b) -> p a b", a=4)
        GS = carve("G1", GF, 4 * L1, "p (a b) -> p a b", a=4)
        ST = carve("G1", GF, 2 * 3 * L1, "p (z a b) -> p z a b", z=2, a=3)
        DT = carve("B1", B, RH * 3 * L1, "p (h a b) -> p h a b", h=RH, a=3)
        RC = carve("B1", B, L1, None)
        RS = carve("B1", B, 2 * L1, "p (a b) -> p a b", a=2)
        IC = carve("B1", B, 2 * L1, "p (a b) -> p a b", a=2)
        XP = carve("B1", B, 2 * (16 + L1), "p (a b) -> p a b", a=2)
        PT_ = [carve("B1", B, 2 * (16 + L1), "p (a b) -> p a b", a=2) for _ in range(4)]
        WN = carve("B1", B, 2 * L1, "p (a b) -> p a b", a=2)
        PM = carve("B1", B, 2 * L1, "p (a b) -> p a b", a=2)
        CA = carve("B1", B, 2 * L1, "p (a b) -> p a b", a=2)
        CSG = carve("B1", B, 2 * L1, "p (a b) -> p a b", a=2)
        CP = carve("B1", B, 2 * (TAPS - 1 + L1), "p (a b) -> p a b", a=2)
        ACC = carve("B1", B, 2 * L1, "p (a b) -> p a b", a=2)
        T1 = carve("B1", B, 2 * L1, "p (a b) -> p a b", a=2)
        T2 = carve("B1", B, 2 * L1, "p (a b) -> p a b", a=2)
        CY = carve("B1", B, 2 * L1, "p (a b) -> p a b", a=2)
        CSQ = carve("B1", B, 2 * L1, "p (a b) -> p a b", a=2)
        PW = carve("B1", B, 2 * P, "p (a b) -> p a b", a=2)
        CSTD = carve("B1", B, L1, None)
        AW = carve("B1", B, 2 * D, "p (j k c) -> p j k c", j=2, k=CT)
        AP_ = carve("B1", B, 2 * 2 * P, "p (g j c) -> p g j c", g=2, j=2)
        IDN = carve("B2", B, P, None)
        YM2 = carve("B2", B, CT * L2, "p (a b) -> p a b", a=CT)
        CB = [carve("B2", B, 2 * 2 * 258, "p (a g b) -> p a g b", a=2, g=2) for _ in range(2)]
        AC = [carve("B2", B, 2 * L2, "p (a g b) -> p a g b", a=2, g=2) for _ in range(2)]
        FCW = [carve("B2", B, FT * 2 * 4, "p (f a c) -> p f a c", f=FT, a=2) for _ in range(2)]
        TM = carve("B2", B, 2 * 512, "p (d w) -> p d w", d=2)
        SS = [TM[:, 0, :], TM[:, 1, :]]
        PR = [carve("B2", B, 512, None) for _ in range(2)]
        PTT = [carve("B2", B, 512, "p (a b) -> p a b", a=4) for _ in range(2)]
        STAT = carve("B2", B, 64, None)
        assert used["B2"] == B2_SHARED, used["B2"]
        assert B2_SHARED + 2 * 2 * 2 * D <= BW
        VN = carve("B2", B, 4 * 512, "p (a b) -> p a b", a=4)
        VM = carve("B2", B, 4 * 512, "p (a b) -> p a b", a=4)
        MASK = carve("B2", B, 2 * 3 * 512, "p (d w) -> p d w", d=2)
        GB = carve("B2", B, 2 * 512, "p (d w) -> p d w", d=2)
        assert used["B2"] == B2_SHARED + 2 * 2 * 2 * D
        EVW = carve("B2", B, 8 * 4, "p (f c) -> p f c", c=4)
        WG = carve("B2", B, CT * 16, "p (a b) -> p a b", a=CT)
        GR = SG
        SEL = carve("B2", B, MLH * P, None)
        GBIAS = carve("B2", B, 16, None)
        GT = carve("B2", B, 64, "p (a b) -> p a b", a=4)
        GE = carve("B2", B, 64, "p (a b) -> p a b", a=4)
        LS = carve("B2", B, 64, "p (a b) -> p a b", a=4)
        NF = carve("B2", B, 32, "p (d t h) -> p d t h", d=2, t=4)
        MLG = carve("B2", B, MLH, None)
        used["B3"] = B2_SHARED
        WUQ = carve("B3", B, 12 * 2 * P, "p (f k c) -> p f k c", f=12, k=2)
        WUKV = carve("B3", B, 2 * D, None)
        DQ = carve("B3", B, 2 * SEQ, "p (a b) -> p a b", a=2)
        CKV = carve("B3", B, L2, None)
        KPE = carve("B3", B, L2, None)
        RT = carve("B3", B, 2 * SEQ, "p (a b) -> p a b", a=2)
        PERM = carve("B3", B, P, None)
        SW = carve("B3", B, 4 * SEQ, "p (a b) -> p a b", a=4)
        QNG = carve("B3", B, 3, None)
        QT = carve("G3", GF, 12 * SEQ, "p (a b) -> p a b", a=12)
        KN = carve("G3", GF, 8 * L2, "p (a b) -> p a b", a=8)
        VV = carve("G3", GF, 4 * D, "p (a b) -> p a b", a=4)
        SQF = SQ[:, :, :].rearrange("p a b -> p (a b)")
        NU = SQF.rearrange("p (d s t) -> p d s t", d=2, s=4)
        TMS, GBS = [TM, SQ[:, 0:2, :]], [GB, SQ[:, 2:4, :]]
        ML_KEYS = (2, 2, 4, 4)
        ML_ITEMS = 4 * MLH
        ML_STD = SQ[:, 4:8, :]
        BIAS = PRE[:, :, :].rearrange("p a (q r c) -> p a q r c", q=2, r=ROWS)

        WIN = carve("B2", B, GRID_W, None)

        def item(qk, keys, scale, v, rows, o, bias=None):
            return {"qk": qk, "keys": keys, "scale": scale, "v": v, "rows": rows, "out": o, "bias": bias,
                    "sb": bias is not None}

        def na_item(h, t):
            q = slice(64 * (h % 2), 64 * (h % 2) + 64)
            keys = CTX if t < 2 else L2
            return item([(G[q, h // 2, t * P:(t + 1) * P], G[q, 4 + h // 2, 0:keys])], keys, NAD ** -0.5,
                        lambda j: VN[:, j, h * NAD:(h + 1) * NAD], q, YM2[q, h // 2, t * P:(t + 1) * P],
                        None if t < 2 else BIAS[:, h, t - 2, :, :].rearrange("p r c -> p (r c)"))

        def mla_item(h, t):
            q, r = slice(64 * (h % 2), 64 * (h % 2) + 64), slice(32 * (h % 4), 32 * (h % 4) + 32)
            cols = slice(t * P, (t + 1) * P)
            return item([(QT[q, h // 2, cols], KN[q, h // 2, :]), (QT[r, 8 + h // 4, cols], KPE[r, :])],
                        L2, 96.0 ** -0.5, lambda j: VV[:, j, h * 64:(h + 1) * 64], q,
                        YM2[q, h // 2, CTX + t * P:CTX + (t + 1) * P])

        EVEN_ITEMS = [na_item(h, t) for t in range(4) for h in range(NAH)]
        ODD_ITEMS = [mla_item(h, t) for h in range(MLAH) for t in range(2)]

        GAIN_STEPS = DEPTH * 2 * 5
        ABS_AT = 3
        LS_AT = ABS_AT + 2
        NF_AT = LS_AT + 2
        EVEN_AT = NF_AT + 4 * MLH * 9 + sum(4 if i["sb"] else 2 for i in EVEN_ITEMS) + 1
        ODD_Q_AT = EVEN_AT + 11
        ODD_ROPE_AT = ODD_Q_AT + 6
        ODD_STD_AT = 3

        XL = X[:, :, X0:L2]
        PL = PRE[:, :, 0:L1]
        SL = SQ[:, :, 0:L1]

        w_loaded = [sem("w_loaded0"), sem("w_loaded1")]
        unit_done = [sem("unit_done0"), sem("unit_done1")]
        unit_taken = [sem("unit_taken0"), sem("unit_taken1")]
        x_loaded = sem("x_loaded")
        start_loaded = sem("start_loaded")
        start_set = sem("start_set")
        w_high = [sem("w_high0"), sem("w_high1")]
        w_split = [sem("w_split0"), sem("w_split1")]
        x_high, x_split = sem("x_high"), sem("x_split")
        mask_loaded = sem("mask_loaded")
        vec_loaded = sem("vec_loaded")
        silu_c = sem("silu_c")
        ada_loaded, ada_summed, ada_done, ada_taken = (sem("ada_loaded"), sem("ada_summed"), sem("ada_done"),
                                                       sem("ada_taken"))
        ada_step, ada_last_loaded = sem("ada_step"), sem("ada_last_loaded")
        gains_step = sem("gains_step")
        silu_done = [sem("silu_done0"), sem("silu_done1")]
        residual_scaled = sem("residual_scaled")
        ln_mean, ln_centred, ln_squared, ln_var = sem("ln_mean"), sem("ln_centred"), sem("ln_squared"), sem("ln_var")
        ln_std, ln_rstd, ln_scaled, ln_out = sem("ln_std"), sem("ln_rstd"), sem("ln_scaled"), sem("ln_out")
        sum_added, sum_squared = sem("sum_added"), sem("sum_squared")
        conv_gate, silu_g = sem("conv_gate"), sem("silu_g")
        mix_step, conv_tap, pool_step = sem("mix_step"), sem("conv_tap"), sem("pool_step")
        ret_scores, ret_decayed, ret_out, ret_copied = (sem("ret_scores"), sem("ret_decayed"), sem("ret_out"),
                                                        sem("ret_copied"))
        cv_mean, cv_squared, cv_var, cv_std, cv_silu = (sem("cv_mean"), sem("cv_squared"), sem("cv_var"),
                                                        sem("cv_std"), sem("cv_silu"))
        gn_stat, gn_squared, gn_std, gn_y = sem("gn_stat"), sem("gn_squared"), sem("gn_std"), sem("gn_y")
        pooled_taken = sem("pooled_taken")
        ctx_loaded, tab_loaded, u_loaded, bias_loaded, odd_loaded = (sem("ctx_loaded"), sem("tab_loaded"),
                                                                     sem("u_loaded"), sem("bias_loaded"),
                                                                     sem("odd_loaded"))
        rm_squared, rm_var, rm_std, rm_rstd, rm_scaled, rm_in, rm_out = (
            sem("rm_squared"), sem("rm_var"), sem("rm_std"), sem("rm_rstd"), sem("rm_scaled"), sem("rm_in"),
            sem("rm_out"))
        side_step = [sem("side_step0"), sem("side_step1")]
        tap_side = [sem("tap_side0"), sem("tap_side1")]
        tap_silu = [sem("tap_silu0"), sem("tap_silu1")]
        tap_prod = [sem("tap_prod0"), sem("tap_prod1")]
        borders_zero = sem("borders_zero")
        vec_step, act_step, pe_step = sem("vec_step"), sem("act_step"), sem("pe_step")
        at_scores, at_max, at_exp, at_probs, at_turned, at_copied, at_pv, at_out = (
            sem("at_scores"), sem("at_max"), sem("at_exp"), sem("at_probs"), sem("at_turned"), sem("at_copied"),
            sem("at_pv"), sem("at_out"))
        ml_bc, ml_bcopied, ml_arg, ml_w, ml_probs, ml_scores, ml_turned, ml_copied, ml_pv, ml_out = (
            sem("ml_bc"), sem("ml_bcopied"), sem("ml_arg"), sem("ml_w"), sem("ml_probs"), sem("ml_scores"),
            sem("ml_turned"), sem("ml_copied"), sem("ml_pv"), sem("ml_out"))
        ml_mean, ml_centred, ml_squared, ml_std, ml_rstd, ml_normed, bias_ready = (
            sem("ml_mean"), sem("ml_centred"), sem("ml_squared"), sem("ml_std"), sem("ml_rstd"), sem("ml_normed"),
            sem("bias_ready"))
        out_stored = sem("out_stored")
        passed = {e: sem("passed_" + e) for e in ("pool", "vector", "tensor")}

        def lay(l, per, n):
            return n if l is None else l * per + n

        U_FFN_A, U_MIX, U_FFN_B = 0, PAIRS_FFN, PAIRS_FFN + PAIRS_MIX
        U_EVEN = DEPTH * PAIRS_LAYER
        U_FFN2 = [U_EVEN + PAIRS_EVEN, U_EVEN + PAIRS_EVEN + PAIRS_FFN + PAIRS_ODD]
        U_ODD = U_FFN2[0] + PAIRS_FFN
        VIRTUAL = PAIRS_ODD - 3

        class Steps:

            def __init__(self, eng, s, base=0, total=None):
                self.eng, self.s, self.base, self.n, self.total = eng, s, base, 0, total

            def did(self, ins):
                self.n += 1
                ins.then_inc(self.s, 1)
                return ins

            def wait(self, back=0):
                self.eng.wait_ge(self.s, self.base + (self.n - back))

            def link(self, ins):
                self.did(ins)
                self.wait()

            def end(self):
                assert self.total is None or self.n == self.total, (self.n, self.total)

        MIX_STEPS = 21
        POOL_STEPS = 9

        def mm(pe, o, w, x, first, last):
            return pe.matmul(o, w, x, start=first, stop=last)

        block = ctx.enter_context(nc.Block())

        @block.sync
        def _(sp):
            def load(src, u_prev, s, words):
                sp.wait_ge(unit_done[s], u_prev + 1)
                sp.dma_start(RING[:, s, 0:words], src).then_inc(w_loaded[s], 16)

            def ffn_load(up, dn, l, row, u, ada=None):
                with sp.Fori(0, PAIRS_UP) as i:
                    for s in range(2):
                        r = (l * FT + i * 2 + (row * FT + s)) if l is not None else (i * 2 + (row * FT + s))
                        load(up[r, :, :], u + i, s, 2 * D)
                        if s == 0 and ada is not None:
                            ada_load(ada + i)
                with sp.Fori(0, PAIRS_DN) as i:
                    for s in range(2):
                        r = (l * CT + i * 2 + (row * CT + s)) if l is not None else (i * 2 + (row * CT + s))
                        load(dn[r, :, :], u + i + PAIRS_UP, s, SLOT)

            def ffn_load_split(f, u):
                for s in range(2):
                    load(A["up_c"][f * FT + s, :, :], u, s, 2 * D)
                with sp.Fori(1, PAIRS_UP) as i:
                    for s in range(2):
                        sp.wait_ge(w_split[s], i + (SPLIT_EVEN // 2 + PAIRS_UP * f))
                        sp.dma_start(RING[:, s, 0:2 * D], A["up_c"][i * 2 + (f * FT + s), :, :]).then_inc(w_loaded[s], 16)
                for s in range(2):
                    sp.wait_ge(w_split[s], SPLIT_EVEN // 2 + PAIRS_UP * (f + 1))
                    sp.dma_start(RING[:, s, :], A["dn_c"][f * CT + s, :, :]).then_inc(w_loaded[s], 16)
                with sp.Fori(1, PAIRS_DN) as i:
                    for s in range(2):
                        load(A["dn_c"][i * 2 + (f * CT + s), :, :], u + i + PAIRS_UP, s, SLOT)

            def ada_load(n):
                sp.wait_ge(ada_summed, n + 1)
                sp.dma_start(AW, A["ada"][n, :, :].rearrange("p (j k c) -> p j k c", j=2, k=CT)).then_inc(ada_loaded, 16)

            with sp.Fori(0, DEPTH) as l:
                ffn_load(A["up_a"], A["dn_a"], l, 0, l * PAIRS_LAYER + U_FFN_A, l * (2 * ADA_UNITS))
                with sp.Fori(0, PAIRS_MIX) as i:
                    for s in range(2):
                        load(A["mix"][l * (2 * PAIRS_MIX) + i * 2 + s, :, :], l * PAIRS_LAYER + i + U_MIX, s, 2 * D)
                ffn_load(A["up_b"], A["dn_b"], l, 0, l * PAIRS_LAYER + U_FFN_B, l * (2 * ADA_UNITS) + ADA_UNITS)
            with sp.Fori(0, PAIRS_EVEN) as i:
                for s in range(2):
                    load(A["even"][i * 2 + s, :, :], i + U_EVEN, s, 2 * D)
            ffn_load_split(0, U_FFN2[0])
            for n in range(6):
                u_prev = U_ODD + (0 if n < 2 else 1 if n < 4 else PAIRS_ODD - 1)
                load(A["odd"][n, :, :], u_prev, n % 2, 2 * D)
            ffn_load_split(1, U_FFN2[1])
            sp.wait_ge(rm_out, 4 * 4)
            sp.dma_start(out, X[:, :, CTX:L2]).then_inc(out_stored, 16)
            sp.wait_ge(out_stored, 16)

        @block.gpsimd
        def _(pool):
            for n, v in enumerate((1.0 / D, 1.0 / 256, 1.0 / P)):
                pool.memset(ONES[:, n, :], v).then_inc(start_set, 1)
            pool.memset(ONE[:, :], 1.0).then_inc(start_set, 1)
            pool.memset(EPS5[:, :], 1e-5).then_inc(start_set, 1)
            pool.memset(EPS6[:, :], 1e-6).then_inc(start_set, 1)
            pool.memset(XP[:, :, 0:16], 0.0).then_inc(start_set, 1)
            for t in PT_:
                pool.memset(t[:, :, 0:16], 0.0).then_inc(start_set, 1)
            pool.memset(CP[:, :, 0:TAPS - 1], 0.0).then_inc(start_set, 1)
            pool.wait_ge(start_set, N_SET)

            def scale_residual(norms):
                pool.wait_ge(ln_out, norms)
                pool.sem_inc(passed["pool"], 1)
                pool.tensor_scalar(PL, XL, ALPHA, None, ALU.mult).then_inc(residual_scaled, 1)

            for dst, name in ((PL, "x"), (LNIN[:, :, :], "ln_in"), (SC[:, :, :], "c")):
                pool.dma_start(dst, A[name]).then_inc(x_loaded, 16)
            for dst, name in ((ADAB[:, :], "ada_b"), (NG[:, :, :, :], "norm_g"), (DT, "decay"), (RC, "rope_c"), (RS, "rope_s"), (IC, "inv_count")):
                pool.dma_start(dst, A[name]).then_inc(start_loaded, 16)

            def ada_load(n):
                pool.wait_ge(ada_summed, n + 1)
                pool.dma_start(AW, A["ada"][n, :, :].rearrange("p (j k c) -> p j k c", j=2, k=CT))\
                    .then_inc(ada_last_loaded, 16)

            with pool.Fori(0, DEPTH) as l:
                pool.wait_ge(ln_out, l * 24 + 8)
                pool.dma_start(VEC[:, :], A["vec"][l, :, :]).then_inc(vec_loaded, 16)
                pool.dma_start(PW, A["pool_w"][l, :, :, :]).then_inc(vec_loaded, 16)
                scale_residual(l * 24 + 8)
                ada_load(l * (2 * ADA_UNITS) + (ADA_UNITS - 1))
                scale_residual(l * 24 + 16)
                st = Steps(pool, pool_step, l * POOL_STEPS, POOL_STEPS)
                pool.wait_ge(unit_taken[0], l * PAIRS_LAYER + U_MIX + 2)
                src, n = XP, 16 + L1
                for j in range(4):
                    w = 1 << j
                    lo = 2 * w - 1
                    st.link(pool.tensor_tensor(PT_[j][:, :, lo:n], src[:, :, lo:n], src[:, :, lo - w:n - w], ALU.add))
                    src = PT_[j]
                for j in range(4):
                    q = slice(64 * (j % 2), 64 * (j % 2) + 64)
                    st.did(pool.tensor_tensor(WN[q, j // 2, :], PT_[j][q, j // 2, 16:n], IC[q, j // 2, :], ALU.mult))
                st.wait()
                st.did(pool.tensor_tensor(PM, WN, XP[:, :, 16:n], ALU.subtract))
                st.end()
                scale_residual(l * 24 + 24)
                ada_load(l * (2 * ADA_UNITS) + (2 * ADA_UNITS - 1))

            pool.wait_ge(ln_out, 8 * 7)
            pool.dma_start(X[:, :, 0:CTX], A["ctx"]).then_inc(ctx_loaded, 16)
            for dst, name in ((IDN, "ident"), (FCW[0], "fcw0"), (FCW[1], "fcw1"), (EVW, "evw"), (WG, "wg"),
                              (SEL[0:4, :], "sel"), (WIN, "win"), (GBIAS, "gate_b"), (MLG, "ml_g")):
                pool.dma_start(dst, A[name]).then_inc(tab_loaded, 16)
            for c in CB:
                pool.memset(c[:, :, :, 0:258:257], 0.0).then_inc(borders_zero, 1)
            for s in range(2):
                pool.wait_ge(unit_done[s], U_EVEN + SPLIT_EVEN // 2 + 1)
            pool.dma_start(MASK, A["mask"]).then_inc(mask_loaded, 16)
            pool.dma_start(NU, A["seen"]).then_inc(u_loaded, 16)
            for s in range(2):
                pool.wait_ge(unit_done[s], U_EVEN + 7 + 1)
            pool.wait_ge(pe_step, 1)
            for r in range(ROWS):
                for h in range(NAH):
                    src = bass.AP(A["rpb"].tensor, ((h * 7) + (ROWS - 1 - r)) * RPB_ROW + (GRID_W - 1),
                                  [[RPB_PERIOD - 1, GRID_W], [RPB_ROW, ROWS], [1, GRID_W]])
                    pool.dma_start(BIAS[GRID_W * (r % 2):GRID_W * (r % 2) + GRID_W, h, r // 2, :, :], src)\
                        .then_inc(bias_loaded, 16)
            pool.wait_ge(bias_loaded, 16 * ROWS * NAH)
            for h in range(NAH):
                q = BIAS[:, h, :, :, :].rearrange("p q r c -> p (q r) c")
                pool.tensor_tensor(q, q, WIN.rearrange("p (o n) -> p o n", o=1).to_broadcast([P, 8, GRID_W]), ALU.add)\
                    .then_inc(bias_ready, 1)
            for s in range(2):
                pool.wait_ge(unit_done[s], U_FFN2[0] + PAIRS_UP + 1)
            for dst, name in ((WUQ, "uq"), (WUKV, "ukv"), (RT, "rope2"), (PERM, "perm"), (QNG, "qkv_g")):
                pool.dma_start(dst, A[name]).then_inc(odd_loaded, 16)

        @block.tensor
        def _(pe):
            pe.wait_ge(start_set, N_SET)
            for s in range(2):
                mm(pe, PS[:, 2 * s, 0:P], ONES[:, 0, :], ONES[:, 1, :], True, True).then_inc(unit_done[s], 1)
            mm(pe, PS[:, 6, 0:P], ONES[:, 0, :], ONES[:, 1, :], True, True).then_inc(ada_done, 1)

            def begin(s, ld, u):
                pe.wait_ge(w_loaded[s], ld * 16 + 16)
                pe.wait_ge(unit_taken[s], u + 1)

            def two_tiles(s, rhs, n):
                for j in range(2):
                    for k in range(CT):
                        last = mm(pe, PS[:, 2 * s + j, 0:n], RING[:, s, (j * CT + k) * P:(j * CT + k + 1) * P],
                                  rhs[:, k, :], k == 0, k == CT - 1)
                return last

            def token_major(s, lhs, tts):
                c0 = 0
                for t, w in enumerate(tts):
                    o = PS[0:w, 2 * s + t // 2, 256 * (t % 2):256 * (t % 2) + 256]
                    for k in range(CT):
                        last = mm(pe, o, lhs[:, k, c0:c0 + w], RING[:, s, k * 256:(k + 1) * 256], k == 0, k == CT - 1)
                    c0 += w
                return last

            def ada_unit(n):
                pe.wait_ge(ada_summed, n + 2)
                pe.wait_ge(ada_taken, n + 1)
                for j in range(2):
                    for g in range(2):
                        last = mm(pe, PS[:, 6, 2 * j + g:2 * j + g + 1], AP_[:, g, j, :], ONE[:, :], True, True)
                last.then_inc(ada_done, 1)

            def two_tiles_split(s, c0, xlo):
                for j in range(2):
                    for k in range(CT):
                        w = slice((j * CT + k) * P, (j * CT + k + 1) * P)
                        for z, (a, b) in enumerate(((WHI, XHI), (WHI, xlo), (WLO, XHI))):
                            last = mm(pe, PS[:, 2 * s + j, 0:L2 - c0], a[:, s, w], b[:, k, c0:L2],
                                      k == 0 and z == 0, k == CT - 1 and z == 2)
                return last

            def ffn(u, ld, rhs, n, hidden_ready, ada=None, split=None):
                with pe.Fori(0, PAIRS_UP) as i:
                    for s in range(2):
                        if split is None:
                            begin(s, ld + i, u + i)
                            two_tiles(s, rhs, n).then_inc(unit_done[s], 1)
                        else:
                            pe.wait_ge(w_split[s], i + (SPLIT_EVEN // 2 + PAIRS_UP * split + 1))
                            pe.wait_ge(unit_taken[s], u + i + 1)
                            two_tiles_split(s, L2 - n, XLO).then_inc(unit_done[s], 1)
                    if ada is not None:
                        ada_unit(ada + i)
                def down(s, i, late=0):
                    begin(s, ld + i + PAIRS_UP, u + i + PAIRS_UP)
                    for k in range(FT):
                        if late and k == FT - late:
                            for z in range(2):
                                hidden_ready(z, 1)
                        last = mm(pe, PS[:, 2 * s, 0:n], RING[:, s, k * P:(k + 1) * P], G[:, k, 0:n], k == 0,
                                  k == FT - 1)
                    last.then_inc(unit_done[s], 1)

                for s in range(2):
                    hidden_ready(s, 0)
                down(0, 0, 2)
                down(1, 0)
                with pe.Fori(1, PAIRS_DN) as i:
                    for s in range(2):
                        down(s, i)
                if ada is not None:
                    ada_unit(ada + (ADA_UNITS - 1))

            def layer_norm(l, e, du):
                if du is None:
                    pe.wait_ge(x_loaded, 16 * N_X)
                else:
                    for s in range(2):
                        pe.wait_ge(unit_taken[s], lay(l, PAIRS_LAYER, du + 1))
                src, nt = (PL, CT) if du is None else (SUMS[:, :, 0:L1], 2)
                for k in range(nt):
                    last = mm(pe, PS[:, 4, 0:L1], ONES[:, 0, :], src[:, k, :], k == 0, k == nt - 1)
                last.then_inc(ln_mean, 1)
                for c in range(4):
                    pe.wait_ge(ln_squared, lay(l, 12, 4 * e + c + 1))
                    for k in (2 * c, 2 * c + 1):
                        last = mm(pe, PS[:, 5, 0:L1], ONES[:, 0, :], SL[:, k, :], k == 0, k == CT - 1)
                last.then_inc(ln_var, 1)

            layer_norm(None, 0, None)

            def mixer(l):
                u, n = l * PAIRS_LAYER, 0
                pe.wait_ge(ln_out, l * 24 + 16)
                for n in range(9):
                    s = n % 2
                    begin(s, u + (U_MIX + n // 2), u + (U_MIX + n // 2))
                    two_tiles(s, XL, L1).then_inc(unit_done[s], 1)
                for n in (9, 10):
                    s = n % 2
                    begin(s, u + (U_MIX + n // 2), u + (U_MIX + n // 2))
                    token_major(s, XL, (P, P, META)).then_inc(unit_done[s], 1)

                def scores(h):
                    if h == 0:
                        pe.wait_ge(mix_step, l * MIX_STEPS + 12)
                    else:
                        pe.wait_ge(ret_decayed, l * 4 + h)
                    q = slice(64 * (h % 2), 64 * (h % 2) + 64)
                    for jt in range(3):
                        w = P if jt < 2 else META
                        for a in range(2):
                            last = mm(pe, PS[0:w, 4 + jt, 0:L1], QK[q, 4 + 2 * (h // 2) + a, jt * P:jt * P + w],
                                      QK[q, 2 * (h // 2) + a, :], a == 0, a == 1)
                    last.then_inc(ret_scores, 1)

                def values(h):
                    pe.wait_ge(ret_decayed, l * 4 + h + 1)
                    if h == 0:
                        for s in range(2):
                            pe.wait_ge(unit_taken[s], u + (U_MIX + (5 if s else 6) + 1))
                    else:
                        pe.wait_ge(ret_copied, l * 4 + h)
                    for jt in range(3):
                        w = P if jt < 2 else META
                        last = mm(pe, PS[:, 7, 0:L1], V1[0:w, jt, h * P:(h + 1) * P], ST[0:w, h % 2, jt, :],
                                  jt == 0, jt == 2)
                    last.then_inc(ret_out, 1)

                scores(0)
                pe.wait_ge(unit_taken[0], u + (U_MIX + 6 + 1))
                pe.wait_ge(conv_tap, l * 62 + 62)
                for t in range(2):
                    last = mm(pe, PS[:, 0, 0:L1], ONES[:, 1, :], ACC[:, t, :], t == 0, t == 1)
                last.then_inc(cv_mean, 1)
                scores(1)
                values(0)
                pe.wait_ge(cv_squared, l + 1)
                for t in range(2):
                    last = mm(pe, PS[:, 1, 0:L1], ONES[:, 1, :], CSQ[:, t, :], t == 0, t == 1)
                last.then_inc(cv_var, 1)
                scores(2)
                values(1)
                scores(3)
                values(2)
                values(3)
                pe.wait_ge(ret_copied, l * 4 + 4)
                for h in range(RH):
                    last = mm(pe, PS[:, 4 + h, 0:L1], ONES[:, 2, :], OT[:, h, :], True, True)
                last.then_inc(gn_stat, 1)
                begin(1, u + (U_MIX + 5), u + (U_MIX + 5))
                pe.wait_ge(pool_step, l * POOL_STEPS + POOL_STEPS)
                pe.wait_ge(vec_loaded, l * 32 + 32)
                for t in range(2):
                    last = mm(pe, PS[:, 2 + t, 0:L1], PW[:, t, :], PM[:, t, :], True, True)
                last.then_inc(gn_stat, 1)
                pe.wait_ge(pooled_taken, l + 1)
                pe.wait_ge(cv_silu, l * 2 + 2)
                for j in range(2):
                    for k in range(2):
                        last = mm(pe, PS[:, 2 + j, 0:L1], RING[:, 1, (j * 2 + k) * P:(j * 2 + k + 1) * P],
                                  CY[:, k, :], k == 0, k == 1)
                last.then_inc(unit_done[1], 1)
                pe.wait_ge(gn_squared, l + 1)
                for h in range(RH):
                    last = mm(pe, PS[:, 4 + h, 0:L1], ONES[:, 2, :], SL[:, h, :], True, True)
                last.then_inc(gn_stat, 1)
                pe.wait_ge(gn_y, l * 4 + 4)
                pe.wait_ge(unit_taken[1], u + (U_MIX + 6 + 1))
                for n in range(12, 16):
                    s = n % 2
                    begin(s, u + (U_MIX + n // 2), u + (U_MIX + n // 2))
                    two_tiles(s, YM, L1).then_inc(unit_done[s], 1)

            with pe.Fori(0, DEPTH) as l:
                def hidden(off):
                    return lambda s, last: pe.wait_ge(unit_taken[s], l * PAIRS_LAYER + (off + PAIRS_UP + last))
                pe.wait_ge(ln_out, l * 24 + 8)
                pe.sem_inc(passed["tensor"], 1)
                ffn(l * PAIRS_LAYER + U_FFN_A, l * PAIRS_LAYER + U_FFN_A, XL, L1, hidden(U_FFN_A),
                    l * (2 * ADA_UNITS))
                layer_norm(l, 1, U_FFN_A + PAIRS_FFN)
                mixer(l)
                layer_norm(l, 2, U_MIX + PAIRS_MIX)
                pe.wait_ge(ln_out, l * 24 + 24)
                pe.sem_inc(passed["tensor"], 1)
                ffn(l * PAIRS_LAYER + U_FFN_B, l * PAIRS_LAYER + U_FFN_B, XL, L1, hidden(U_FFN_B),
                    l * (2 * ADA_UNITS) + ADA_UNITS)
                layer_norm(l, 3, U_FFN_B + PAIRS_FFN)

            def rms(e, c0):
                for c in range(4):
                    pe.wait_ge(rm_squared, 2 * e + c + 1)
                    for k in (2 * c, 2 * c + 1):
                        last = mm(pe, PS[:, 4, 0:L2 - c0], ONES[:, 0, :], SQ[:, k, c0:L2], k == 0, k == CT - 1)
                last.then_inc(rm_var, 1)

            def rms_sums(e, c0, u):
                for s in range(2):
                    pe.wait_ge(unit_taken[s], u + 1)
                for s in range(2):
                    last = mm(pe, PS[:, 4, 0:L2 - c0], ONES[:, 0, :], SUMS[:, s, c0:L2], s == 0, s == 1)
                last.then_inc(rm_var, 1)

            def attend(items, base):
                def scores(n):
                    it = items[n]
                    if base + n >= 4:
                        pe.wait_ge(at_max, base + n - 3)
                        pe.wait_ge(at_exp, base + n - 3)
                    o = PS[:, n % 4, 0:it["keys"]]
                    for j, (a, b) in enumerate(it["qk"]):
                        last = mm(pe, o, a, b, j == 0, j == len(it["qk"]) - 1)
                    last.then_inc(at_scores, 1)

                def turn(n):
                    it = items[n]
                    pe.wait_ge(at_probs, base + n + 1)
                    if base + n >= 2:
                        pe.wait_ge(at_copied, base + n - 1)
                    for j in range(it["keys"] // P):
                        last = pe.transpose(PS[:, 4 + n % 2, j * P:(j + 1) * P], PR[n % 2][:, j * P:(j + 1) * P], IDN)
                    last.then_inc(at_turned, 1)

                def values(n):
                    it = items[n]
                    pe.wait_ge(at_copied, base + n + 1)
                    if base + n >= 2:
                        pe.wait_ge(at_out, base + n - 1)
                    nk = it["keys"] // P
                    for j in range(nk):
                        last = mm(pe, PS[it["rows"], 6 + n % 2, 0:P], it["v"](j), PTT[n % 2][:, j, :], j == 0, j == nk - 1)
                    last.then_inc(at_pv, 1)

                scores(0)
                scores(1)
                for n in range(len(items)):
                    if n + 2 < len(items):
                        scores(n + 2)
                    turn(n)
                    if n >= 1:
                        values(n - 1)
                values(len(items) - 1)

            rms(0, 0)
            pe.wait_ge(x_split, 4)
            for n in range(SPLIT_EVEN):
                s, u = n % 2, U_EVEN + n // 2
                pe.wait_ge(w_split[s], n // 2 + 1)
                pe.wait_ge(unit_taken[s], u + 1)
                two_tiles_split(s, 0, XLO2).then_inc(unit_done[s], 1)
            for n in range(SPLIT_EVEN, 14):
                s, u = n % 2, U_EVEN + n // 2
                begin(s, u, u)
                token_major(s, PRE, (P,) * 4).then_inc(unit_done[s], 1)
            pe.wait_ge(tab_loaded, 16 * N_TABLES)
            for t in range(4):
                for k in range(CT):
                    last = mm(pe, PS[:, 5, 16 * t:16 * t + 16], PRE[:, k, t * P:(t + 1) * P], WG[:, k, :],
                              k == 0, k == CT - 1)
            last.then_inc(pe_step, 1)
            pe.wait_ge(vec_step, LS_AT)
            pe.wait_ge(u_loaded, 16)
            for d in range(2):
                for st in range(4):
                    mm(pe, PS[0:4, 6 + d, :], LS[:, st, 8 * d + 4:8 * d + 8], NU[:, d, st, :], st == 0, False)
                for st in range(4):
                    mm(pe, PS[0:4, 6 + d, st * P:(st + 1) * P], GT[:, st, 8 * d:8 * d + 4], IDN, False, st == 3)
            for d in range(2):
                for t in range(4):
                    for st in range(4):
                        last = mm(pe, PS[:, 4, 16 * d + 4 * t:16 * d + 4 * t + 4], NU[:, d, st, t * P:(t + 1) * P],
                                  LS[:, st, 8 * d + 4:8 * d + 8], st == 0, st == 3)
            last.then_inc(pe_step, 1)
            pe.wait_ge(vec_step, NF_AT)
            for s in range(2):
                pe.wait_ge(unit_taken[s], U_EVEN + 7 + 1)
                pe.wait_ge(tap_prod[s], 2)
            def ml_broadcast(h):
                if h >= 1:
                    pe.wait_ge(ml_bcopied, h)
                for d in range(2):
                    last = mm(pe, PS[:, 4 + d, :], SEL[0:4, h * P:(h + 1) * P], GR[0:4, d, :], True, True)
                last.then_inc(ml_bc, 1)

            def ml_score(n):
                h, t = n // 4, n % 4
                if n >= 2:
                    pe.wait_ge(ml_probs, n - 1)
                mm(pe, PS[:, (6, 1)[n % 2], 0:ML_KEYS[t] * P], G[:, 8 + h, t * P:(t + 1) * P],
                   G[:, 12 + h, 0:ML_KEYS[t] * P], True, True).then_inc(ml_scores, 1)

            def ml_turn(n):
                pe.wait_ge(ml_probs, n + 1)
                if n >= 2:
                    pe.wait_ge(ml_copied, n - 1)
                for j in range(ML_KEYS[n % 4]):
                    last = pe.transpose(PS[:, (7, 2)[n % 2], j * P:(j + 1) * P], PR[n % 2][:, j * P:(j + 1) * P], IDN)
                last.then_inc(ml_turned, 1)

            def ml_values(n):
                h, t = n // 4, n % 4
                pe.wait_ge(ml_copied, n + 1)
                if t == 0 and h >= 2:
                    pe.wait_ge(ml_out, h - 1)
                for j in range(ML_KEYS[t]):
                    last = mm(pe, PS[:, (0, 3)[h % 2], t * P:(t + 1) * P], VM[:, j, h * P:(h + 1) * P],
                              PTT[n % 2][:, j, :], j == 0, j == ML_KEYS[t] - 1)
                last.then_inc(ml_pv, 1)

            ml_broadcast(0)
            ml_score(0)
            for n in range(ML_ITEMS):
                if n + 1 < ML_ITEMS:
                    ml_score(n + 1)
                ml_turn(n)
                if n >= 1:
                    ml_values(n - 1)
                if n % 4 == 0 and n // 4 + 1 < MLH:
                    ml_broadcast(n // 4 + 1)
            ml_values(ML_ITEMS - 1)
            for h in range(MLH):
                pe.wait_ge(ml_out, h + 1)
                mm(pe, PS[:, 4 + h, :], ONES[:, 2, :], G[:, 16 + h, :], True, True).then_inc(ml_mean, 1)
            for h in range(MLH):
                pe.wait_ge(ml_squared, h + 1)
                last = mm(pe, PS[:, 4 + h, :], ONES[:, 2, :], SQ[:, h, :], True, True)
            last.then_inc(pe_step, 1)
            pe.wait_ge(ml_std, 1)
            attend(EVEN_ITEMS, 0)
            pe.wait_ge(at_out, len(EVEN_ITEMS))
            pe.wait_ge(ml_normed, MLH)
            for n in range(14, 18):
                s, u = n % 2, U_EVEN + n // 2
                begin(s, u, u)
                two_tiles(s, YM2, L2).then_inc(unit_done[s], 1)
            rms_sums(1, 0, U_EVEN + PAIRS_EVEN)
            rms(2, 0)
            pe.wait_ge(x_split, 8)
            ffn(U_FFN2[0], U_FFN2[0], None, L2, lambda s, last: pe.wait_ge(tap_prod[s], 1 + PAIRS_UP + last), split=0)
            rms_sums(3, 0, U_FFN2[0] + PAIRS_FFN)
            rms(4, 0)
            pe.wait_ge(rm_in, 24)
            u = U_ODD
            begin(0, u, u)
            two_tiles(0, PRE[:, :, CTX:L2], SEQ).then_inc(unit_done[0], 1)
            begin(1, u, u)
            two_tiles(1, PRE, L2).then_inc(unit_done[1], 1)
            pe.wait_ge(odd_loaded, 16 * N_ODD)
            for s in range(2):
                pe.wait_ge(unit_taken[s], u + 2)
            for t in range(2):
                mm(pe, PS[:, 4, 0:SEQ], ONES[:, 1, :], SQ[:, t, 0:SEQ], t == 0, t == 1)
            mm(pe, PS[:, 5, :], ONES[:, 2, :], SQ[:, 2, :], True, True)
            mm(pe, PS[:, 6, 0:SEQ], PERM, KPE[:, CTX:L2], True, True).then_inc(pe_step, 1)
            pe.wait_ge(vec_step, ODD_Q_AT)
            for n in range(4):
                s, u = n % 2, U_ODD + 1 + n // 2
                pe.wait_ge(unit_taken[s], u + 1)
                for j in range(3):
                    for k in range(2):
                        last = mm(pe, PS[:, 2 * s + j // 2, 256 * (j % 2):256 * (j % 2) + 256],
                                  WUQ[:, 3 * n + j, k, :], DQ[:, k, :], k == 0, k == 1)
                last.then_inc(unit_done[s], 1)
            for n in range(4):
                s, u = n % 2, U_ODD + 3 + n // 2
                pe.wait_ge(unit_taken[s], u + 1)
                for j in range(2):
                    last = mm(pe, PS[:, 2 * s + j, :], WUKV[:, (2 * n + j) * P:(2 * n + j + 1) * P], CKV, True, True)
                last.then_inc(unit_done[s], 1)
            for n in range(4):
                s, u = n % 2, U_ODD + 5 + n // 2
                pe.wait_ge(unit_taken[s], u + 1)
                for j in range(2):
                    last = mm(pe, PS[:, 2 * s + j, :], CKV[:, n * P:(n + 1) * P],
                              WUKV[:, D + j * 512:D + (j + 1) * 512], True, True)
                last.then_inc(unit_done[s], 1)
            for s in range(2):
                pe.wait_ge(unit_taken[s], U_ODD + 7 + 1)
            for t in range(4):
                last = mm(pe, PS[:, 4 + t // 2, 256 * (t % 2):256 * (t % 2) + 256], PERM, QT[:, 8 + t, :], True, True)
            last.then_inc(pe_step, 1)
            pe.wait_ge(vec_step, ODD_ROPE_AT)
            attend(ODD_ITEMS, len(EVEN_ITEMS))
            pe.wait_ge(at_out, len(EVEN_ITEMS) + len(ODD_ITEMS))
            for n in range(4):
                s, u = n % 2, U_ODD + 7 + n // 2
                begin(s, U_ODD + 1 + n // 2, u)
                two_tiles(s, YM2[:, :, CTX:L2], SEQ).then_inc(unit_done[s], 1)
            rms_sums(5, CTX, U_ODD + PAIRS_ODD)
            rms(6, CTX)
            pe.wait_ge(x_split, 12)
            ffn(U_FFN2[1], U_FFN2[1] - VIRTUAL, None, SEQ,
                lambda s, last: pe.wait_ge(tap_prod[s], 1 + 2 * PAIRS_UP + last), split=1)
            rms_sums(7, CTX, U_FFN2[1] + PAIRS_FFN)

        @block.scalar
        def _(act):
            act.wait_ge(x_loaded, 16 * N_X)
            act.activation(SC[:, :, :], SC[:, :, :], ACT.Silu).then_inc(silu_c, 1)

            def layer_norm(l, e, gain, bias):
                for c in range(4):
                    act.wait_ge(ln_centred, lay(l, 12, 4 * e + c + 1))
                    act.activation(SL[:, 2 * c:2 * c + 2, :], PL[:, 2 * c:2 * c + 2, :], ACT.Square)\
                        .then_inc(ln_squared, 1)
                act.wait_ge(ln_var, lay(l, 3, e + 1))
                act.activation(RSTD[:, 0:L1], PS[:, 5, 0:L1], ACT.Sqrt, bias=EPS5[:, 0:1]).then_inc(ln_std, 1)
                for k in range(ACT_TILES):
                    if k % 2 == 0:
                        act.wait_ge(ln_scaled, lay(l, 12, 4 * e + k // 2 + 1))
                    act.activation(XL[:, k, :], PL[:, k, :], ACT.Identity, scale=gain(k), bias=bias(k))\
                        .then_inc(ln_out, 1)

            def ffn_gate(l, u, f):
                with act.Fori(0, PAIRS_UP) as i:
                    for s in range(2):
                        act.wait_ge(unit_done[s], u + i + 2)
                        act.activation(SG[:, s, 0:L1], PS[:, 2 * s, 0:L1], ACT.Silu).then_inc(silu_done[s], 1)

            layer_norm(None, 0, lambda k: LNIN[:, 0, k:k + 1], lambda k: LNIN[:, 1, k:k + 1])

            with act.Fori(0, DEPTH) as l:
                def vec_norm(e):
                    layer_norm(l, e, lambda k: VEC[:, V_LNG + 8 * (e - 1) + k:V_LNG + 8 * (e - 1) + k + 1],
                               lambda k: VEC[:, V_LNB + 8 * (e - 1) + k:V_LNB + 8 * (e - 1) + k + 1])
                u = l * PAIRS_LAYER
                act.wait_ge(vec_loaded, l * 32 + 32)
                ffn_gate(l, u + U_FFN_A, None)
                vec_norm(1)
                act.wait_ge(unit_done[0], u + (U_MIX + 1 + 2))
                act.activation(CSG, PS[:, 0:2, 0:L1], ACT.Sigmoid).then_inc(conv_gate, 1)
                for n in (7, 8):
                    s = n % 2
                    act.wait_ge(unit_done[s], u + (U_MIX + n // 2 + 2))
                    act.activation(GS[:, 2 * (n - 7):2 * (n - 7) + 2, :], PS[:, 2 * s:2 * s + 2, 0:L1], ACT.Silu)\
                        .then_inc(unit_taken[s], 1)
                for n in (9, 10):
                    s = n % 2
                    act.wait_ge(unit_done[s], u + (U_MIX + n // 2 + 2))
                    c = 256 * (n - 9)
                    act.copy(V1[:, 0:2, c:c + 256], PS[:, 2 * s, :].rearrange("p (a b) -> p a b", a=2))
                    act.copy(V1[0:META, 2, c:c + 256], PS[0:META, 2 * s + 1, 0:256]).then_inc(unit_taken[s], 1)

                def copy_head(h):
                    act.wait_ge(ret_out, l * 4 + h + 1)
                    act.copy(OT[:, h, :], PS[:, 7, 0:L1]).then_inc(ret_copied, 1)

                act.wait_ge(mix_step, l * MIX_STEPS + 13)
                act.activation(CSQ, ACC, ACT.Square).then_inc(cv_squared, 1)
                copy_head(0)
                act.wait_ge(cv_var, l + 1)
                act.activation(CSTD, PS[:, 1, 0:L1], ACT.Sqrt, bias=EPS5[:, 0:1]).then_inc(cv_std, 1)
                for h in range(1, RH):
                    copy_head(h)
                act.wait_ge(mix_step, l * MIX_STEPS + 15)
                for t in range(2):
                    act.activation(CY[:, t, :], ACC[:, t, :], ACT.Silu, scale=VEC[:, V_CG + t:V_CG + t + 1],
                                   bias=VEC[:, V_CB + t:V_CB + t + 1]).then_inc(cv_silu, 1)
                act.wait_ge(mix_step, l * MIX_STEPS + 16)
                act.activation(SL[:, 0:4, :], OT, ACT.Square).then_inc(gn_squared, 1)
                act.wait_ge(gn_stat, l * 3 + 3)
                act.activation(STD4, PS[:, 4:8, 0:L1], ACT.Sqrt, bias=EPS5[:, 0:1]).then_inc(gn_std, 1)
                vec_norm(2)
                ffn_gate(l, u + U_FFN_B, None)
                vec_norm(3)

            st = Steps(act, act_step)

            def rms_std(e, c0):
                act.wait_ge(rm_var, e + 1)
                act.activation(RSTD[:, c0:L2], PS[:, 4, 0:L2 - c0], ACT.Sqrt, bias=EPS6[:, 0:1]).then_inc(rm_std, 1)

            def rms_in(e, l, which, c0, wait_tile):
                for c in range(4):
                    wait_tile(c)
                    act.activation(SQ[:, 2 * c:2 * c + 2, c0:L2], X[:, 2 * c:2 * c + 2, c0:L2], ACT.Square)\
                        .then_inc(rm_squared, 1)
                rms_std(e, c0)
                for k in range(ACT_TILES):
                    if k % 2 == 0:
                        act.wait_ge(rm_scaled, 4 * e + k // 2 + 1)
                    for g in range(c0 // CTX, 2):
                        cols = slice(g * CTX, (g + 1) * CTX)
                        last = act.activation(PRE[:, k, cols], PRE[:, k, cols], ACT.Identity,
                                              scale=GIN[:, l, which, k, g:g + 1],
                                              bias=MOD[:, l, 24 * which + k, g:g + 1])
                    last.then_inc(rm_in, 1)

            def projected(u, c0):
                for n in range(4):
                    s = n % 2
                    act.wait_ge(unit_done[s], u + n // 2 + 2)
                    act.activation(SQ[:, 2 * n:2 * n + 2, c0:L2], PS[:, 2 * s:2 * s + 2, 0:L2 - c0], ACT.Square)\
                        .then_inc(sum_squared, 1)

            def conv_taps(s, done, free, n, vec, ngrp):
                if free is not None:
                    act.wait_ge(tap_prod[s], free)
                act.wait_ge(unit_done[s], done)
                cb, ac = CB[s], AC[s]
                src = PS[:, 2 * s:2 * s + 2, 0:n]
                if ngrp == 2:
                    for a in range(2):
                        act.copy(cb[:, a, :, 1:257], PS[:, 2 * s + a, :].rearrange("p (g t) -> p g t", g=2))
                else:
                    act.copy(cb[:, :, 1, 1:257], src)
                for a in range(2):
                    o = ac[:, a, :, :] if ngrp == 2 else ac[:, a, 1, :]
                    i = PS[:, 2 * s + a, :].rearrange("p (g t) -> p g t", g=2) if ngrp == 2 else PS[:, 2 * s + a, 0:n]
                    last = act.activation(o, i, ACT.Identity, scale=vec(a, 1), bias=vec(a, 3))
                last.then_inc(unit_taken[s], 1)

            def high_input(normed, c0):
                act.wait_ge(rm_in, normed)
                for c in range(4):
                    act.copy(XHI[:, 2 * c:2 * c + 2, c0:L2], PRE[:, 2 * c:2 * c + 2, c0:L2]).then_inc(x_high, 1)

            def high_weights(s, ld, u):
                act.wait_ge(w_loaded[s], ld * 16 + 16)
                act.wait_ge(unit_done[s], u + 1)
                act.copy(WHI[:, s, :], RING[:, s, 0:2 * D]).then_inc(w_high[s], 1)

            def ffn2(f, u, ld, n, ngrp):
                high_input(16 * (f + 1), L2 - n)

                def high(s, i):
                    high_weights(s, ld + i, u + i)

                def taps(s, i):
                    conv_taps(s, i + (u + 2), i + (2 + PAIRS_UP * f), n,
                              lambda a, c: FCW[f].rearrange("p f a c -> p f (a c)")[:, bass.ds(i * 2 + s, 1), 4 * a + c],
                              ngrp)

                def silu(s, i):
                    act.wait_ge(tap_side[s], i + (2 + PAIRS_UP * f + 1))
                    act.activation(SG[:, s, 0:n], AC[s][:, 1, 2 - ngrp:2, :].rearrange("p g t -> p (g t)"),
                                   ACT.Silu).then_inc(tap_silu[s], 1)

                for s in range(2):
                    high(s, 0)
                high(0, 1)
                taps(0, 0)
                with act.Fori(0, PAIRS_UP - 2) as i:
                    high(1, i + 1)
                    taps(1, i)
                    silu(0, i)
                    high(0, i + 2)
                    taps(0, i + 1)
                    silu(1, i)
                z = PAIRS_UP - 1
                high(1, z)
                taps(1, z - 1)
                silu(0, z - 1)
                taps(0, z)
                silu(1, z - 1)
                taps(1, z)
                silu(0, z)
                silu(1, z)
                with act.Fori(0, PAIRS_DN) as i:
                    for s in range(2):
                        act.wait_ge(unit_done[s], i + (u + PAIRS_UP + 2))
                        act.activation(SQ[:, bass.ds(i * 2 + s, 1), L2 - n:L2],
                                       PS[:, 2 * s, 0:n].rearrange("p (o n) -> p o n", o=1), ACT.Square)\
                            .then_inc(sum_squared, 1)

            def softmax(items, base):
                for n, it in enumerate(items):
                    b = base + n
                    w = it["keys"]
                    act.wait_ge(at_max, b + 1)
                    if n >= 2:
                        act.wait_ge(at_turned, b - 1)
                    act.activation(PR[n % 2][:, 0:w], SS[n % 2][:, 0:w] if it["sb"] else PS[:, n % 4, 0:w],
                                   ACT.Exp, bias=STAT[:, 4 + n % 2:5 + n % 2],
                                   scale=1.0 if it["sb"] else it["scale"],
                                   accum_out=STAT[:, 8 + n % 2:9 + n % 2]).then_inc(at_exp, 1)
                    if n >= 1:
                        copy_turned(items, base, n - 1)
                copy_turned(items, base, len(items) - 1)

            def copy_turned(items, base, n):
                act.wait_ge(at_turned, base + n + 1)
                if base + n >= 2:
                    act.wait_ge(at_pv, base + n - 1)
                nk = items[n]["keys"] // P
                act.copy(PTT[n % 2][:, 0:nk, :], PS[:, 4 + n % 2, 0:nk * P].rearrange("p (a b) -> p a b", a=nk))\
                    .then_inc(at_copied, 1)

            def first_tiles(c):
                if c == 0:
                    act.wait_ge(ctx_loaded, 16)
                    act.wait_ge(ln_out, 56)

            def after_post(e):
                return lambda c: act.wait_ge(rm_out, 4 * e + c + 1)

            act.wait_ge(gains_step, GAIN_STEPS)
            rms_in(0, 0, 0, 0, first_tiles)
            act.wait_ge(tab_loaded, 16 * N_TABLES)
            act.wait_ge(borders_zero, 2)
            high_input(8, 0)
            for n in range(2):
                high_weights(n % 2, U_EVEN, U_EVEN)
            for n in range(4):
                high_weights(n % 2, U_EVEN + n // 2 + 1, U_EVEN + n // 2 + 1)
            for n in range(4, 8):
                high_weights(n % 2, U_EVEN + n // 2 + 1, U_EVEN + n // 2 + 1)
                s, j = n % 2, n - 4
                conv_taps(s, U_EVEN + n // 2 + 2, j // 2 or None, L2, lambda a, c: EVW[:, 2 * j + a, c:c + 1], 2)
                act.wait_ge(tap_side[s], j // 2 + 1)
                for a in range(2):
                    last = act.activation(G[:, 8 + 2 * j + a, :], AC[s][:, a, :, :].rearrange("p g t -> p (g t)"),
                                          ACT.Silu)
                last.then_inc(tap_prod[s], 1)
            for n in (8, 9):
                s = n % 2
                act.wait_ge(unit_done[s], U_EVEN + n // 2 + 2)
                act.activation(G[:, 16 + 2 * (n - 8):18 + 2 * (n - 8), :], PS[:, 2 * s:2 * s + 2, :], ACT.Sigmoid)\
                    .then_inc(unit_taken[s], 1)
            for n in range(10, 14):
                s, c = n % 2, 256 * (n % 2)
                act.wait_ge(unit_done[s], U_EVEN + n // 2 + 2)
                act.copy((VN if n < 12 else VM)[:, :, c:c + 256],
                         PS[:, 2 * s:2 * s + 2, :].rearrange("p a (b c) -> p (a b) c", b=2)).then_inc(unit_taken[s], 1)
            act.wait_ge(vec_step, ABS_AT)
            st.link(act.activation(GE, GE, ACT.Exp, scale=-1.0))
            st.did(act.activation(GE, GE, ACT.Ln, bias=1.0))
            def ml_copy_rows(h):
                act.wait_ge(ml_bc, h + 1)
                for d in range(2):
                    last = act.copy(GBS[h % 2][:, d, :], PS[:, 4 + d, :])
                last.then_inc(ml_bcopied, 1)

            def ml_copy_turned(n):
                nk = ML_KEYS[n % 4]
                act.wait_ge(ml_turned, n + 1)
                if n >= 2:
                    act.wait_ge(ml_pv, n - 1)
                act.copy(PTT[n % 2][:, 0:nk, :], PS[:, (7, 2)[n % 2], 0:nk * P].rearrange("p (a b) -> p a b", a=nk))\
                    .then_inc(ml_copied, 1)

            ml_copy_rows(0)
            for n in range(ML_ITEMS):
                act.wait_ge(ml_arg, n + 1)
                c = 16 * (n % 2)
                for d in range(2):
                    q = TMS[n % 2][:, d, 0:ML_KEYS[n % 4] * P]
                    act.activation(q, q, ACT.Exp, bias=STAT[:, c + 18 + d:c + 19 + d])
                act.activation(STAT[:, c + 20:c + 22], STAT[:, c + 20:c + 22], ACT.Exp).then_inc(ml_w, 1)
                if n >= 1:
                    ml_copy_turned(n - 1)
                if n % 4 == 1 and n // 4 + 1 < MLH:
                    ml_copy_rows(n // 4 + 1)
            ml_copy_turned(ML_ITEMS - 1)
            for h in range(MLH):
                act.wait_ge(ml_centred, h + 1)
                act.activation(SQ[:, h, :], G[:, 16 + h, :], ACT.Square).then_inc(ml_squared, 1)
            act.wait_ge(pe_step, 3)
            act.activation(ML_STD, PS[:, 4:8, :], ACT.Sqrt, bias=EPS6[:, 0:1]).then_inc(ml_std, 1)
            softmax(EVEN_ITEMS, 0)
            projected(U_EVEN + 7, 0)
            rms_std(1, 0)
            rms_in(2, 0, 1, 0, after_post(0))
            ffn2(0, U_FFN2[0], U_FFN2[0], L2, 2)
            rms_std(3, 0)
            rms_in(4, 1, 0, 0, after_post(1))
            act.wait_ge(unit_done[0], U_ODD + 2)
            act.copy(DQ, PS[:, 0:2, 0:SEQ])
            act.activation(SQ[:, 0:2, 0:SEQ], PS[:, 0:2, 0:SEQ], ACT.Square).then_inc(unit_taken[0], 1)
            act.wait_ge(unit_done[1], U_ODD + 2)
            act.wait_ge(odd_loaded, 16 * N_ODD)
            act.copy(CKV, PS[:, 2, :])
            act.copy(KPE, PS[:, 3, :])
            act.activation(SQ[:, 2, :], PS[:, 2, :], ACT.Square).then_inc(unit_taken[1], 1)
            act.wait_ge(pe_step, 4)
            act.activation(SQ[:, 3, 0:SEQ], PS[:, 4, 0:SEQ], ACT.Sqrt, bias=EPS6[:, 0:1])
            st.did(act.activation(SQ[:, 4, :], PS[:, 5, :], ACT.Sqrt, bias=EPS6[:, 0:1]))
            for n in range(4):
                s = n % 2
                act.wait_ge(unit_done[s], U_ODD + 1 + n // 2 + 2)
                act.copy(QT[:, 3 * n:3 * n + 2, :], PS[:, 2 * s, :].rearrange("p (a b) -> p a b", a=2))
                act.copy(QT[:, 3 * n + 2, :], PS[:, 2 * s + 1, 0:SEQ]).then_inc(unit_taken[s], 1)
            for n in range(4):
                s = n % 2
                act.wait_ge(unit_done[s], U_ODD + 3 + n // 2 + 2)
                act.copy(KN[:, 2 * n:2 * n + 2, :], PS[:, 2 * s:2 * s + 2, :]).then_inc(unit_taken[s], 1)
            for n in range(4):
                s = n % 2
                act.wait_ge(unit_done[s], U_ODD + 5 + n // 2 + 2)
                act.copy(VV[:, n, :].rearrange("p (a b) -> p a b", a=2), PS[:, 2 * s:2 * s + 2, :])\
                    .then_inc(unit_taken[s], 1)
            softmax(ODD_ITEMS, len(EVEN_ITEMS))
            projected(U_ODD + 7, CTX)
            rms_std(5, CTX)
            rms_in(6, 1, 1, CTX, after_post(2))
            ffn2(1, U_FFN2[1], U_FFN2[1] - VIRTUAL, SEQ, 1)
            rms_std(7, CTX)

        @block.vector
        def _(v):
            for s in range(2):
                v.memset(SG[:, s, :], 0.0).then_inc(unit_taken[s], 1)
            v.memset(MODF[:, :, :], 0.0).then_inc(ada_taken, 1)
            v.memset(AP_, 0.0).then_inc(ada_summed, 1)

            def ada_sum(n, loaded, loads):
                v.wait_ge(loaded, loads)
                v.wait_ge(ada_done, n + 1)
                for k in range(CT):
                    for g in range(2):
                        c = SC[:, k, g:g + 1]
                        if k == 0:
                            ins = v.tensor_scalar(AP_[:, g, :, :], AW[:, :, k, :], c, None, ALU.mult)
                        else:
                            v.wait_ge(ada_step, n * (2 * CT) + (2 * k - 1 + g))
                            ins = v.scalar_tensor_tensor(AP_[:, g, :, :], AW[:, :, k, :], c, AP_[:, g, :, :],
                                                         ALU.mult, ALU.add)
                        if k == CT - 1 and g == 1:
                            ins.then_inc(ada_summed, 1)
                        else:
                            ins.then_inc(ada_step, 1)
                v.sem_inc(ada_step, 1)

            def ada_take(n):
                v.wait_ge(ada_done, n + 2)
                v.tensor_tensor(MODF[:, bass.ds(n * 2, 2), :], PS[:, 6, 0:4].rearrange("p (a b) -> p a b", a=2),
                                ADAB[:, bass.ds(n * 2, 2)].rearrange("p (a o) -> p a o", o=1).to_broadcast([P, 2, 2]),
                                ALU.add).then_inc(ada_taken, 1)

            def bc(t, n):
                return t.rearrange("p (o n) -> p o n", o=1).to_broadcast([P, n, t.shape[-1]])

            def layer_norm(l, e, gain, bias):
                v.wait_ge(ln_mean, lay(l, 3, e + 1))
                for c in range(4):
                    q = PL[:, 2 * c:2 * c + 2, :]
                    v.tensor_tensor(q, q, bc(PS[:, 4, 0:L1], 2), ALU.subtract).then_inc(ln_centred, 1)
                v.wait_ge(ln_std, lay(l, 3, e + 1))
                v.reciprocal(RSTD[:, 0:L1], RSTD[:, 0:L1]).then_inc(ln_rstd, 1)
                v.wait_ge(ln_rstd, lay(l, 3, e + 1))
                for c in range(4):
                    q = PL[:, 2 * c:2 * c + 2, :]
                    v.tensor_tensor(q, q, bc(RSTD[:, 0:L1], 2), ALU.mult).then_inc(ln_scaled, 1)
                v.wait_ge(ln_scaled, lay(l, 12, 4 * e + 4))
                for k in range(ACT_TILES, CT):
                    v.tensor_scalar(XL[:, k, :], PL[:, k, :], gain(k), bias(k), ALU.mult, ALU.add).then_inc(ln_out, 1)

            def ffn_half(l, u, f, ada):
                with v.Fori(0, PAIRS_UP) as i:
                    for s in range(2):
                        v.wait_ge(silu_done[s], l * (2 * PAIRS_UP) + i + (f * PAIRS_UP + 1))
                        v.tensor_tensor(G[:, bass.ds(i * 2 + s, 1), 0:L1],
                                        SG[:, s, 0:L1].rearrange("p (o n) -> p o n", o=1),
                                        PS[:, 2 * s + 1, 0:L1].rearrange("p (o n) -> p o n", o=1), ALU.mult)\
                            .then_inc(unit_taken[s], 1)
                        if s == 0:
                            ada_sum(ada + i, ada_loaded, l * (32 * PAIRS_UP) + i * 16 + (f * PAIRS_UP * 16 + 16))
                        else:
                            ada_take(ada + i)
                ada_sum(ada + (ADA_UNITS - 1), ada_last_loaded, l * 32 + (16 * f + 16))
                v.wait_ge(residual_scaled, l * 3 + (1 if f == 0 else 3))
                v.memset(SUMS[:, :, 0:L1], 0.0).then_inc(sum_added, 1)
                with v.Fori(0, PAIRS_DN) as i:
                    for s in range(2):
                        v.wait_ge(unit_done[s], u + i + (PAIRS_UP + 2))
                        q = PL[:, bass.ds(i * 2 + s, 1), :]
                        v.scalar_tensor_tensor(q, PS[:, 2 * s, 0:L1].rearrange("p (o n) -> p o n", o=1), 0.5, q,
                                               ALU.mult, ALU.add).then_inc(sum_added, 1)
                        v.wait_ge(sum_added, l * 23 + i * 2 + (14 * f + 2 + s))
                        t = SUMS[:, s:s + 1, 0:L1]
                        v.tensor_tensor(t, t, q, ALU.add).then_inc(unit_taken[s], 1)
                ada_take(ada + (ADA_UNITS - 1))

            layer_norm(None, 0, lambda k: LNIN[:, 0, k:k + 1], lambda k: LNIN[:, 1, k:k + 1])
            v.wait_ge(silu_c, 1)
            v.wait_ge(start_loaded, 16 * N_START)
            v.sem_inc(passed["vector"], 1)

            with v.Fori(0, DEPTH) as l:
                u = l * PAIRS_LAYER

                def vec_norm(e):
                    layer_norm(l, e, lambda k: VEC[:, V_LNG + 8 * (e - 1) + k:V_LNG + 8 * (e - 1) + k + 1],
                               lambda k: VEC[:, V_LNB + 8 * (e - 1) + k:V_LNB + 8 * (e - 1) + k + 1])
                ffn_half(l, u + U_FFN_A, 0, l * (2 * ADA_UNITS))
                v.wait_ge(vec_loaded, l * 32 + 32)
                vec_norm(1)
                st = Steps(v, mix_step, l * MIX_STEPS, MIX_STEPS)

                def taken(n):
                    s = n % 2
                    v.wait_ge(unit_done[s], u + (U_MIX + n // 2 + 2))
                    return s, PS[:, 2 * s:2 * s + 2, 0:L1]

                s, b = taken(0)
                v.tensor_copy(XP[:, :, 16:16 + L1], b).then_inc(unit_taken[s], 1)
                s, b = taken(1)
                v.tensor_copy(CA, b).then_inc(unit_taken[s], 1)
                v.wait_ge(conv_gate, l + 1)
                v.wait_ge(unit_taken[1], u + (U_MIX + 2))
                v.tensor_tensor(CP[:, :, TAPS - 1:TAPS - 1 + L1], CA, CSG, ALU.mult).then_inc(unit_taken[0], 1)
                v.wait_ge(unit_taken[0], u + (U_MIX + 3))
                v.wait_ge(vec_loaded, l * 32 + 32)

                def taps(a, b):
                    for t in range(a, b):
                        for j in range(2):
                            w = VEC[:, V_DW + 2 * t + j:V_DW + 2 * t + j + 1]
                            if t == 0:
                                ins = v.tensor_scalar(ACC[:, j, :], CP[:, j, 0:L1], w,
                                                      VEC[:, V_DB + j:V_DB + j + 1], ALU.mult, ALU.add)
                            else:
                                v.wait_ge(conv_tap, l * 62 + (2 * t + j - 1))
                                ins = v.scalar_tensor_tensor(ACC[:, j, :], CP[:, j, t:t + L1], w, ACC[:, j, :],
                                                             ALU.mult, ALU.add)
                            ins.then_inc(conv_tap, 1)

                def rotate(n):
                    s, b = taken(n)
                    if st.n:
                        st.wait()
                    st.did(v.tensor_tensor(T1, b, bc(RC, 2), ALU.mult))
                    st.did(v.tensor_tensor(T2[:, 0, :], PS[:, 2 * s + 1, 0:L1], RS[:, 0, :], ALU.mult))
                    v.tensor_tensor(T2[:, 1, :], PS[:, 2 * s, 0:L1], RS[:, 1, :], ALU.mult)\
                        .then_inc(unit_taken[s], 1)
                    v.wait_ge(unit_taken[s], u + (U_MIX + n // 2 + 2))
                    st.wait()
                    st.did(v.tensor_tensor(QK[:, 2 * (n - 3):2 * (n - 3) + 2, :], T1, T2, ALU.add))

                for j, n in enumerate((3, 4, 5, 6)):
                    taps(8 * j, min(8 * j + 8, TAPS))
                    rotate(n)

                def decay(h):
                    v.wait_ge(ret_scores, l * 4 + h + 1)
                    if h >= 2:
                        v.wait_ge(ret_out, l * 4 + h - 1)
                    v.tensor_tensor(ST[:, h % 2, 0:2, :], PS[:, 4:6, 0:L1], DT[:, h, 0:2, :], ALU.mult)
                    v.tensor_tensor(ST[0:META, h % 2, 2, :], PS[0:META, 6, 0:L1], DT[0:META, h, 2, :], ALU.mult)\
                        .then_inc(ret_decayed, 1)

                decay(0)
                v.wait_ge(cv_mean, l + 1)
                st.did(v.tensor_tensor(ACC, ACC, bc(PS[:, 0, 0:L1], 2), ALU.subtract))
                decay(1)
                decay(2)
                v.wait_ge(cv_std, l + 1)
                st.link(v.reciprocal(CSTD, CSTD))
                st.did(v.tensor_tensor(ACC, ACC, bc(CSTD, 2), ALU.mult))
                decay(3)
                v.wait_ge(gn_stat, l * 3 + 1)
                st.did(v.tensor_tensor(OT, OT, PS[:, 4:8, 0:L1], ALU.subtract))
                v.wait_ge(gn_stat, l * 3 + 2)
                for t in range(2):
                    last = v.tensor_scalar(YM[:, t, :], PS[:, 2 + t, 0:L1], VEC[:, V_PS + t:V_PS + t + 1], None,
                                           ALU.mult)
                last.then_inc(pooled_taken, 1)
                s, b = taken(11)
                v.tensor_copy(YM[:, 2:4, :], b).then_inc(unit_taken[s], 1)
                for h in range(RH):
                    last = v.scalar_tensor_tensor(GS[:, h, :], OT[:, h, :], VEC[:, V_GN + h:V_GN + h + 1], GS[:, h, :],
                                                  ALU.mult, ALU.mult)
                st.did(last)
                v.wait_ge(gn_std, l + 1)
                for h in range(RH):
                    st.did(v.reciprocal(STD4[:, h, :], STD4[:, h, :]))
                for h in range(RH):
                    st.wait(RH - 1 - h)
                    v.tensor_tensor(YM[:, 4 + h, :], GS[:, h, :], STD4[:, h, :], ALU.mult).then_inc(gn_y, 1)
                v.wait_ge(residual_scaled, l * 3 + 2)
                sums = SUMS[:, :, 0:L1]
                v.memset(sums, 0.0).then_inc(sum_added, 1)
                for n in range(12, 16):
                    s, b = taken(n)
                    q = PL[:, 2 * (n - 12):2 * (n - 12) + 2, :]
                    v.tensor_tensor(q, b, q, ALU.add).then_inc(sum_added, 1)
                    v.wait_ge(sum_added, l * 23 + (n - 12 + 11))
                    v.tensor_tensor(sums, sums, q, ALU.add).then_inc(unit_taken[s], 1)
                st.end()
                vec_norm(2)
                ffn_half(l, u + U_FFN_B, 1, l * (2 * ADA_UNITS) + ADA_UNITS)
                vec_norm(3)

            v.wait_ge(ada_taken, 4 * ADA_UNITS + 1)
            gst = Steps(v, gains_step)
            for l in range(DEPTH):
                for w in range(2):
                    m = MOD[:, l, 24 * w:24 * w + 24, :]
                    gst.did(v.tensor_scalar(GIN[:, l, w, :, :], m[:, 8:16, :], 1.0, None, ALU.add))
                    for g in range(2):
                        gst.did(v.tensor_tensor(GOUT[:, l, w, :, g], m[:, 16:24, g], NG[:, l, 2 * w + 1, :], ALU.mult))
            gst.wait()
            for l in range(DEPTH):
                for w in range(2):
                    for g in range(2):
                        gst.did(v.tensor_tensor(GIN[:, l, w, :, g], GIN[:, l, w, :, g], NG[:, l, 2 * w, :], ALU.mult))
            assert gst.n == GAIN_STEPS

            st = Steps(v, vec_step)

            def rms_rstd(e, c0):
                v.wait_ge(rm_std, e + 1)
                v.reciprocal(RSTD[:, c0:L2], RSTD[:, c0:L2]).then_inc(rm_rstd, 1)
                v.wait_ge(rm_rstd, e + 1)

            def rms_in(e, l, which, c0):
                rms_rstd(e, c0)
                for c in range(4):
                    v.tensor_tensor(PRE[:, 2 * c:2 * c + 2, c0:L2], X[:, 2 * c:2 * c + 2, c0:L2],
                                    bc(RSTD[:, c0:L2], 2), ALU.mult).then_inc(rm_scaled, 1)
                v.wait_ge(rm_scaled, 4 * e + 4)
                for k in range(ACT_TILES, CT):
                    for g in range(c0 // CTX, 2):
                        cols = slice(g * CTX, (g + 1) * CTX)
                        last = v.tensor_scalar(PRE[:, k, cols], PRE[:, k, cols], GIN[:, l, which, k, g:g + 1],
                                               MOD[:, l, 24 * which + k, g:g + 1], ALU.mult, ALU.add)
                    last.then_inc(rm_in, 1)

            def rms_post(e, c0):
                rms_rstd(e, c0)
                for c in range(5):
                    if c < 4:
                        q = PRE[:, 2 * c:2 * c + 2, c0:L2]
                        v.tensor_tensor(q, q, bc(RSTD[:, c0:L2], 2), ALU.mult).then_inc(rm_scaled, 1)
                    if c >= 1:
                        k = 2 * c - 2
                        v.wait_ge(rm_scaled, 4 * e + c)
                        v.tensor_tensor(X[:, k:k + 2, c0:L2], X[:, k:k + 2, c0:L2], PRE[:, k:k + 2, c0:L2], ALU.add)\
                            .then_inc(rm_out, 1)

            def projected(u, l, c0, squared):
                sums = SUMS[:, :, c0:L2]
                st.link(v.memset(sums, 0.0))
                for n in range(4):
                    s = n % 2
                    v.wait_ge(sum_squared, squared + n + 1)
                    for a in range(2):
                        for g in range(c0 // CTX, 2):
                            v.tensor_scalar(PRE[:, 2 * n + a, g * CTX:(g + 1) * CTX],
                                            PS[:, 2 * s + a, g * CTX - c0:(g + 1) * CTX - c0],
                                            GOUT[:, l, 0, 2 * n + a, g:g + 1], None, ALU.mult)
                    if n >= 1:
                        v.wait_ge(unit_taken[1 - s], u + (n - 1) // 2 + 2)
                    v.tensor_tensor(sums, sums, SQ[:, 2 * n:2 * n + 2, c0:L2], ALU.add).then_inc(unit_taken[s], 1)

            def side_taps(s, mid, vec, ngrp):
                v.wait_ge(unit_taken[s], mid)
                for a in range(2):
                    for c in (0, 2):
                        ac, cb = AC[s][:, a, :, :], CB[s][:, a, :, :]
                        if ngrp == 1:
                            ac, cb = ac[:, 1:2, :], cb[:, 1:2, :]
                        if c == 2:
                            st_side[s].wait()
                        ins = v.scalar_tensor_tensor(ac, cb[:, :, c:c + 256], vec(a, c), ac, ALU.mult, ALU.add)
                        if c == 0:
                            st_side[s].did(ins)
                        elif a == 0:
                            st_side[s].did(ins)
                ins.then_inc(tap_side[s], 1)

            class LoopSteps:
                def __init__(self, s):
                    self.s, self.base, self.n = s, 0, 0

                def did(self, ins):
                    self.n += 1
                    ins.then_inc(self.s, 1)

                def wait(self):
                    v.wait_ge(self.s, self.base + self.n)

            st_side = [LoopSteps(side_step[0]), LoopSteps(side_step[1])]

            def rest_input(f, c0, xlo):
                for c in range(4):
                    q = (slice(0, P), slice(2 * c, 2 * c + 2), slice(c0, L2))
                    v.wait_ge(x_high, 4 * f + c + 1)
                    v.tensor_tensor(xlo[q], PRE[q], XHI[q].bitcast(F32), ALU.subtract).then_inc(x_split, 1)

            def rest_weights(s, i):
                v.wait_ge(w_high[s], i + 1)
                v.tensor_tensor(WLO[:, s, :], RING[:, s, 0:2 * D], WHI[:, s, :].bitcast(F32), ALU.subtract)\
                    .then_inc(w_split[s], 1)

            def ffn2(f, u, n, ngrp, squared):
                rest_input(f + 1, L2 - n, XLO)

                def rest(s, i):
                    rest_weights(s, i + (SPLIT_EVEN // 2 + PAIRS_UP * f))

                def taps(s, i):
                    st_side[s].base = i * 3 + 3 * (2 + PAIRS_UP * f)
                    st_side[s].n = 0
                    side_taps(s, i + (u + 2),
                              lambda a, c: FCW[f].rearrange("p f a c -> p f (a c)")[:, bass.ds(i * 2 + s, 1), 4 * a + c],
                              ngrp)

                def product(s, i):
                    v.wait_ge(tap_silu[s], i + (PAIRS_UP * f + 1))
                    v.tensor_tensor(G[:, bass.ds(i * 2 + s, 1), 0:n],
                                    AC[s][:, 0:1, 2 - ngrp:2, :].rearrange("p o g t -> p o (g t)"),
                                    SG[:, s, 0:n].rearrange("p (o n) -> p o n", o=1), ALU.mult)\
                        .then_inc(tap_prod[s], 1)

                for s in range(2):
                    rest(s, 0)
                rest(0, 1)
                taps(0, 0)
                with v.Fori(0, PAIRS_UP - 2) as i:
                    rest(1, i + 1)
                    taps(1, i)
                    product(0, i)
                    rest(0, i + 2)
                    taps(0, i + 1)
                    product(1, i)
                z = PAIRS_UP - 1
                rest(1, z)
                taps(1, z - 1)
                product(0, z - 1)
                taps(0, z)
                product(1, z - 1)
                taps(1, z)
                product(0, z)
                product(1, z)
                c0 = L2 - n
                for s in range(2):
                    v.wait_ge(tap_prod[s], 2 + PAIRS_UP * (f + 1))
                st.did(v.memset(SUMS[:, :, c0:L2], 0.0))
                st.wait()
                with v.Fori(0, PAIRS_DN) as i:
                    for s in range(2):
                        v.wait_ge(sum_squared, i * 2 + (squared + s + 1))
                        for g in range(c0 // CTX, 2):
                            v.tensor_scalar(PRE[:, bass.ds(i * 2 + s, 1), g * CTX:(g + 1) * CTX],
                                            PS[:, 2 * s, g * CTX - c0:(g + 1) * CTX - c0]
                                            .rearrange("p (o n) -> p o n", o=1),
                                            GOUT[:, f, 1, bass.ds(i * 2 + s, 1), g], None, ALU.mult)
                        t = SUMS[:, s:s + 1, c0:L2]
                        v.tensor_tensor(t, t, SQ[:, bass.ds(i * 2 + s, 1), c0:L2], ALU.add).then_inc(unit_taken[s], 1)

            def attend(items, base, between=lambda n: None):
                def top(n):
                    it, b = items[n], base + n
                    w = it["keys"]
                    v.wait_ge(at_scores, b + 1)
                    src = PS[:, n % 4, 0:w]
                    if it["sb"]:
                        v.wait_ge(bias_ready, NAH)
                        if n >= 2:
                            v.wait_ge(at_exp, b - 1)
                        st.did(v.tensor_scalar(SS[n % 2][:, 0:CTX], src[:, 0:CTX], it["scale"], None, ALU.mult))
                        st.did(v.scalar_tensor_tensor(SS[n % 2][:, CTX:L2], src[:, CTX:L2], it["scale"], it["bias"],
                                                      ALU.mult, ALU.add))
                        st.wait()
                        src = SS[n % 2][:, 0:w]
                    st.link(v.tensor_reduce(STAT[:, n % 2:n % 2 + 1], src, AX.X, ALU.max))
                    v.tensor_scalar(STAT[:, 4 + n % 2:5 + n % 2], STAT[:, n % 2:n % 2 + 1],
                                    -1.0 if it["sb"] else -it["scale"], None, ALU.mult).then_inc(at_max, 1)

                def norm(n):
                    it, b = items[n], base + n
                    v.wait_ge(at_exp, b + 1)
                    st.link(v.reciprocal(STAT[:, 12 + n % 2:13 + n % 2], STAT[:, 8 + n % 2:9 + n % 2]))
                    q = PR[n % 2][:, 0:it["keys"]]
                    v.tensor_scalar(q, q, STAT[:, 12 + n % 2:13 + n % 2], None, ALU.mult).then_inc(at_probs, 1)

                def place(n):
                    it, b = items[n], base + n
                    v.wait_ge(at_pv, b + 1)
                    v.tensor_copy(it["out"], PS[it["rows"], 6 + n % 2, 0:P]).then_inc(at_out, 1)

                top(0)
                top(1)
                for n in range(len(items)):
                    norm(n)
                    if n + 2 < len(items):
                        top(n + 2)
                    if n >= 2:
                        place(n - 2)
                    between(n)
                for n in range(len(items) - 2, len(items)):
                    place(n)

            v.wait_ge(gains_step, GAIN_STEPS)
            rms_in(0, 0, 0, 0)
            rest_input(0, 0, XLO2)
            for n in range(2):
                rest_weights(n, 0)
            for n in range(4):
                s = n % 2
                rest_weights(s, n // 2 + 1)
                v.wait_ge(unit_done[s], U_EVEN + n // 2 + 2)
                v.tensor_copy(G[:, 2 * n:2 * n + 2, :], PS[:, 2 * s:2 * s + 2, :]).then_inc(unit_taken[s], 1)
            for n in range(4, 8):
                s, j = n % 2, n - 4
                rest_weights(s, n // 2 + 1)
                st_side[s].base, st_side[s].n = 3 * (j // 2), 0
                side_taps(s, U_EVEN + n // 2 + 2, lambda a, c: EVW[:, 2 * j + a, c:c + 1], 2)
            v.wait_ge(pe_step, 1)
            v.wait_ge(tab_loaded, 16 * N_TABLES)
            st.link(v.tensor_tensor(GT, PS[:, 5, 0:64].rearrange("p (a b) -> p a b", a=4), bc(GBIAS, 4), ALU.add))
            st.link(v.tensor_scalar(GE, GT, -1.0, None, ALU.mult))
            st.did(v.tensor_tensor(GE, GE, GT, ALU.max))
            assert st.n == ABS_AT
            st.link(v.tensor_scalar(LS, GT, 0.0, None, ALU.min))
            v.wait_ge(act_step, 2)
            st.did(v.tensor_tensor(LS, LS, GE, ALU.subtract))
            assert st.n == LS_AT
            v.wait_ge(pe_step, 2)
            st.did(v.tensor_copy(GR[0:4, :, :], PS[0:4, 6:8, :]))
            st.did(v.tensor_copy(NF, PS[:, 4, 0:32].rearrange("p (d t h) -> p d t h", d=2, t=4)))
            assert st.n == NF_AT
            def ml_args(n):
                h, t, c = n // 4, n % 4, 16 * (n % 2)
                w, m0 = ML_KEYS[t] * P, (0, 256, 512, 1024)[t]
                if t == 0:
                    v.wait_ge(ml_bcopied, h + 1)
                st.wait()
                if n >= 2:
                    v.wait_ge(ml_probs, n - 1)
                for d in range(2):
                    st.did(v.tensor_tensor_reduce(TMS[n % 2][:, d, 0:w], GBS[h % 2][:, d, 0:w], MASK[:, d, m0:m0 + w],
                                                  1.0, -3e38, ALU.add, ALU.max, STAT[:, c + 16 + d:c + 17 + d]))
                st.wait()
                st.did(v.tensor_scalar(STAT[:, c + 18:c + 20], STAT[:, c + 16:c + 18], -1.0, None, ALU.mult))
                v.tensor_tensor(STAT[:, c + 20:c + 22], NF[:, :, t, h], STAT[:, c + 16:c + 18], ALU.subtract)\
                    .then_inc(ml_arg, 1)

            def ml_weigh(n):
                c, w = 16 * (n % 2), ML_KEYS[n % 4] * P
                tm, q = TMS[n % 2], PR[n % 2][:, 0:w]
                total, low, by = STAT[:, c + 22:c + 24], STAT[:, c + 24:c + 26], STAT[:, c + 26:c + 28]
                v.wait_ge(ml_scores, n + 1)
                v.wait_ge(ml_w, n + 1)
                for d in range(2):
                    st.did(v.tensor_tensor_reduce(tm[:, d, 0:w], tm[:, d, 0:w], PS[:, (6, 1)[n % 2], 0:w], 128.0 ** -0.5,
                                                  0.0, ALU.mult, ALU.add, STAT[:, c + 22 + d:c + 23 + d]))
                st.wait()
                st.link(v.scalar_tensor_tensor(low, total, -1.0, total, ALU.mult, ALU.max))
                st.link(v.tensor_tensor(low, low, STAT[:, c + 20:c + 22], ALU.max))
                st.link(v.reciprocal(by, low))
                if n >= 2:
                    v.wait_ge(ml_turned, n - 1)
                st.link(v.tensor_scalar(q, tm[:, 0, 0:w], STAT[:, c + 26:c + 27], None, ALU.mult))
                v.scalar_tensor_tensor(q, tm[:, 1, 0:w], STAT[:, c + 27:c + 28], q, ALU.mult, ALU.add)\
                    .then_inc(ml_probs, 1)

            def ml_gate(h):
                v.wait_ge(ml_pv, 4 * h + 4)
                v.tensor_tensor(G[:, 16 + h, :], G[:, 16 + h, :], PS[:, (0, 3)[h % 2], :], ALU.mult).then_inc(ml_out, 1)

            v.wait_ge(mask_loaded, 16)
            ml_args(0)
            for n in range(ML_ITEMS):
                if n + 1 < ML_ITEMS:
                    ml_args(n + 1)
                ml_weigh(n)
                if n % 4 == 1 and n >= 4:
                    ml_gate(n // 4 - 1)
            ml_gate(MLH - 1)
            for h in range(MLH):
                v.wait_ge(ml_mean, h + 1)
                v.tensor_tensor(G[:, 16 + h, :], G[:, 16 + h, :], PS[:, 4 + h, :], ALU.subtract).then_inc(ml_centred, 1)

            def ml_norm(piece):
                h, part = piece // 3, piece % 3
                if part < 2:
                    q = ML_STD[:, h, 256 * part:256 * part + 256]
                    v.wait_ge(ml_std, 1)
                    v.reciprocal(q, q).then_inc(ml_rstd, 1)
                else:
                    v.wait_ge(ml_rstd, 2 * h + 2)
                    v.wait_ge(ml_centred, h + 1)
                    v.scalar_tensor_tensor(YM2[:, 4 + h, :], G[:, 16 + h, :], MLG[:, h:h + 1], ML_STD[:, h, :],
                                           ALU.mult, ALU.mult).then_inc(ml_normed, 1)

            attend(EVEN_ITEMS, 0, lambda n: ml_norm(n - 2) if 2 <= n < 2 + 3 * MLH else None)
            projected(U_EVEN + 7, 0, 0, 0)
            rms_post(1, 0)
            rms_in(2, 0, 1, 0)
            ffn2(0, U_FFN2[0], L2, 2, 4)
            rms_post(3, 0)
            rms_in(4, 1, 0, 0)
            v.wait_ge(act_step, ODD_STD_AT)
            v.wait_ge(odd_loaded, 16 * N_ODD)
            st.did(v.reciprocal(SQ[:, 3, 0:SEQ], SQ[:, 3, 0:SEQ]))
            st.link(v.reciprocal(SQ[:, 4, :], SQ[:, 4, :]))
            st.did(v.tensor_tensor(DQ, DQ, bc(SQ[:, 3, 0:SEQ], 2), ALU.mult))
            st.did(v.tensor_tensor(CKV, CKV, SQ[:, 4, :], ALU.mult))
            st.did(v.tensor_tensor(KPE[:, CTX:L2], KPE[:, CTX:L2], RT[:, 0, :], ALU.mult))
            st.did(v.tensor_tensor(SW[:, 0, :], PS[:, 6, 0:SEQ], RT[:, 1, :], ALU.mult))
            st.wait()
            for t in range(2):
                st.did(v.tensor_scalar(DQ[:, t, :], DQ[:, t, :], QNG[:, t:t + 1], None, ALU.mult))
            st.did(v.tensor_scalar(CKV, CKV, QNG[:, 2:3], None, ALU.mult))
            st.did(v.tensor_tensor(KPE[:, CTX:L2], KPE[:, CTX:L2], SW[:, 0, :], ALU.add))
            assert st.n == ODD_Q_AT, st.n
            v.wait_ge(pe_step, 5)
            st.wait()
            for t in range(4):
                st.did(v.tensor_tensor(SW[:, t, :], PS[:, 4 + t // 2, 256 * (t % 2):256 * (t % 2) + 256], RT[:, 1, :],
                                       ALU.mult))
            q = QT[:, 8:12, :]
            st.link(v.tensor_tensor(q, q, bc(RT[:, 0, :], 4), ALU.mult))
            st.did(v.tensor_tensor(q, q, SW, ALU.add))
            assert st.n == ODD_ROPE_AT, st.n
            attend(ODD_ITEMS, len(EVEN_ITEMS))
            projected(U_ODD + 7, 1, CTX, 12)
            rms_post(5, CTX)
            rms_in(6, 1, 1, CTX)
            ffn2(1, U_FFN2[1], SEQ, 1, 16)
            rms_post(7, CTX)


def feature_major(a):
    return a.T.reshape(-1, P, a.shape[0]).transpose(1, 0, 2)


def columns(v):
    t = v.reshape(v.shape[:-1] + (-1, P))
    return np.moveaxis(t, -1, 0)


def tile_pairs(w):
    f = w.shape[1] // (2 * P)
    return w.reshape(CT, P, f, 2, P).transpose(2, 1, 3, 0, 4).reshape(f, P, 2 * D)


def wide(w):
    f = w.shape[1] // 256
    return w.reshape(CT, P, f, 256).transpose(2, 1, 0, 3).reshape(f, P, 2 * D)


def up_units(w):
    h = w.shape[1] // 2
    w = np.pad(w.reshape(D, 2, h), ((0, 0), (0, 0), (0, FF - h)))
    return w.reshape(CT, P, 2, FT, P).transpose(3, 1, 2, 0, 4).reshape(FT, P, 2 * D)


def down_units(w):
    w = np.pad(w, ((0, FF - w.shape[0]), (0, 0)))
    return w.reshape(FT, P, CT, P).transpose(2, 1, 0, 3).reshape(CT, P, SLOT)


def shape_tables():
    t = {}
    pos = np.arange(L1)
    half = 64
    ang = pos[None, :] * (10000.0 ** (-np.arange(0, 128, 2) / 128.0))[:, None]
    ang = np.concatenate([ang, ang], 0)
    t["rope_c"] = np.cos(ang)
    t["rope_s"] = np.stack([-np.sin(ang), np.sin(ang)], 1)
    decay = np.zeros((P, RH, 3, L1))
    chunk = (pos + (-META) % 64) // 64
    for h in range(RH):
        gamma = 1.0 - 2.0 ** (-5.0 - h)
        m = gamma ** np.abs(pos[None, :] - pos[:, None]) * (chunk[:, None] <= chunk[None, :]) * 128.0 ** -0.5
        for j in range(3):
            rows = m[j * P:(j + 1) * P]
            decay[:len(rows), h, j] = rows
    t["decay"] = decay
    cnt = np.zeros((P, 2, L1))
    for g, w in enumerate((2, 4, 8, 16)):
        cnt[64 * (g % 2):64 * (g % 2) + 64, g // 2] = 1.0 / np.minimum(pos + 1, w)
    t["inv_count"] = cnt
    t["ident"] = np.eye(P)
    s = np.arange(L2)
    is_ctx = s < CTX
    fwd = s[:, None] <= s[None, :]
    bwd = np.where(is_ctx[:, None], np.where(is_ctx[None, :], s[:, None] >= s[None, :], True),
                   np.where(is_ctx[None, :], False, s[:, None] >= s[None, :]))
    seen = np.stack([fwd, bwd]).astype(np.float64)
    t["seen"] = (-seen).reshape(2, 4, P, L2).transpose(2, 0, 1, 3)
    mask = np.where(seen > 0, 0.0, NEG)
    parts = [mask[:, 0:w, q * P:(q + 1) * P].transpose(2, 0, 1) for q, w in ((0, CTX), (1, CTX), (2, L2), (3, L2))]
    t["mask"] = np.concatenate(parts, 2)
    sel = np.zeros((MLH, MLH, P))
    for h in range(MLH):
        sel[h, h] = 1.0
    t["sel"] = sel.reshape(MLH, MLH * P)
    col = np.arange(GRID_W)
    cs = np.clip(col - 8, 0, GRID_W - 16)
    inside = (col[None, :] >= cs[:, None]) & (col[None, :] < cs[:, None] + 16)
    t["win"] = np.tile(np.where(inside, 0.0, NEG), (2, 1))
    d = np.arange(P) % 32
    x = np.arange(SEQ)
    where = np.where((d < 16)[:, None], (x // GRID_W)[None, :], (x % GRID_W)[None, :])
    ang = where * (10000.0 ** (-(d % 8) / 8.0))[:, None]
    t["rope2"] = np.stack([np.cos(ang), np.where((d % 16 < 8)[:, None], -np.sin(ang), np.sin(ang))], 1)
    perm = np.zeros((P, P))
    perm[np.arange(P), np.arange(P) ^ 8] = 1.0
    t["perm"] = perm
    return {k: np.ascontiguousarray(v, dtype=np.float32) for k, v in t.items()}


def lay_out(i):
    cat = np.concatenate
    a = {}
    a["x"] = feature_major(cat([i["meta"], i["x"][0]], 0))
    a["ctx"] = feature_major(i["ctx_2"][0])
    a["c"] = columns(np.stack([i["c_ctx_2"], i["c_2"][0]])).transpose(0, 2, 1)
    a["ln_in"] = columns(np.stack([i["ln_in_g"], i["ln_in_b"]]))
    a["ada"] = cat([tile_pairs(w) for w in i["ada_w_2"]], 0)
    a["ada_b"] = columns(i["ada_b_2"]).reshape(P, DEPTH * 48)
    a["norm_g"] = columns(i["norm_g_2"])
    for key, n in (("a", "ffn1"), ("b", "ffn2")):
        a["up_" + key] = cat([up_units(w) for w in i[n + "_w13"]], 0)
        a["dn_" + key] = cat([down_units(w) for w in i[n + "_w2"]], 0)
    a["up_c"] = cat([up_units(w) for w in i["ffn_w_up_2"]], 0)
    a["dn_c"] = cat([down_units(w) for w in i["ffn_w_down_2"]], 0)
    halves = np.array([[h * P + a_ * 64 + e for h in (2 * g, 2 * g + 1) for e in range(64)]
                       for g in range(2) for a_ in range(2)]).reshape(-1)
    mix, vec, pw = [], [], []
    for l in range(DEPTH):
        w = i["w_in"][l]
        pws = i["conv_pw"][l].reshape(2, P, 2, P).transpose(1, 2, 0, 3).reshape(P, 512)
        mix.append(cat([tile_pairs(w[:, 0:768]), tile_pairs(w[:, 768:1280][:, halves]),
                        tile_pairs(w[:, 1280:1792][:, halves]), tile_pairs(w[:, 2304:2816]), wide(w[:, 1792:2304]),
                        np.pad(pws, ((0, 0), (0, 2 * D - 512)))[None], tile_pairs(i["w_out"][l])], 0))
        dw = columns(i["conv_dw"][l]).reshape(P, 2 * TAPS)
        vec.append(cat([columns(i["ln_g"][l]).reshape(P, 24), columns(i["ln_b"][l]).reshape(P, 24),
                        columns(i["pool_scale"][l]), dw, columns(i["conv_db"][l]), columns(i["conv_ln_g"][l]),
                        columns(i["conv_ln_b"][l]), columns(i["ret_gn_g"][l])], 1))
        g4 = i["pool_w"][l]
        blocks = np.zeros((P, 2, P), np.float32)
        for g in range(4):
            q = slice(64 * (g % 2), 64 * (g % 2) + 64)
            blocks[q, g // 2, q] = g4[g]
        pw.append(blocks)
    a["mix"], a["vec"], a["pool_w"] = cat(mix, 0), np.stack(vec), np.stack(pw)
    w = i["ev_w_in_2"][0]
    a["even"] = cat([tile_pairs(w[:, 0:1024]), tile_pairs(w[:, 1536:2560]), tile_pairs(w[:, 3072:3584]),
                     wide(w[:, 1024:1536]), wide(w[:, 2560:3072]), tile_pairs(i["ev_w_out_2"][0])], 0)
    a["wg"] = w[:, 3584:3600].reshape(CT, P, 16).transpose(1, 0, 2)
    a["gate_b"] = np.tile(i["ev_gate_b_2"], (P, 1))
    a["ml_g"] = columns(i["ev_ml_norm_g_2"][0])

    def taps(w, b, lead):
        t = columns(cat([w, b[None]], 0)).transpose(0, 2, 1)
        return t if lead is None else t.reshape(P, 2, -1, 4).transpose(0, 2, 1, 3)
    a["evw"] = taps(i["ev_conv_w_2"][0], i["ev_conv_b_2"][0], None)
    for l in range(DEPTH):
        a[f"fcw{l}"] = taps(i["ffn_conv_w_2"][l], i["ffn_conv_b_2"][l], 2)
    r = i["ev_rpb_2"][0][:, 8 - ROWS:7 + ROWS]
    r = np.pad(r, ((0, 0), (0, 0), (GRID_W - 16, GRID_W - 16)))
    a["rpb"] = np.tile(r, (1, 1, GRID_W))
    kv = i["od_w_dkv_2"][0]
    a["odd"] = cat([tile_pairs(i["od_w_dq_2"][0]), tile_pairs(cat([kv[:, 0:128]] + [kv[:, 128:160]] * 4, 1)),
                    tile_pairs(i["od_w_o_2"][0])], 0)
    uq = i["od_w_uq_2"][0].reshape(256, MLAH, 96)
    uq = cat([uq[:, :, 0:64].reshape(256, 1024), uq[:, :, 64:96].reshape(256, 512)], 1)
    a["uq"] = uq.reshape(2, P, 12, P).transpose(1, 2, 0, 3)
    ukv = i["od_w_ukv_2"][0].reshape(128, MLAH, 128)
    a["ukv"] = cat([ukv[:, :, 0:64].reshape(128, 1024), ukv[:, :, 64:128].reshape(128, 1024)], 1)
    a["qkv_g"] = cat([columns(i["od_q_norm_g_2"][0]), columns(i["od_kv_norm_g_2"][0])], 1)
    a.update(shape_tables())
    return {k: np.ascontiguousarray(v) for k, v in a.items()}


def kernel(**inputs):
    import concourse.bacc as bacc
    from concourse.bass_utils import run_bass_kernel_spmd

    nc = bacc.Bacc("TRN2", target_bir_lowering=False, num_devices=1)
    arrays = {"in_" + k: v for k, v in lay_out({k: np.asarray(v) for k, v in inputs.items()}).items()}
    A = {k[3:]: nc.dram_tensor(k, v.shape, F32, kind="ExternalInput").ap() for k, v in arrays.items()}
    out = nc.dram_tensor("out", (P, CT, SEQ), F32, kind="ExternalOutput").ap()
    build(nc, A, out)
    r = run_bass_kernel_spmd(nc, [arrays], core_ids=[0]).results[0]["out"]
    return np.ascontiguousarray(r.transpose(1, 0, 2).reshape(D, SEQ).T)[None]
```
